# Optimizing a Trainium2 kernel written in Bass

```python
import jax, jax.numpy as jnp
from jax import lax
import numpy as np
import math

D_MODEL = 1024
BATCH = 1
SEQ = 512
DEPTH = 2

MLA_HEADS = 4
MLA_Q_LORA = 384
MLA_KV_LORA = 256
MLA_NOPE_DIM = 128
MLA_ROPE_DIM = 64
MLA_V_DIM = 128
MLA_WIDTH = MLA_HEADS * MLA_V_DIM
ROPE_THETA = 10000.0
Q_BLOCK = 128
MLSTM_HEADS = 4
MLSTM_HEAD_DIM = 64
MLSTM_WIDTH = MLSTM_HEADS * MLSTM_HEAD_DIM
MLSTM_CONV = 5
MLSTM_CHUNK = 64
FNET_GROUPS = 4
FNET_GROUP_DIM = 64
FNET_WIDTH = FNET_GROUPS * FNET_GROUP_DIM
MIX_WIDTH = MLA_WIDTH + MLSTM_WIDTH + FNET_WIDTH
IN_SPLITS = (MLA_Q_LORA, MLA_KV_LORA, MLA_ROPE_DIM, MLSTM_WIDTH, MLSTM_WIDTH, MLSTM_WIDTH, 4 * MLSTM_HEADS, FNET_WIDTH)
D_IN = MLA_Q_LORA + MLA_KV_LORA + MLA_ROPE_DIM + 3 * MLSTM_WIDTH + 4 * MLSTM_HEADS + FNET_WIDTH
D_FF = 2816
PLE_DIM = 256
EPS = 1e-6


def rmsnorm(x, g):
    xf = x.astype(jnp.float32)
    y = xf * lax.rsqrt(jnp.mean(xf * xf, axis=-1, keepdims=True) + EPS)
    return (y * g.astype(jnp.float32)).astype(x.dtype)

def swiglu(x, w_gate, w_up, w_down):
    return (jax.nn.silu(x @ w_gate) * (x @ w_up)) @ w_down

def split_cols(z, sizes):
    offs = [int(o) for o in np.cumsum(sizes)[:-1]]
    return jnp.split(z, offs, axis=-1)

def rope_tables(positions):
    inv = 1.0 / (ROPE_THETA ** (jnp.arange(0, MLA_ROPE_DIM, 2, dtype=jnp.float32) / MLA_ROPE_DIM))
    ang = positions.astype(jnp.float32)[..., None] * inv
    return jnp.cos(ang), jnp.sin(ang)

def apply_rope(x, cos, sin):
    xf = x.astype(jnp.float32)
    x1, x2 = jnp.split(xf, 2, axis=-1)
    out = jnp.concatenate([x1 * cos - x2 * sin, x2 * cos + x1 * sin], axis=-1)
    return out.astype(x.dtype)

def mla_mixer(c_q, c_kv, k_rope, cos, sin, q_norm, w_uq, kv_norm, w_ukv):
    B, S, _ = c_q.shape
    q = (rmsnorm(c_q, q_norm) @ w_uq).reshape(B, S, MLA_HEADS, MLA_NOPE_DIM + MLA_ROPE_DIM)
    q_nope, q_rope = q[..., :MLA_NOPE_DIM], q[..., MLA_NOPE_DIM:]
    q_rope = apply_rope(q_rope, cos[:, :, None, :], sin[:, :, None, :])
    kv = (rmsnorm(c_kv, kv_norm) @ w_ukv).reshape(B, S, MLA_HEADS, MLA_NOPE_DIM + MLA_V_DIM)
    k_nope, v = kv[..., :MLA_NOPE_DIM], kv[..., MLA_NOPE_DIM:]
    k_rope = apply_rope(k_rope, cos, sin)
    scale = (MLA_NOPE_DIM + MLA_ROPE_DIM) ** -0.5
    nb = S // Q_BLOCK

    def attend(args):
        qn, qr = args
        s = jnp.einsum('bqhd,bkhd->bhqk', qn, k_nope) + jnp.einsum('bqhr,bkr->bhqk', qr, k_rope)
        pr = jax.nn.softmax(s.astype(jnp.float32) * scale, axis=-1).astype(v.dtype)
        return jnp.einsum('bhqk,bkhd->bqhd', pr, v)

    qn_b = jnp.moveaxis(q_nope.reshape(B, nb, Q_BLOCK, MLA_HEADS, MLA_NOPE_DIM), 1, 0)
    qr_b = jnp.moveaxis(q_rope.reshape(B, nb, Q_BLOCK, MLA_HEADS, MLA_ROPE_DIM), 1, 0)
    o = lax.map(attend, (qn_b, qr_b))
    return jnp.moveaxis(o, 0, 1).reshape(B, S, MLA_WIDTH)

def mlstm_chunkwise(q, k, v, i_pre, f_pre):
    B, H, S, d = q.shape
    L = MLSTM_CHUNK
    nc = S // L
    q = q * d ** -0.5
    lf = jax.nn.log_sigmoid(f_pre)
    causal = jnp.tril(jnp.ones((L, L), dtype=bool))

    def chunks(t):
        return jnp.moveaxis(t.reshape((B, H, nc, L) + t.shape[3:]), 2, 0)

    def step(carry, xs):
        C, n, m = carry
        qc, kc, vc, ic, lfc = xs
        b = jnp.cumsum(lfc, axis=-1)
        D = jnp.where(causal, b[..., :, None] - b[..., None, :] + ic[..., None, :], -jnp.inf)
        m_inter = b + m[..., None]
        m_t = jnp.maximum(m_inter, jnp.max(D, axis=-1))
        w_intra = jnp.exp(D - m_t[..., None])
        w_state = jnp.exp(m_inter - m_t)
        s = jnp.einsum('bhtd,bhsd->bhts', qc, kc) * w_intra
        numer = jnp.einsum('bhts,bhsd->bhtd', s, vc) + w_state[..., None] * jnp.einsum('bhvk,bhtk->bhtv', C, qc)
        denom = jnp.sum(s, axis=-1) + w_state * jnp.einsum('bhk,bhtk->bht', n, qc)
        h = numer / jnp.maximum(jnp.abs(denom), jnp.exp(-m_t))[..., None]
        bL = b[..., -1]
        lw = bL[..., None] - b + ic
        m_new = jnp.maximum(bL + m, jnp.max(lw, axis=-1))
        ws = jnp.exp(lw - m_new[..., None])
        dec = jnp.exp(bL + m - m_new)
        C = dec[..., None, None] * C + jnp.einsum('bhs,bhsv,bhsk->bhvk', ws, vc, kc)
        n = dec[..., None] * n + jnp.einsum('bhs,bhsk->bhk', ws, kc)
        return (C, n, m_new), h

    init = (jnp.zeros((B, H, d, d), jnp.float32), jnp.zeros((B, H, d), jnp.float32), jnp.zeros((B, H), jnp.float32))
    _, h = lax.scan(step, init, (chunks(q), chunks(k), chunks(v), chunks(i_pre), chunks(lf)))
    return jnp.moveaxis(h, 0, 2).reshape(B, H, S, d)

def mlstm_mixer(m_x, m_v, m_o, m_if, conv_w, conv_b, w_q, w_k, i_bias, f_bias, head_norm, skip):
    B, S, _ = m_x.shape
    pad = MLSTM_CONV // 2
    xc = lax.conv_general_dilated(m_x, conv_w[:, None, :], window_strides=(1,), padding=[(pad, pad)],
                                  dimension_numbers=('NWC', 'WIO', 'NWC'), feature_group_count=MLSTM_WIDTH)
    xc = jax.nn.silu(xc + conv_b)
    xh = xc.reshape(B, S, MLSTM_HEADS, MLSTM_HEAD_DIM)
    q = jnp.einsum('bshd,hde->bhse', xh, w_q).astype(jnp.float32)
    k = jnp.einsum('bshd,hde->bhse', xh, w_k).astype(jnp.float32)
    v = m_v.reshape(B, S, MLSTM_HEADS, MLSTM_HEAD_DIM).transpose(0, 2, 1, 3).astype(jnp.float32)
    g = m_if.astype(jnp.float32).reshape(B, S, 2, 2, MLSTM_HEADS)
    i_pre = jnp.transpose(g[:, :, 0] + i_bias.astype(jnp.float32), (2, 0, 3, 1))
    f_pre = jnp.transpose(g[:, :, 1] + f_bias.astype(jnp.float32), (2, 0, 3, 1))
    h_fwd = mlstm_chunkwise(q, k, v, i_pre[0], f_pre[0])
    flip = lambda t: jnp.flip(t, axis=2)
    h_bwd = flip(mlstm_chunkwise(flip(q), flip(k), flip(v), flip(i_pre[1]), flip(f_pre[1])))
    h = (h_fwd + h_bwd).transpose(0, 2, 1, 3)
    h = h * lax.rsqrt(jnp.mean(h * h, axis=-1, keepdims=True) + EPS)
    h = h.reshape(B, S, MLSTM_WIDTH) * head_norm.astype(jnp.float32)
    out = (h + skip.astype(jnp.float32) * xc.astype(jnp.float32)) * jax.nn.sigmoid(m_o.astype(jnp.float32))
    return out.astype(m_x.dtype)

def fnet_mixer(z, w, b):
    B, S, _ = z.shape
    zg = z.reshape(B, S, FNET_GROUPS, FNET_GROUP_DIM).astype(jnp.float32)
    y = jnp.fft.fftn(zg, axes=(1, 3), norm='ortho').real.astype(z.dtype)
    return jnp.einsum('bsgc,gce->bsge', y, w).reshape(B, S, FNET_WIDTH) + b

def first_inputs(seed: int = 0) -> dict:
    key = jax.random.key(seed)
    ks = iter(jax.random.split(key, 40))
    f32 = jnp.float32

    def nrm(shape, fan_in):
        return jax.random.normal(next(ks), shape, f32) * fan_in ** -0.5

    def gain(shape):
        return 1.0 + 0.02 * jax.random.normal(next(ks), shape, f32)

    Ld = DEPTH
    x = jax.random.normal(next(ks), (BATCH, SEQ, D_MODEL), f32)
    p = jax.random.normal(next(ks), (DEPTH, BATCH, SEQ, PLE_DIM), f32)
    offsets = jax.random.randint(next(ks), (BATCH, 1), 0, 4096, dtype=jnp.int32)
    positions = offsets + jnp.arange(SEQ, dtype=jnp.int32)[None, :]
    f_lin = jnp.linspace(3.0, 6.0, MLSTM_HEADS, dtype=f32)
    return {
        'x': x,
        'p': p,
        'positions': positions,
        'ffn1_norm': gain((Ld, D_MODEL)),
        'ffn1_w_gate': nrm((Ld, D_MODEL, D_FF), D_MODEL),
        'ffn1_w_up': nrm((Ld, D_MODEL, D_FF), D_MODEL),
        'ffn1_w_down': nrm((Ld, D_FF, D_MODEL), D_FF),
        'mix_norm': gain((Ld, D_MODEL)),
        'w_in': nrm((Ld, D_MODEL, D_IN), D_MODEL),
        'mla_q_norm': gain((Ld, MLA_Q_LORA)),
        'mla_w_uq': nrm((Ld, MLA_Q_LORA, MLA_HEADS * (MLA_NOPE_DIM + MLA_ROPE_DIM)), MLA_Q_LORA),
        'mla_kv_norm': gain((Ld, MLA_KV_LORA)),
        'mla_w_ukv': nrm((Ld, MLA_KV_LORA, MLA_HEADS * (MLA_NOPE_DIM + MLA_V_DIM)), MLA_KV_LORA),
        'mlstm_conv_w': nrm((Ld, MLSTM_CONV, MLSTM_WIDTH), MLSTM_CONV),
        'mlstm_conv_b': 0.02 * jax.random.normal(next(ks), (Ld, MLSTM_WIDTH), f32),
        'mlstm_w_q': nrm((Ld, MLSTM_HEADS, MLSTM_HEAD_DIM, MLSTM_HEAD_DIM), MLSTM_HEAD_DIM),
        'mlstm_w_k': nrm((Ld, MLSTM_HEADS, MLSTM_HEAD_DIM, MLSTM_HEAD_DIM), MLSTM_HEAD_DIM),
        'mlstm_i_bias': 0.1 * jax.random.normal(next(ks), (Ld, 2, MLSTM_HEADS), f32),
        'mlstm_f_bias': f_lin + 0.1 * jax.random.normal(next(ks), (Ld, 2, MLSTM_HEADS), f32),
        'mlstm_head_norm': gain((Ld, MLSTM_WIDTH)),
        'mlstm_skip': gain((Ld, MLSTM_WIDTH)),
        'fnet_w': nrm((Ld, FNET_GROUPS, FNET_GROUP_DIM, FNET_GROUP_DIM), FNET_GROUP_DIM),
        'fnet_b': 0.02 * jax.random.normal(next(ks), (Ld, FNET_WIDTH), f32),
        'w_out': nrm((Ld, MIX_WIDTH, D_MODEL), MIX_WIDTH),
        'ffn2_norm': gain((Ld, D_MODEL)),
        'ffn2_w_gate': nrm((Ld, D_MODEL, D_FF), D_MODEL),
        'ffn2_w_up': nrm((Ld, D_MODEL, D_FF), D_MODEL),
        'ffn2_w_down': nrm((Ld, D_FF, D_MODEL), D_FF),
        'ple_gate_norm': gain((Ld, D_MODEL)),
        'ple_w_gate': nrm((Ld, D_MODEL, D_MODEL), D_MODEL),
        'ple_w_proj': nrm((Ld, PLE_DIM, D_MODEL), PLE_DIM),
        'ple_post_norm': gain((Ld, D_MODEL)),
        'final_norm': gain((D_MODEL,)),
    }

def first_block(x, p, positions, ffn1_norm, ffn1_w_gate, ffn1_w_up, ffn1_w_down, mix_norm, w_in,
              mla_q_norm, mla_w_uq, mla_kv_norm, mla_w_ukv, mlstm_conv_w, mlstm_conv_b, mlstm_w_q, mlstm_w_k,
              mlstm_i_bias, mlstm_f_bias, mlstm_head_norm, mlstm_skip, fnet_w, fnet_b, w_out,
              ffn2_norm, ffn2_w_gate, ffn2_w_up, ffn2_w_down, ple_gate_norm, ple_w_gate, ple_w_proj,
              ple_post_norm, final_norm):
    cos, sin = rope_tables(positions)
    h = x
    for i in range(DEPTH):
        h = h + 0.5 * swiglu(rmsnorm(h, ffn1_norm[i]), ffn1_w_gate[i], ffn1_w_up[i], ffn1_w_down[i])
        u = rmsnorm(h, mix_norm[i]) @ w_in[i]
        c_q, c_kv, k_rope, m_x, m_v, m_o, m_if, f_in = split_cols(u, IN_SPLITS)
        y_mla = mla_mixer(c_q, c_kv, k_rope, cos, sin, mla_q_norm[i], mla_w_uq[i], mla_kv_norm[i], mla_w_ukv[i])
        y_mlstm = mlstm_mixer(m_x, m_v, m_o, m_if, mlstm_conv_w[i], mlstm_conv_b[i], mlstm_w_q[i], mlstm_w_k[i],
                              mlstm_i_bias[i], mlstm_f_bias[i], mlstm_head_norm[i], mlstm_skip[i])
        y_fnet = fnet_mixer(f_in, fnet_w[i], fnet_b[i])
        y = jnp.concatenate([y_mla, y_mlstm, y_fnet], axis=-1)
        h = h + y @ w_out[i]
        h = h + 0.5 * swiglu(rmsnorm(h, ffn2_norm[i]), ffn2_w_gate[i], ffn2_w_up[i], ffn2_w_down[i])
        e = rmsnorm(p[i] @ ple_w_proj[i], ple_post_norm[i])
        gate = jax.nn.sigmoid(rmsnorm(h, ple_gate_norm[i]) @ ple_w_gate[i])
        h = h + gate * e
    return rmsnorm(h, final_norm)


HEAD_DIM = 64
A_Q_HEADS = 8
A_KV_HEADS = 2
WINDOW = 128
ROPE_DIM = HEAD_DIM // 4
ROPE_THETA_2 = 500000.0
B_HEADS = 4
B_DK = 64
B_DV = 64
C_HEADS = 4
C_DK = 64
C_DV = 64
CONV_WIDTH = 4
CHUNK = 64
D_FF_2 = -(-8 * D_MODEL // (3 * 256)) * 256
D_MIX = A_Q_HEADS * HEAD_DIM + B_HEADS * B_DV + C_HEADS * C_DV
C_CONV_CH = C_HEADS * (2 * C_DK + C_DV)
IN_SIZES = (A_Q_HEADS * HEAD_DIM, A_KV_HEADS * HEAD_DIM, A_KV_HEADS * HEAD_DIM,
            B_HEADS * B_DK, B_HEADS * B_DK, B_HEADS * B_DV, B_HEADS * B_DV,
            C_CONV_CH, C_HEADS * C_DV, C_HEADS, C_HEADS)
D_IN_2 = sum(IN_SIZES)
NORM_EPS = 1e-6


def rmsnorm_2(x, gain):
    xf = x.astype(jnp.float32)
    y = xf * lax.rsqrt(jnp.mean(xf * xf, axis=-1, keepdims=True) + NORM_EPS)
    return (y * gain.astype(jnp.float32)).astype(x.dtype)

def l2norm(x):
    return x * lax.rsqrt(jnp.sum(x * x, axis=-1, keepdims=True) + NORM_EPS)

def partial_rope(x, positions):
    half = ROPE_DIM // 2
    inv_freq = ROPE_THETA_2 ** (-jnp.arange(half, dtype=jnp.float32) * 2.0 / ROPE_DIM)
    ang = positions.astype(jnp.float32)[..., None] * inv_freq
    cos = jnp.cos(ang)[:, :, None, :]
    sin = jnp.sin(ang)[:, :, None, :]
    xf = x.astype(jnp.float32)
    x1, x2, xp = xf[..., :half], xf[..., half:ROPE_DIM], xf[..., ROPE_DIM:]
    out = jnp.concatenate([x1 * cos - x2 * sin, x2 * cos + x1 * sin, xp], axis=-1)
    return out.astype(x.dtype)

def sliding_window_attention(q, k, v, sinks):
    b, s, hq, d = q.shape
    hkv = k.shape[2]
    grp = hq // hkv
    nb = s // WINDOW
    qb = q.reshape(b, nb, WINDOW, hkv, grp, d)

    def band(t):
        tb = t.reshape(b, nb, WINDOW, hkv, d)
        prev = jnp.concatenate([jnp.zeros_like(tb[:, :1]), tb[:, :-1]], axis=1)
        return jnp.concatenate([prev, tb], axis=2)

    kb, vb = band(k), band(v)
    scores = jnp.einsum('bnqhgd,bnkhd->bnhgqk', qb, kb).astype(jnp.float32) * (d ** -0.5)
    qi = jnp.arange(WINDOW)[:, None]
    kj = jnp.arange(2 * WINDOW)[None, :]
    delta = qi + WINDOW - kj
    blk = jnp.arange(nb)[:, None, None]
    valid = (delta >= 0) & (delta < WINDOW) & (blk * WINDOW + kj - WINDOW >= 0)
    scores = jnp.where(valid[None, :, None, None], scores, -jnp.inf)
    sink = sinks.astype(jnp.float32).reshape(hkv, grp)[None, None, :, :, None, None]
    m = jnp.maximum(scores.max(axis=-1, keepdims=True), sink)
    p = jnp.exp(scores - m)
    denom = p.sum(axis=-1, keepdims=True) + jnp.exp(sink - m)
    out = jnp.einsum('bnhgqk,bnkhd->bnqhgd', (p / denom).astype(v.dtype), vb)
    return out.reshape(b, s, hq * d)

def hgrn2_chunked(q, log_f, v):
    b, s, h, dk = q.shape
    dv = v.shape[-1]
    nc = s // CHUNK

    def to_chunks(t):
        return t.reshape(b, nc, CHUNK, h, t.shape[-1]).transpose(1, 0, 3, 2, 4)

    causal = jnp.tril(jnp.ones((CHUNK, CHUNK), dtype=bool))

    def step(state, inp):
        qt, lf, vt = inp
        kt = -jnp.expm1(lf)
        cum = jnp.cumsum(lf, axis=2)
        diff = cum[:, :, :, None, :] - cum[:, :, None, :, :]
        decay = jnp.exp(jnp.where(causal[:, :, None], diff, -jnp.inf))
        attn = jnp.einsum('bhtd,bhsd,bhtsd->bhts', qt, kt, decay)
        o = attn @ vt + jnp.einsum('bhtd,bhde->bhte', qt * jnp.exp(cum), state)
        last = cum[:, :, -1:, :]
        state = jnp.exp(last[:, :, 0, :, None]) * state + jnp.einsum('bhsd,bhse->bhde', kt * jnp.exp(last - cum), vt)
        return state, o

    state0 = jnp.zeros((b, h, dk, dv), jnp.float32)
    _, o = lax.scan(step, state0, (to_chunks(q), to_chunks(log_f), to_chunks(v)))
    return o.transpose(1, 0, 3, 2, 4).reshape(b, s, h, dv)

def causal_depthwise_conv(x, w):
    ch = x.shape[-1]
    return lax.conv_general_dilated(x, w[:, None, :].astype(x.dtype), window_strides=(1,),
                                    padding=[(CONV_WIDTH - 1, 0)],
                                    dimension_numbers=('NWC', 'WIO', 'NWC'),
                                    feature_group_count=ch)

def gated_delta_chunked(q, k, v, beta, g):
    b, s, h, dk = q.shape
    dv = v.shape[-1]
    nc = s // CHUNK

    def to_chunks(t):
        return jnp.swapaxes(t.reshape((b, nc, CHUNK) + t.shape[2:]), 2, 3)

    qc, kc, vc, bc, gc = (to_chunks(t) for t in (q, k, v, beta, g))
    G = jnp.cumsum(gc, axis=-1)
    incl = jnp.tril(jnp.ones((CHUNK, CHUNK), dtype=bool))
    strict = jnp.tril(jnp.ones((CHUNK, CHUNK), dtype=bool), k=-1)
    L = jnp.exp(jnp.where(incl, G[..., :, None] - G[..., None, :], -jnp.inf))
    kb = kc * bc[..., None]
    A = jnp.where(strict, jnp.einsum('bnhtd,bnhsd->bnhts', kb, kc) * L, 0.0)
    eye = jnp.eye(CHUNK, dtype=jnp.float32)
    T = lax.linalg.triangular_solve(eye + A, jnp.broadcast_to(eye, A.shape), left_side=True,
                                    lower=True, unit_diagonal=True)
    U = T @ (vc * bc[..., None])
    W = T @ (kb * jnp.exp(G)[..., None])
    qk = jnp.where(incl, jnp.einsum('bnhtd,bnhsd->bnhts', qc, kc) * L, 0.0)
    q_dec = qc * jnp.exp(G)[..., None]
    k_dec = kc * jnp.exp(G[..., -1:] - G)[..., None]
    g_last = jnp.exp(G[..., -1])

    def step(state, inp):
        u, w, qd, kd, qkc, gl = inp
        v_new = u - w @ state
        o = qd @ state + qkc @ v_new
        state = gl[..., None, None] * state + jnp.swapaxes(kd, -1, -2) @ v_new
        return state, o

    xs = tuple(jnp.moveaxis(t, 1, 0) for t in (U, W, q_dec, k_dec, qk, g_last))
    state0 = jnp.zeros((b, h, dk, dv), jnp.float32)
    _, o = lax.scan(step, state0, xs)
    return jnp.swapaxes(jnp.moveaxis(o, 0, 1), 2, 3).reshape(b, s, h, dv)

def hybrid_mixer(h, positions, w_in, q_norm, k_norm, sinks, lb, hgrn_norm, conv_w, a_log, dt_bias,
                 gdn_norm, w_out):
    b, s, _ = h.shape
    f32 = jnp.float32
    proj = h @ w_in
    split_at = [int(i) for i in np.cumsum(IN_SIZES)[:-1]]
    aq, ak, av, bq, bf, bv, bg, cqkv, cg, cb, ca = jnp.split(proj, split_at, axis=-1)

    aq = partial_rope(rmsnorm_2(aq.reshape(b, s, A_Q_HEADS, HEAD_DIM), q_norm), positions)
    ak = partial_rope(rmsnorm_2(ak.reshape(b, s, A_KV_HEADS, HEAD_DIM), k_norm), positions)
    av = av.reshape(b, s, A_KV_HEADS, HEAD_DIM)
    out_a = sliding_window_attention(aq, ak, av, sinks)

    lb = lb.astype(f32).reshape(B_HEADS, B_DK)
    z = bf.reshape(b, s, B_HEADS, B_DK).astype(f32)
    log_f = jnp.logaddexp(jnp.log(lb), jnp.log1p(-lb) + jax.nn.log_sigmoid(z))
    o_b = hgrn2_chunked(bq.reshape(b, s, B_HEADS, B_DK).astype(f32), log_f,
                        bv.reshape(b, s, B_HEADS, B_DV).astype(f32))
    out_b = rmsnorm_2(o_b, hgrn_norm) * jax.nn.silu(bg.reshape(b, s, B_HEADS, B_DV).astype(f32))
    out_b = out_b.reshape(b, s, B_HEADS * B_DV).astype(h.dtype)

    cqkv = jax.nn.silu(causal_depthwise_conv(cqkv, conv_w))
    cq, ck, cv = jnp.split(cqkv, [C_HEADS * C_DK, 2 * C_HEADS * C_DK], axis=-1)
    cq = l2norm(cq.reshape(b, s, C_HEADS, C_DK).astype(f32)) * (C_DK ** -0.5)
    ck = l2norm(ck.reshape(b, s, C_HEADS, C_DK).astype(f32))
    cv = cv.reshape(b, s, C_HEADS, C_DV).astype(f32)
    beta = jax.nn.sigmoid(cb.astype(f32))
    g = -jnp.exp(a_log.astype(f32)) * jax.nn.softplus(ca.astype(f32) + dt_bias.astype(f32))
    o_c = gated_delta_chunked(cq, ck, cv, beta, g)
    out_c = rmsnorm_2(o_c, gdn_norm) * jax.nn.silu(cg.reshape(b, s, C_HEADS, C_DV).astype(f32))
    out_c = out_c.reshape(b, s, C_HEADS * C_DV).astype(h.dtype)

    mixed = jnp.concatenate([out_a, out_b, out_c], axis=-1)
    return mixed @ w_out

def swiglu_2(h, w_gate, w_up, w_down):
    return (jax.nn.silu(h @ w_gate) * (h @ w_up)) @ w_down

def second_inputs(seed: int = 0) -> dict:
    key = jax.random.key(seed)
    ks = jax.random.split(key, 24)
    f32 = jnp.float32

    def nrm(k, shape, scale):
        return jax.random.normal(k, shape, f32) * scale

    x = nrm(ks[0], (BATCH, SEQ, D_MODEL), 1.0)
    c = nrm(ks[1], (BATCH, D_MODEL), 1.0)
    positions = jnp.broadcast_to(jnp.arange(SEQ, dtype=jnp.int32)[None, :], (BATCH, SEQ))
    ada_w = nrm(ks[2], (DEPTH, D_MODEL, 6 * D_MODEL), 0.5 * D_MODEL ** -0.5)
    ada_b = nrm(ks[3], (DEPTH, 6 * D_MODEL), 0.02)
    norm_mix = 1.0 + nrm(ks[4], (DEPTH, D_MODEL), 0.05)
    w_in = nrm(ks[5], (DEPTH, D_MODEL, D_IN_2), D_MODEL ** -0.5)
    attn_q_norm = 1.0 + nrm(ks[6], (DEPTH, HEAD_DIM), 0.05)
    attn_k_norm = 1.0 + nrm(ks[7], (DEPTH, HEAD_DIM), 0.05)
    attn_sinks = nrm(ks[8], (DEPTH, A_Q_HEADS), 1.0)
    hgrn_lb_logits = nrm(ks[9], (DEPTH, B_HEADS * B_DK), 1.0)
    hgrn_out_norm = 1.0 + nrm(ks[10], (DEPTH, B_DV), 0.05)
    gdn_conv_w = nrm(ks[11], (DEPTH, CONV_WIDTH, C_CONV_CH), CONV_WIDTH ** -0.5)
    gdn_a_log = jnp.log(jax.random.uniform(ks[12], (DEPTH, C_HEADS), f32, 1.0, 16.0))
    dt = jnp.exp(jax.random.uniform(ks[13], (DEPTH, C_HEADS), f32, math.log(1e-3), math.log(1e-1)))
    gdn_dt_bias = dt + jnp.log(-jnp.expm1(-dt))
    gdn_out_norm = 1.0 + nrm(ks[14], (DEPTH, C_DV), 0.05)
    w_out = nrm(ks[15], (DEPTH, D_MIX, D_MODEL), D_MIX ** -0.5)
    norm_ffn = 1.0 + nrm(ks[16], (DEPTH, D_MODEL), 0.05)
    w_gate = nrm(ks[17], (DEPTH, D_MODEL, D_FF_2), D_MODEL ** -0.5)
    w_up = nrm(ks[18], (DEPTH, D_MODEL, D_FF_2), D_MODEL ** -0.5)
    w_down = nrm(ks[19], (DEPTH, D_FF_2, D_MODEL), D_FF_2 ** -0.5)
    return {'x': x, 'c': c, 'positions': positions, 'ada_w': ada_w, 'ada_b': ada_b,
            'norm_mix': norm_mix, 'w_in': w_in, 'attn_q_norm': attn_q_norm,
            'attn_k_norm': attn_k_norm, 'attn_sinks': attn_sinks, 'hgrn_lb_logits': hgrn_lb_logits,
            'hgrn_out_norm': hgrn_out_norm, 'gdn_conv_w': gdn_conv_w, 'gdn_a_log': gdn_a_log,
            'gdn_dt_bias': gdn_dt_bias, 'gdn_out_norm': gdn_out_norm, 'w_out': w_out,
            'norm_ffn': norm_ffn, 'w_gate': w_gate, 'w_up': w_up, 'w_down': w_down}

def second_block(x, c, positions, ada_w, ada_b, norm_mix, w_in, attn_q_norm, attn_k_norm, attn_sinks,
              hgrn_lb_logits, hgrn_out_norm, gdn_conv_w, gdn_a_log, gdn_dt_bias, gdn_out_norm, w_out,
              norm_ffn, w_gate, w_up, w_down):
    lb_cum = jnp.cumsum(jax.nn.softmax(hgrn_lb_logits.astype(jnp.float32), axis=0), axis=0)
    lower_bounds = lb_cum - lb_cum[:1]
    cond = jax.nn.silu(c)
    for l in range(DEPTH):
        mod = cond @ ada_w[l] + ada_b[l]
        sh_m, sc_m, gt_m, sh_f, sc_f, gt_f = [m[:, None, :] for m in jnp.split(mod, 6, axis=-1)]
        h = rmsnorm_2(x, norm_mix[l]) * (1 + sc_m) + sh_m
        y = hybrid_mixer(h, positions, w_in[l], attn_q_norm[l], attn_k_norm[l], attn_sinks[l],
                         lower_bounds[l], hgrn_out_norm[l], gdn_conv_w[l], gdn_a_log[l],
                         gdn_dt_bias[l], gdn_out_norm[l], w_out[l])
        x = x + gt_m * y
        h = rmsnorm_2(x, norm_ffn[l]) * (1 + sc_f) + sh_f
        x = x + gt_f * swiglu_2(h, w_gate[l], w_up[l], w_down[l])
    return x


def setup_inputs(seed=0):
    out = dict(first_inputs(seed))
    for name, value in second_inputs(seed + 1).items():
        if name != "x":
            out[name + "_2"] = value
    return out


def reference(
    x, p, positions, ffn1_norm, ffn1_w_gate, ffn1_w_up, ffn1_w_down, mix_norm, w_in, mla_q_norm,
    mla_w_uq, mla_kv_norm, mla_w_ukv, mlstm_conv_w, mlstm_conv_b, mlstm_w_q, mlstm_w_k,
    mlstm_i_bias, mlstm_f_bias, mlstm_head_norm, mlstm_skip, fnet_w, fnet_b, w_out, ffn2_norm,
    ffn2_w_gate, ffn2_w_up, ffn2_w_down, ple_gate_norm, ple_w_gate, ple_w_proj, ple_post_norm,
    final_norm, c_2, positions_2, ada_w_2, ada_b_2, norm_mix_2, w_in_2, attn_q_norm_2,
    attn_k_norm_2, attn_sinks_2, hgrn_lb_logits_2, hgrn_out_norm_2, gdn_conv_w_2, gdn_a_log_2,
    gdn_dt_bias_2, gdn_out_norm_2, w_out_2, norm_ffn_2, w_gate_2, w_up_2, w_down_2,
):
    x = first_block(
        x, p, positions, ffn1_norm, ffn1_w_gate, ffn1_w_up, ffn1_w_down, mix_norm, w_in,
        mla_q_norm, mla_w_uq, mla_kv_norm, mla_w_ukv, mlstm_conv_w, mlstm_conv_b, mlstm_w_q,
        mlstm_w_k, mlstm_i_bias, mlstm_f_bias, mlstm_head_norm, mlstm_skip, fnet_w, fnet_b,
        w_out, ffn2_norm, ffn2_w_gate, ffn2_w_up, ffn2_w_down, ple_gate_norm, ple_w_gate,
        ple_w_proj, ple_post_norm, final_norm,
    )
    return second_block(
        x, c_2, positions_2, ada_w_2, ada_b_2, norm_mix_2, w_in_2, attn_q_norm_2, attn_k_norm_2,
        attn_sinks_2, hgrn_lb_logits_2, hgrn_out_norm_2, gdn_conv_w_2, gdn_a_log_2,
        gdn_dt_bias_2, gdn_out_norm_2, w_out_2, norm_ffn_2, w_gate_2, w_up_2, w_down_2,
    )


_drawn_inputs = setup_inputs


def setup_inputs(seed=0):
    import zlib

    import numpy as np

    out = dict(_drawn_inputs(seed))
    spreads = {}
    factors = {'ffn1_norm': 4.462,
     'mix_norm': 2.796,
     'mla_q_norm': 8.0,
     'mla_kv_norm': 8.0,
     'mlstm_conv_b': 2.794,
     'mlstm_i_bias': 8.0,
     'mlstm_head_norm': 8.0,
     'mlstm_skip': 8.0,
     'fnet_b': 3.896,
     'ffn2_norm': 5.568,
     'ple_gate_norm': 8.0,
     'ple_post_norm': 4.555,
     'norm_mix_2': 2.685,
     'attn_q_norm_2': 8.0,
     'attn_k_norm_2': 8.0,
     'attn_sinks_2': 200.0,
     'hgrn_out_norm_2': 7.925,
     'gdn_a_log_2': 3.366,
     'gdn_out_norm_2': 7.901,
     'norm_ffn_2': 5.479}
    for name, (base, spread) in spreads.items():
        noise = np.random.default_rng([zlib.crc32(name.encode()), seed]).standard_normal(out[name].shape)
        drawn = base * np.exp(spread * noise) if base else spread * noise
        out[name] = __import__('jax').numpy.asarray(drawn.astype(out[name].dtype))
    for name, factor in factors.items():
        out[name] = (out[name] * factor).astype(out[name].dtype)
    return out
```

```python
import math
from contextlib import ExitStack

import numpy as np

import concourse.bass as bass
from concourse import mybir

F32 = mybir.dt.float32
I32 = mybir.dt.int32
ALU = mybir.AluOpType
ACT = mybir.ActivationFunctionType
AX = mybir.AxisListType

P = 128
S = 512
ST = S // P
D = 1024
DT = D // P
FF = 2816
FT = FF // P
DEPTH = 2
HD = 64
H = 4
EPS = 1e-6
BIG = 1e30
LEVELS = [1 << e for e in range(7)]
MLA_SCALE = (128 + 64) ** -0.5


def constant_columns():
    f = np.float32
    i = np.arange(P)
    same64 = (i[:, None] // 64 == i[None, :] // 64)
    out = {"ident": np.eye(P, dtype=f), "ones": np.ones((P, P), f), "heads": same64.astype(f)}

    def rotation(width):
        r = np.zeros((P, P), f)
        for base in (0, 64):
            for m in range(width // 2):
                r[base + m + width // 2, base + m] = -1.0
                r[base + m, base + m + width // 2] = 1.0
        return r

    out["rot_mla"] = rotation(64)
    out["rot_win"] = rotation(16)
    out["upto"] = (i[:, None] <= i[None, :]).astype(f)
    out["from"] = (i[:, None] >= i[None, :]).astype(f)
    out["strict4"] = np.tile((i[:, None] < i[None, :]).astype(f), (1, ST))
    lev = [((i[:, None] // (2 * L) == i[None, :] // (2 * L)) & (i[:, None] % (2 * L) < L)
            & (i[None, :] % (2 * L) >= L)).astype(f) for L in LEVELS]
    out["levels"] = np.concatenate(lev, 1)
    q, k = i[:, None], np.arange(2 * P)[None, :]
    delta = q + P - k
    rest = np.where((delta >= 0) & (delta < P), 0.0, -BIG).astype(f)
    first = np.where(k >= P, rest, -BIG).astype(f)
    out["window"] = np.concatenate([first, rest, rest], 1)
    out["restart"] = np.tile((np.arange(S) % P != 0).astype(f), (P, 1))
    c = np.arange(HD)
    ang = 2 * np.pi * ((c[:, None] * c[None, :]) % HD) / HD
    z = np.zeros((P, P), f)
    dc, ds = z.copy(), z.copy()
    for b in (0, HD):
        dc[b:b + HD, b:b + HD] = np.cos(ang)
        ds[b:b + HD, b:b + HD] = -np.sin(ang)
    out["dft_c"], out["dft_s"] = dc, ds
    sel = np.zeros((36, 8, P), f)
    selp = np.zeros((36, 4, P), f)
    for d in range(2):
        for h in range(H):
            sel[32 * d + h, 4 * d + h] = 1.0
            selp[32 * d + h, 2 * d + h // 2, 64 * (h % 2):64 * (h % 2) + 64] = 1.0
    out["sel"] = sel.reshape(36, -1)
    out["selp"] = selp.reshape(36, -1)
    inv1 = np.zeros((P, 1), f)
    inv2 = np.zeros((P, 1), f)
    for b in (0, 64):
        t = 1.0 / (10000.0 ** (np.arange(0, 64, 2) / 64.0))
        inv1[b:b + 32, 0] = t
        inv1[b + 32:b + 64, 0] = t
        t = 500000.0 ** (-np.arange(8) * 2.0 / 16.0)
        inv2[b:b + 8, 0] = t
        inv2[b + 8:b + 16, 0] = t
    out["inv_mla"], out["inv_win"] = inv1, inv2
    out["eps"] = np.full((P, 1), EPS, f)
    out["one"] = np.full((P, 1), 1.0, f)
    return out


def pack(columns):
    at, where = 0, {}
    for name, a in columns.items():
        where[name] = (at, a.shape[1], a.shape[0])
        at += a.shape[1]
    whole = np.zeros((P, at), np.float32)
    for name, a in columns.items():
        whole[:a.shape[0], where[name][0]:where[name][0] + a.shape[1]] = a
    return whole, where


PAR1 = {"ffn1_norm": 8, "mix_norm": 8, "q_norm": 3, "kv_norm": 2, "conv_w": 10, "conv_b": 2, "i_bias": 1,
        "f_bias": 1, "head_norm": 2, "skip": 2, "fnet_b": 2, "ffn2_norm": 8, "gate_norm": 8, "post_norm": 8}
PAR2 = {"norm_mix": 8, "q_norm": 1, "k_norm": 1, "sinks": 8, "hgrn_norm": 1, "conv_w": 24, "a_log": 1,
        "dt_bias": 1, "gdn_norm": 1, "norm_ffn": 8, "ada_b": 48}
PARG = {"final_norm": 8, "cond": 8, "lb": 4}


def columns_of(table):
    at, out = 0, {}
    for name, n in table.items():
        out[name] = (at, n)
        at += n
    return out, at


def build(nc, t, where):
    ctx = ExitStack()
    with ctx:
        program(nc, t, where, ctx)


def program(nc, t, where, ctx):
    def sb(name, shape, dt=F32):
        return ctx.enter_context(nc.sbuf_tensor(name, shape, dt))

    h = sb("stream", [P, DT, S])
    n = sb("normed", [P, DT, S])
    cst = sb("consts", [P, t["cst"].shape[1]])
    c1, n1 = columns_of(PAR1)
    c2, n2 = columns_of(PAR2)
    cg, ng = columns_of(PARG)
    par = sb("par", [P, max(n1, n2)])
    parg = sb("parg", [P, ng])
    rope = sb("rope", [P, 4, S])
    mod = sb("mod", [P, DEPTH, 48])
    lbt = sb("lbt", [P, DEPTH, 3, 2])
    ARENA = 36500
    arena = sb("arena", [P, ARENA])
    ps = [ctx.enter_context(nc.psum_tensor(f"ps{i}", [P, S], F32)) for i in range(8)]

    class Stage:

        def __init__(self):
            self.held = ExitStack()
            self.sems = {}

        def sem(self, name):
            if name not in self.sems:
                self.sems[name] = self.held.enter_context(nc.semaphore(name))
            return self.sems[name]

        def __enter__(self):
            self.manager = nc.Block()
            self.block = self.manager.__enter__()
            return self

        def __exit__(self, *e):
            r = self.manager.__exit__(*e)
            if e[0] is None:
                with nc.Block() as cleared:
                    @cleared.sync
                    def _(sp):
                        for sem in self.sems.values():
                            sp.sem_clear(sem)
            self.held.close()
            return r

    class Order:

        def __init__(self, eng, sem):
            self.eng, self.sem, self.count = eng, sem, 0

        def tick(self, ins):
            ins.then_inc(self.sem, 1)
            self.count += 1
            return self.count

        def done(self, ins):
            self.tick(ins)
            self.eng.wait_ge(self.sem, self.count)

    class Space:

        def __init__(self, at=0):
            self.at = at

        def get(self, *shape):
            size = int(np.prod(shape))
            a = arena[:, self.at:self.at + size]
            self.at += size
            assert self.at <= ARENA, self.at
            names = "abcd"[:len(shape)]
            if len(shape) > 1:
                a = a.rearrange(f"p ({' '.join(names)}) -> p {' '.join(names)}",
                                **dict(zip(names[1:], shape[1:])))
            return a

    def C(name, rows=None, a=0, b=None):
        at, width, r = where[name]
        return cst[0:(rows or r), at + a:at + (width if b is None else b)]

    def col(table, name, k=0, rows=P):
        at, width = table[name]
        src = parg if table is cg else par
        return src[0:rows, at + k:at + k + 1]

    V, A, T, G = nc.vector, nc.scalar, nc.tensor, nc.gpsimd

    class Norm:

        def __init__(self, st, name, src, dst, gains, width, space, bank, lhs="ones", shifts=None, mult=None):
            self.src, self.dst, self.gains, self.width, self.lhs = src, dst, gains, width, lhs
            self.shifts = shifts
            self.k = len(src)
            self.bank = bank
            self.sq = space.get(2, S)
            self.root = space.get(S)
            self.rstd = space.get(S)
            self.squares = st.sem(name + "_squares")
            self.summed = st.sem(name + "_summed")
            self.rooted = st.sem(name + "_rooted")
            self.inverted = st.sem(name + "_inverted")
            self.ready = st.sem(name + "_ready")
            self.scaled = st.sem(name + "_scaled") if shifts else None

        def act(self, act):
            for k in range(self.k):
                if k >= 2:
                    act.wait_ge(self.summed, k - 1)
                A.activation(self.sq[:, k % 2, :], self.src[k], ACT.Square).then_inc(self.squares, 1)
            act.wait_ge(self.summed, self.k)
            A.activation(self.root, self.bank, ACT.Sqrt, scale=1.0 / self.width, bias=C("eps")) \
             .then_inc(self.rooted, 1)
            if self.shifts:
                for k in range(self.k):
                    act.wait_ge(self.scaled, k + 1)
                    A.activation(self.dst[k], self.dst[k], ACT.Identity, bias=self.shifts[k]) \
                     .then_inc(self.ready, 1)

        def pe(self, pe):
            for k in range(self.k):
                pe.wait_ge(self.squares, k + 1)
                T.matmul(self.bank, C(self.lhs), self.sq[:, k % 2, :], start=(k == 0), stop=(k == self.k - 1)) \
                 .then_inc(self.summed, 1)

        def dve(self, dve):
            dve.wait_ge(self.rooted, 1)
            V.reciprocal(self.rstd, self.root).then_inc(self.inverted, 1)
            dve.wait_ge(self.inverted, 1)
            for k in range(self.k):
                V.scalar_tensor_tensor(out=self.dst[k], in0=self.src[k], scalar=self.gains[k], in1=self.rstd,
                                       op0=ALU.mult, op1=ALU.mult) \
                 .then_inc(self.scaled if self.shifts else self.ready, 1)

    def feed_forward(l, w_gu, w_dn, gains, shifts=None, gate=None):
        sp_ = Space()
        hid = sp_.get(FT, S)
        gu = [sp_.get(2, DT, P) for _ in range(2)]
        dn = [sp_.get(FT, P) for _ in range(2)]
        sil = sp_.get(2, S)
        with Stage() as st:
            norm = Norm(st, "norm", [h[:, k, :] for k in range(DT)], [n[:, k, :] for k in range(DT)],
                        gains, D, sp_, ps[6][:, :], shifts=shifts)
            gu_free, dn_free = st.sem("gu_free"), st.sem("dn_free")
            gu_landed = [st.sem(f"gu_landed{b}") for b in range(2)]
            dn_landed = [st.sem(f"dn_landed{b}") for b in range(2)]
            gu_done, silu_ready = st.sem("gu_done"), st.sem("silu_ready")
            hid_ready, down_done, h_updated = st.sem("hid_ready"), st.sem("down_done"), st.sem("h_updated")

            @st.block.sync
            def _(sp):
                with sp.Fori(0, FT // 2) as i:
                    for b in range(2):
                        sp.wait_ge(gu_free, 2 * i + (b + 1))
                        sp.dma_start(gu[b].rearrange("p a k m -> p (a k m)"), w_gu[l, 2 * i + b, :, :]) \
                          .then_inc(gu_landed[b], 16)
                with sp.Fori(0, DT // 2) as i:
                    for b in range(2):
                        sp.wait_ge(dn_free, 2 * i + (b + 1))
                        sp.dma_start(dn[b].rearrange("p k m -> p (k m)"), w_dn[l, 2 * i + b, :, :]) \
                          .then_inc(dn_landed[b], 16)

            @st.block.tensor
            def _(pe):
                pe.sem_inc(gu_free, 2)
                pe.sem_inc(dn_free, 2)
                norm.pe(pe)
                pe.wait_ge(norm.ready, DT)
                with pe.Fori(0, FT // 2) as i:
                    for b in range(2):
                        pe.wait_ge(gu_landed[b], 16 * i + 16)
                        pe.wait_ge(hid_ready, 2 * i + (b + 1))
                        for a in range(2):
                            for k in range(DT):
                                mm = T.matmul(ps[2 * b + a][:, :], gu[b][:, a, k, :], n[:, k, :],
                                              start=(k == 0), stop=(k == DT - 1))
                            mm.then_inc(gu_done if a == 0 else gu_free, 1)
                pe.wait_ge(hid_ready, 2 + FT)
                with pe.Fori(0, DT // 2) as i:
                    for b in range(2):
                        pe.wait_ge(dn_landed[b], 16 * i + 16)
                        pe.wait_ge(h_updated, 2 * i + (b + 1))
                        for k in range(FT):
                            mm = T.matmul(ps[4 + b][:, :], dn[b][:, k, :], hid[:, k, :],
                                          start=(k == 0), stop=(k == FT - 1))
                        mm.then_inc(dn_free, 1)

            @st.block.scalar
            def _(act):
                norm.act(act)
                A.activation(sil[:, 0, 0:1], C("one"), ACT.Silu).then_inc(st.sem("table"), 1)
                act.wait_ge(st.sem("table"), 1)
                with act.Fori(0, FT // 2) as i:
                    for b in range(2):
                        act.wait_ge(gu_done, 2 * i + (b + 1))
                        act.wait_ge(hid_ready, 2 * i + (b + 1))
                        A.activation(sil[:, b, :], ps[2 * b][:, :], ACT.Silu).then_inc(silu_ready, 1)

            @st.block.vector
            def _(dve):
                dve.sem_inc(hid_ready, 2)
                dve.sem_inc(h_updated, 2)
                norm.dve(dve)
                with dve.Fori(0, FT // 2) as i:
                    for b in range(2):
                        dve.wait_ge(silu_ready, 2 * i + (b + 1))
                        dve.wait_ge(gu_free, 2 * i + (b + 3))
                        V.tensor_tensor(hid[:, bass.ds(2 * i + b, 1), :].rearrange("p a s -> p (a s)"),
                                        sil[:, b, :], ps[2 * b + 1][:, :], ALU.mult).then_inc(hid_ready, 1)
                if gate is None:
                    with dve.Fori(0, DT // 2) as i:
                        for b in range(2):
                            dve.wait_ge(dn_free, 2 * i + (b + 3))
                            hx = h[:, bass.ds(2 * i + b, 1), :].rearrange("p a s -> p (a s)")
                            V.scalar_tensor_tensor(out=hx, in0=ps[4 + b][:, :], scalar=0.5, in1=hx,
                                                   op0=ALU.mult, op1=ALU.add).then_inc(h_updated, 1)
                else:
                    for d in range(DT):
                        dve.wait_ge(dn_free, d + 3)
                        V.scalar_tensor_tensor(out=h[:, d, :], in0=ps[4 + d % 2][:, :], scalar=gate[d],
                                               in1=h[:, d, :], op0=ALU.mult, op1=ALU.add).then_inc(h_updated, 1)

    def products(bank, lhs, rhs, kt):
        for k in range(kt):
            mm = T.matmul(bank, lhs(k), rhs(k), start=(k == 0), stop=(k == kt - 1))
        return mm

    def load_inputs():
        sp_ = Space()
        posi = arena[:, 0:2 * S].bitcast(I32)
        sp_.at = 2 * S
        pos, turns, ang, red = sp_.get(2, S), sp_.get(S), sp_.get(S), sp_.get(S)
        shifted, over = sp_.get(S), sp_.get(S)
        lbx = sp_.get(16)
        c_hi = 6.28125
        c_mid = float(np.float32(2 * math.pi - c_hi))
        c_lo = float(2 * math.pi - c_hi - c_mid)
        magic = 1.5 * 2.0 ** 23
        top = 3.1415925
        with Stage() as st:
            landed, table_ready, reduced = st.sem("landed"), st.sem("table_ready"), st.sem("reduced")
            bounds_in, bounds_out = st.sem("bounds_in"), st.sem("bounds_out")

            @st.block.sync
            def _(sp):
                sp.dma_start(cst[:, :], t["cst"]).then_inc(landed, 16)
                sp.dma_start(parg[:, :], t["parg"]).then_inc(landed, 16)
                sp.dma_start(posi[:, 0:S], t["pos"].partition_broadcast(P)).then_inc(landed, 16)
                sp.dma_start(posi[:, S:2 * S], t["pos2"].partition_broadcast(P)).then_inc(landed, 16)
                sp.dma_start(h[:, :, :], t["x"].rearrange("(k p) s -> p k s", p=P)).then_inc(landed, 16)
                sp.wait_ge(landed, 80)

            @st.block.vector
            def _(dve):
                order = Order(dve, st.sem("dve_order"))
                dve.wait_ge(landed, 80)
                order.done(V.tensor_copy(pos.rearrange("p a s -> p (a s)"), posi))
                for r, inv in enumerate(("inv_mla", "inv_win")):
                    order.done(V.tensor_scalar(ang, pos[:, r, :], C(inv), None, ALU.mult))
                    order.done(V.tensor_scalar(turns, ang, 1.0 / (2 * math.pi), magic, ALU.mult, ALU.add))
                    order.done(V.tensor_scalar(turns, turns, magic, None, ALU.subtract))
                    order.done(V.scalar_tensor_tensor(out=red, in0=turns, scalar=-c_hi, in1=ang, op0=ALU.mult, op1=ALU.add))
                    order.done(V.scalar_tensor_tensor(out=red, in0=turns, scalar=-c_mid, in1=red, op0=ALU.mult, op1=ALU.add))
                    order.done(V.scalar_tensor_tensor(out=red, in0=turns, scalar=-c_lo, in1=red, op0=ALU.mult, op1=ALU.add))
                    order.done(V.tensor_scalar(shifted, red, math.pi / 2, None, ALU.add))
                    order.done(V.tensor_scalar(over, shifted, math.pi, -2 * math.pi, ALU.is_gt, ALU.mult))
                    order.done(V.tensor_tensor(shifted, shifted, over, ALU.add))
                    order.done(V.tensor_scalar(rope[:, 2 * r, :], shifted, top, -top, ALU.min, ALU.max))
                    V.tensor_scalar(rope[:, 2 * r + 1, :], red, top, -top, ALU.min, ALU.max).then_inc(reduced, 1)
                l0 = parg[:, cg["lb"][0]:cg["lb"][0] + 2]
                l1 = parg[:, cg["lb"][0] + 2:cg["lb"][0] + 4]
                top_ = lbx[:, 0:2]
                order.done(V.tensor_tensor(top_, l0, l1, ALU.max))
                order.done(V.tensor_tensor(lbx[:, 2:4], l0, top_, ALU.subtract))
                order.done(V.tensor_tensor(lbx[:, 4:6], l1, top_, ALU.subtract))
                V.tensor_copy(lbx[:, 12:14], lbx[:, 4:6]).then_inc(bounds_in, 1)
                dve.wait_ge(bounds_out, 1)
                order.done(V.tensor_tensor(lbx[:, 10:12], lbx[:, 6:8], lbx[:, 8:10], ALU.add))
                order.done(V.reciprocal(lbx[:, 12:14], lbx[:, 10:12]))
                V.tensor_copy(lbx[:, 14:16], lbx[:, 10:12]).then_inc(bounds_in, 1)
                order.done(V.memset(lbt[:, 0, 0, :], -BIG))
                order.done(V.memset(lbt[:, 0, 1, :], 0.0))
                order.done(V.memset(lbt[:, 0, 2, :], 1.0))
                order.done(V.tensor_tensor(lbt[:, 1, 2, :], lbx[:, 6:8], lbx[:, 12:14], ALU.mult))
                dve.wait_ge(bounds_out, 2)
                order.done(V.tensor_tensor(lbt[:, 1, 0, :], lbx[:, 4:6], lbx[:, 14:16], ALU.subtract))
                order.done(V.tensor_tensor(lbt[:, 1, 1, :], lbx[:, 2:4], lbx[:, 14:16], ALU.subtract))

            @st.block.scalar
            def _(act):
                for r in range(2):
                    act.wait_ge(reduced, r + 1)
                    for j in range(2):
                        A.activation(rope[:, 2 * r + j, :], rope[:, 2 * r + j, :], ACT.Sin).then_inc(table_ready, 1)
                act.wait_ge(bounds_in, 1)
                A.activation(lbx[:, 6:10], lbx[:, 2:6], ACT.Exp).then_inc(bounds_out, 1)
                act.wait_ge(bounds_in, 2)
                A.activation(lbx[:, 14:16], lbx[:, 14:16], ACT.Ln).then_inc(bounds_out, 1)

    def load_parameters(l, name, width):
        with Stage() as st:
            @st.block.sync
            def _(sp):
                sp.dma_start(par[:, 0:width], t[name][l, :, :]).then_inc(st.sem("landed"), 16)
                sp.wait_ge(st.sem("landed"), 16)

    m1 = Space()
    y = m1.get(DT, S)
    cq, ckv, kr = m1.get(3, S), m1.get(2, S), m1.get(S)
    mx = m1.get(2, S + 4)
    mo = m1.get(2, S)
    gi, gf = m1.get(S), m1.get(S)
    vz = m1.get(ST, S)
    uq, ukv = m1.get(3, 768), m1.get(2, 1024)
    M1_END = m1.at

    def mixer1_project(l):
        sp_ = Space(M1_END)
        w = sp_.get(10, DT, P)
        wg = sp_.get(DT, 2, 36)
        wr_at = sp_.at
        wr = sp_.get(DT, S)
        dst = [cq[:, 0, :], cq[:, 1, :], cq[:, 2, :], ckv[:, 0, :], ckv[:, 1, :], mx[:, 0, 2:2 + S], mx[:, 1, 2:2 + S],
               mo[:, 0, :], mo[:, 1, :], kr]
        with Stage() as st:
            norm = Norm(st, "norm", [h[:, k, :] for k in range(DT)], [n[:, k, :] for k in range(DT)],
                        [col(c1, "mix_norm", k) for k in range(DT)], D, sp_, ps[6][:, :])
            landed = [st.sem(f"w_landed{j}") for j in range(12)]
            next_landed = st.sem("next_landed")
            done, copied = st.sem("done"), st.sem("copied")

            @st.block.sync
            def _(sp):
                for j in range(10):
                    sp.dma_start(w[:, j, :, :].rearrange("p k m -> p (k m)"), t["in1_t"][l, j, :, :]).then_inc(landed[j], 16)
                sp.dma_start(wg.rearrange("p k a m -> p (k a m)"), t["in1_g"][l, :, :]).then_inc(landed[10], 16)
                sp.dma_start(wr.rearrange("p k m -> p (k m)"), t["in1_r"][l, :, :]).then_inc(landed[11], 16)
                sp.dma_start(uq.rearrange("p k m -> p (k m)"), t["uq"][l, :, :]).then_inc(next_landed, 16)
                sp.dma_start(ukv.rearrange("p k m -> p (k m)"), t["ukv"][l, :, :]).then_inc(next_landed, 16)
                sp.wait_ge(next_landed, 32)

            @st.block.gpsimd
            def _(pool):
                G.memset(mx[:, :, 0:2], 0.0)
                G.memset(mx[:, :, S + 2:S + 4], 0.0)

            @st.block.tensor
            def _(pe):
                norm.pe(pe)
                pe.wait_ge(norm.ready, DT)
                for j in range(16):
                    if j < 12:
                        pe.wait_ge(landed[min(j, 10)], 16)
                    elif j == 12:
                        pe.wait_ge(landed[11], 16)
                    if j >= 4:
                        pe.wait_ge(copied, j - 3)
                    bank = ps[j % 4]
                    if j < 10:
                        mm = products(bank[:, :], lambda k: w[:, j, k, :], lambda k: n[:, k, :], DT)
                    elif j < 12:
                        mm = products(bank[0:36, :], lambda k: wg[:, k, j - 10, :], lambda k: n[:, k, :], DT)
                    else:
                        mm = products(bank[:, :], lambda k: n[:, k, (j - 12) * P:(j - 11) * P], lambda k: wr[:, k, :], DT)
                    mm.then_inc(done, 1)

            @st.block.scalar
            def _(act):
                norm.act(act)
                for j in range(16):
                    act.wait_ge(done, j + 1)
                    bank = ps[j % 4]
                    if j < 10:
                        A.activation(dst[j], bank[:, :], ACT.Copy).then_inc(copied, 1)
                    elif j < 12:
                        rows_, bias = (gi, "i_bias") if j == 10 else (gf, "f_bias")
                        A.activation(rows_[0:32, :], bank[0:32, :], ACT.Identity, bias=col(c1, bias)[0:32, :])
                        A.activation(rows_[32:36, :], bank[32:36, ::-1], ACT.Identity, bias=col(c1, bias)[32:36, :]) \
                         .then_inc(copied, 1)
                    else:
                        A.activation(vz[:, j - 12, :], bank[:, :], ACT.Copy).then_inc(copied, 1)

            @st.block.vector
            def _(dve):
                norm.dve(dve)

    def rotate(dve, order, x, turned, cos_sin, tmp):
        V.tensor_tensor(x, x, rope[:, cos_sin, :], ALU.mult)
        order.done(V.tensor_tensor(tmp, turned, rope[:, cos_sin + 1, :], ALU.mult))
        return V.tensor_tensor(x, x, tmp, ALU.add)

    def mixer1_attention(l):
        sp_ = Space(M1_END)
        cqn, ckvn = n[:, 0:3, :], n[:, 3:5, :]
        qn, qr, kn, vn = sp_.get(H, S), sp_.get(2, S), sp_.get(H, S), sp_.get(ST, S)
        tmp = sp_.get(S)
        prob = sp_.get(2, S)
        pT = sp_.get(2, ST, S)
        top, nmax, total, inv = sp_.get(16), sp_.get(16), sp_.get(16), sp_.get(16)
        N = H * ST
        turned_src = [qr[:, 0, :], qr[:, 1, :], kr]
        with Stage() as st:
            nq = Norm(st, "nq", [cq[:, k, :] for k in range(3)], [cqn[:, k, :] for k in range(3)],
                      [col(c1, "q_norm", k) for k in range(3)], 384, sp_, ps[6][:, :])
            nk = Norm(st, "nk", [ckv[:, k, :] for k in range(2)], [ckvn[:, k, :] for k in range(2)],
                      [col(c1, "kv_norm", k) for k in range(2)], 256, sp_, ps[7][:, :])
            done, copied = st.sem("done"), st.sem("copied")
            turned, rotated = st.sem("turned"), st.sem("rotated")
            scores_ready, negmax_ready, exp_ready = st.sem("scores_ready"), st.sem("negmax_ready"), st.sem("exp_ready")
            probs_ready, pT_ready, pT_copied = st.sem("probs_ready"), st.sem("pT_ready"), st.sem("pT_copied")
            y_ready, y_copied = st.sem("y_ready"), st.sem("y_copied")

            @st.block.tensor
            def _(pe):
                nq.pe(pe)
                nk.pe(pe)
                pe.wait_ge(nq.ready, 3)
                for j in range(14):
                    if j == 6:
                        pe.wait_ge(nk.ready, 2)
                    if j >= 4:
                        pe.wait_ge(copied, j - 3)
                    bank = ps[j % 4][:, :]
                    if j < 6:
                        mm = products(bank, lambda k: uq[:, k, j * P:(j + 1) * P], lambda k: cqn[:, k, :], 3)
                    elif j < 10:
                        mm = products(bank, lambda k: ukv[:, k, (j - 6) * P:(j - 5) * P], lambda k: ckvn[:, k, :], 2)
                    else:
                        mm = products(bank, lambda k: ckvn[:, k, (j - 10) * P:(j - 9) * P], lambda k: ukv[:, k, 512:1024], 2)
                    mm.then_inc(done, 1)
                pe.wait_ge(copied, 14)
                for r in range(3):
                    T.matmul(ps[4 + r][:, :], C("rot_mla"), turned_src[r], start=True, stop=True).then_inc(turned, 1)
                pe.wait_ge(rotated, 3)
                for m in range(N + 1):
                    if m < N:
                        hd, i = divmod(m, ST)
                        q = slice(i * P, (i + 1) * P)
                        b = 64 * (hd % 2)
                        if m >= 2:
                            pe.wait_ge(exp_ready, m - 1)
                        T.matmul(ps[m % 2][:, :], qn[:, hd, q], kn[:, hd, :], start=True, stop=False)
                        T.matmul(ps[m % 2][:, :], qr[b:b + 64, hd // 2, q], kr[b:b + 64, :], start=False, stop=True) \
                         .then_inc(scores_ready, 1)
                    if m >= 1:
                        g = m - 1
                        hd, i = divmod(g, ST)
                        pe.wait_ge(probs_ready, g + 1)
                        if g >= 2:
                            pe.wait_ge(pT_copied, g - 1)
                        for k in range(ST):
                            mm = T.transpose(ps[2 + g % 2][:, k * P:(k + 1) * P], prob[:, g % 2, k * P:(k + 1) * P],
                                             C("ident"))
                        mm.then_inc(pT_ready, 1)
                        if i == ST - 1:
                            pe.wait_ge(pT_copied, g + 1)
                            if hd >= 2:
                                pe.wait_ge(y_copied, hd - 1)
                            products(ps[4 + hd % 2][:, :], lambda k: vn[:, k, hd * P:(hd + 1) * P],
                                     lambda k: pT[:, hd % 2, k, :], ST).then_inc(y_ready, 1)

            @st.block.scalar
            def _(act):
                nq.act(act)
                nk.act(act)
                for j in range(14):
                    act.wait_ge(done, j + 1)
                    dst = (qn[:, j, :] if j < 4 else qr[:, j - 4, :] if j < 6 else kn[:, j - 6, :] if j < 10
                           else vn[:, j - 10, :])
                    A.activation(dst, ps[j % 4][:, :], ACT.Copy).then_inc(copied, 1)
                for m in range(N):
                    act.wait_ge(negmax_ready, m + 1)
                    if m >= 2:
                        act.wait_ge(pT_ready, m - 1)
                    A.activation(prob[:, m % 2, :], ps[m % 2][:, :], ACT.Exp, scale=MLA_SCALE,
                                 bias=nmax[:, m:m + 1], accum_out=total[:, m:m + 1]).then_inc(exp_ready, 1)
                    if m % ST == 1 and m >= ST:
                        hd = m // ST - 1
                        act.wait_ge(y_ready, hd + 1)
                        A.activation(y[:, hd, :], ps[4 + hd % 2][:, :], ACT.Copy).then_inc(y_copied, 1)
                act.wait_ge(y_ready, H)
                A.activation(y[:, H - 1, :], ps[4 + (H - 1) % 2][:, :], ACT.Copy).then_inc(y_copied, 1)

            @st.block.vector
            def _(dve):
                order = Order(dve, st.sem("dve_order"))
                nq.dve(dve)
                nk.dve(dve)
                for r in range(3):
                    dve.wait_ge(turned, r + 1)
                    rotate(dve, order, turned_src[r], ps[4 + r][:, :], 0, tmp).then_inc(rotated, 1)
                    dve.wait_ge(rotated, r + 1)
                for m in range(N + 2):
                    if m >= 2:
                        hd, i = divmod(m - 2, ST)
                        dve.wait_ge(pT_ready, m - 1)
                        if i == 0 and hd >= 2:
                            dve.wait_ge(y_ready, hd - 1)
                        V.tensor_copy(pT[:, hd % 2, :, i * P:(i + 1) * P],
                                      ps[2 + m % 2][:, :].rearrange("p (k q) -> p k q", k=ST)).then_inc(pT_copied, 1)
                    if m < N:
                        dve.wait_ge(scores_ready, m + 1)
                        order.done(V.reduce_max(top[:, m:m + 1], ps[m % 2][:, :], AX.X))
                        V.tensor_scalar(nmax[:, m:m + 1], top[:, m:m + 1], -MLA_SCALE, None, ALU.mult) \
                         .then_inc(negmax_ready, 1)
                    if 1 <= m <= N:
                        g = m - 1
                        dve.wait_ge(exp_ready, g + 1)
                        order.done(V.reciprocal(inv[:, g:g + 1], total[:, g:g + 1]))
                        V.tensor_scalar(prob[:, g % 2, :], prob[:, g % 2, :], inv[:, g:g + 1], None, ALU.mult) \
                         .then_inc(probs_ready, 1)

    def mixer1_fourier(l):
        sp_ = Space(M1_END)
        dft = sp_.get(2, ST, S)
        part = sp_.get(2, 2, S)
        spec = sp_.get(2, S)
        fw = sp_.get(2, P)
        with Stage() as st:
            landed, w_landed = st.sem("landed"), st.sem("w_landed")
            done, copied = st.sem("done"), st.sem("copied")

            @st.block.sync
            def _(sp):
                sp.dma_start(dft.rearrange("p a j s -> p (a j s)"), t["dft"]).then_inc(landed, 16)
                sp.dma_start(fw.rearrange("p a m -> p (a m)"), t["fnw"][l, :, :]).then_inc(w_landed, 16)

            @st.block.tensor
            def _(pe):
                pe.wait_ge(landed, 16)
                for j in range(4):
                    c, a = divmod(j, 2)
                    products(ps[j][:, :], lambda k: vz[:, k, 256 + c * P:256 + (c + 1) * P], lambda k: dft[:, a, k, :], ST) \
                        .then_inc(done, 1)
                for c in range(2):
                    pe.wait_ge(copied, 2 * c + 2)
                    products(ps[4 + c][:, :], lambda k: C("dft_s") if k else C("dft_c"), lambda k: part[:, c, k, :], 2) \
                        .then_inc(done, 1)
                pe.wait_ge(w_landed, 16)
                for c in range(2):
                    pe.wait_ge(copied, 5 + c)
                    T.matmul(ps[6 + c][:, :], fw[:, c, :], spec[:, c, :], start=True, stop=True).then_inc(done, 1)

            @st.block.scalar
            def _(act):
                for j in range(8):
                    act.wait_ge(done, j + 1)
                    if j < 4:
                        A.activation(part[:, j // 2, j % 2, :], ps[j][:, :], ACT.Copy).then_inc(copied, 1)
                    elif j < 6:
                        A.activation(spec[:, j - 4, :], ps[j][:, :], ACT.Copy).then_inc(copied, 1)
                    else:
                        A.activation(y[:, j, :], ps[j][:, :], ACT.Identity, bias=col(c1, "fnet_b", j - 6)).then_inc(copied, 1)

    def project_out(l, w_dram, gate=None):
        sp_ = Space(DT * S)
        w = sp_.get(DT, DT, P)
        with Stage() as st:
            landed = [st.sem(f"w_landed{j}") for j in range(DT)]
            done, added = st.sem("done"), st.sem("added")

            @st.block.sync
            def _(sp):
                for j in range(DT):
                    sp.dma_start(w[:, j, :, :].rearrange("p k m -> p (k m)"), w_dram[l, j, :, :]).then_inc(landed[j], 16)

            @st.block.tensor
            def _(pe):
                for j in range(DT):
                    pe.wait_ge(landed[j], 16)
                    if j >= 4:
                        pe.wait_ge(added, j - 3)
                    products(ps[j % 4][:, :], lambda k: w[:, j, k, :], lambda k: y[:, k, :], DT).then_inc(done, 1)

            @st.block.vector
            def _(dve):
                for j in range(DT):
                    dve.wait_ge(done, j + 1)
                    V.scalar_tensor_tensor(out=h[:, j, :], in0=ps[j % 4][:, :], scalar=1.0 if gate is None else gate[j],
                                           in1=h[:, j, :], op0=ALU.mult, op1=ALU.add).then_inc(added, 1)

    def embed_layer(l):
        sp_ = Space()
        e = sp_.get(DT, S)
        pt = sp_.get(2, S)
        wp = sp_.get(2, D)
        w = sp_.get(DT, DT, P)
        sig = sp_.get(2, S)
        with Stage() as st:
            landed = [st.sem(f"w_landed{j}") for j in range(DT)]
            p_landed = st.sem("p_landed")
            e_done, e_copied, done, sig_ready = st.sem("e_done"), st.sem("e_copied"), st.sem("done"), st.sem("sig_ready")
            gated, added = st.sem("gated"), st.sem("added")
            ng_ = Norm(st, "norm", [h[:, k, :] for k in range(DT)], [n[:, k, :] for k in range(DT)],
                       [col(c1, "gate_norm", k) for k in range(DT)], D, sp_, ps[6][:, :])
            ne = Norm(st, "ne", [e[:, k, :] for k in range(DT)], [e[:, k, :] for k in range(DT)],
                      [col(c1, "post_norm", k) for k in range(DT)], D, sp_, ps[7][:, :])

            @st.block.sync
            def _(sp):
                sp.dma_start(pt, t["p"][l, :, :].rearrange("(k p) s -> p k s", p=P)).then_inc(p_landed, 16)
                sp.dma_start(wp.rearrange("p k m -> p (k m)"), t["plep"][l, :, :]).then_inc(p_landed, 16)
                for j in range(DT):
                    sp.dma_start(w[:, j, :, :].rearrange("p k m -> p (k m)"), t["pleg"][l, j, :, :]).then_inc(landed[j], 16)

            @st.block.tensor
            def _(pe):
                pe.wait_ge(p_landed, 32)
                for j in range(DT):
                    if j >= 4:
                        pe.wait_ge(e_copied, j - 3)
                    products(ps[j % 4][:, :], lambda k: wp[:, k, j * P:(j + 1) * P], lambda k: pt[:, k, :], 2).then_inc(e_done, 1)
                pe.wait_ge(e_copied, DT)
                ng_.pe(pe)
                ne.pe(pe)
                pe.wait_ge(ng_.ready, DT)
                for j in range(DT):
                    pe.wait_ge(landed[j], 16)
                    if j >= 4:
                        pe.wait_ge(sig_ready, j - 3)
                    products(ps[j % 4][:, :], lambda k: w[:, j, k, :], lambda k: n[:, k, :], DT).then_inc(done, 1)

            @st.block.scalar
            def _(act):
                for j in range(DT):
                    act.wait_ge(e_done, j + 1)
                    A.activation(e[:, j, :], ps[j % 4][:, :], ACT.Copy).then_inc(e_copied, 1)
                ng_.act(act)
                act.wait_ge(e_copied, DT)
                ne.act(act)
                for j in range(DT):
                    act.wait_ge(done, j + 1)
                    if j >= 2:
                        act.wait_ge(gated, j - 1)
                    A.activation(sig[:, j % 2, :], ps[j % 4][:, :], ACT.Sigmoid).then_inc(sig_ready, 1)

            @st.block.vector
            def _(dve):
                ng_.dve(dve)
                ne.dve(dve)
                dve.wait_ge(ne.ready, DT)
                for j in range(DT):
                    dve.wait_ge(sig_ready, j + 1)
                    V.tensor_tensor(e[:, j, :], e[:, j, :], sig[:, j % 2, :], ALU.mult).then_inc(gated, 1)
                    dve.wait_ge(gated, j + 1)
                    V.tensor_tensor(h[:, j, :], h[:, j, :], e[:, j, :], ALU.add).then_inc(added, 1)

    def final_norm():
        sp_ = Space()
        with Stage() as st:
            norm = Norm(st, "norm", [h[:, k, :] for k in range(DT)], [h[:, k, :] for k in range(DT)],
                        [col(cg, "final_norm", k) for k in range(DT)], D, sp_, ps[6][:, :])
            st.block.tensor(norm.pe)
            st.block.scalar(norm.act)
            st.block.vector(norm.dve)

    def mixer1_mlstm(l):
        sp_ = Space(M1_END)
        conv = sp_.get(2, S)
        xc = sp_.get(2, S)
        qk = sp_.get(2, 2, S)
        ws = sp_.get(2, 2, P)
        absf, soft, lf, F, a, M = [sp_.get(S) for _ in range(6)]
        rows_a, rows_m, rows_t = sp_.get(S), sp_.get(S), sp_.get(S)
        acol = sp_.get(ST, 36)
        finish = Space(sp_.at)
        qks = sp_.get(2, ST, S)
        wgt = sp_.get(4, S)
        thr = sp_.get(S)
        den, hdir = sp_.get(S), sp_.get(S)
        hsum = sp_.get(2, S)
        outn, sig = n[:, 0:2, :], n[:, 2:4, :]
        groups = [(p, d, e) for p in range(2) for d in range(2) for e in range(2)]
        steps = [(g, j) for g in range(8) for j in (range(ST) if groups[g][1] == 0 else range(ST - 1, -1, -1))]

        def head(a_, p, e, cols):
            return qk[64 * e:64 * e + 64, a_, p, cols]

        def span(g, j):
            return slice(j * P, S) if groups[g][1] == 0 else slice(0, (j + 1) * P)

        with Stage() as st:
            landed = st.sem("landed")
            conv_ready, xc_ready = st.sem("conv_ready"), st.sem("xc_ready")
            gate_in, gate_out = st.sem("gate_in"), st.sem("gate_out")
            rows_ready, cols_done, cols_ready = st.sem("rows_ready"), st.sem("cols_done"), st.sem("cols_ready")
            maps_done, maps_copied = st.sem("maps_done"), st.sem("maps_copied")
            qk_done, qk_copied = st.sem("qk_done"), st.sem("qk_copied")
            m_spread, arg_ready, exp_ready, wgt_ready = (st.sem("m_spread"), st.sem("arg_ready"), st.sem("exp_ready"),
                                                         st.sem("wgt_ready"))
            used, t_spread, thr_ready, dir_ready = st.sem("used"), st.sem("t_spread"), st.sem("thr_ready"), st.sem("dir_ready")
            zeroed = st.sem("zeroed")

            @st.block.sync
            def _(sp):
                sp.dma_start(ws.rearrange("p a b m -> p (a b m)"), t["mqk"][l, :, :]).then_inc(landed, 16)

            @st.block.tensor
            def _(pe):
                pe.wait_ge(landed, 16)
                for j in range(4):
                    a_, p = divmod(j, 2)
                    pe.wait_ge(xc_ready, p + 1)
                    T.matmul(ps[j][:, :], ws[:, a_, p, :], xc[:, p, :], start=True, stop=True).then_inc(maps_done, 1)
                pe.wait_ge(rows_ready, 1)
                for j in range(ST):
                    mm = T.transpose(ps[7][:, 36 * j:36 * j + 36], rows_a[0:36, j * P:(j + 1) * P], C("ident")[0:36, 0:36])
                mm.then_inc(cols_done, 1)
                pe.wait_ge(maps_copied, 4)
                pe.wait_ge(rows_ready, 3)
                for s_, (g, j) in enumerate(steps):
                    p, d, e = groups[g]
                    b = 64 * e
                    first = s_ % ST == 0
                    if first and d == 0 and e == 0:
                        for m in range(8):
                            hh, jj = divmod(m, ST)
                            mj = 8 * p + m
                            if p and m == 0:
                                pe.wait_ge(wgt_ready, 16)
                            if mj >= 2:
                                pe.wait_ge(qk_copied, mj - 1)
                            T.matmul(ps[m % 2][:, :], head(1, p, hh, slice(jj * P, (jj + 1) * P)), head(0, p, hh, slice(0, S)),
                                     start=True, stop=True).then_inc(qk_done, 1)
                    if first:
                        for g_ in ([0, 1] if g == 0 else [g + 1] if g < 7 else []):
                            p_, d_, e_ = groups[g_]
                            if g_ >= 2:
                                pe.wait_ge(arg_ready, ST * (g_ - 1))
                            c_ = 4 * d_ + 2 * p_ + e_
                            T.matmul(ps[2 + g_ % 2][:, :], C("sel", 36, c_ * P, (c_ + 1) * P), rows_m[0:36, :],
                                     start=True, stop=True).then_inc(m_spread, 1)
                        if e == 0:
                            if g == 0:
                                pe.wait_ge(cols_ready, 1)
                            else:
                                pe.wait_ge(dir_ready, g // 2)
                            T.matmul(ps[7][:, :], C("selp", 36, (2 * d + p) * P, (2 * d + p + 1) * P), rows_t[0:36, :],
                                     start=True, stop=True).then_inc(t_spread, 1)
                    pe.wait_ge(wgt_ready, s_ + 1)
                    r = span(g, j)
                    hd = 2 * p + e
                    T.matmul(ps[5][b:b + 64, r], vz[:, j, hd * HD:(hd + 1) * HD], wgt[:, s_ % 4, r], start=first,
                             stop=(s_ % ST == ST - 1))
                    T.matmul(ps[6][b:b + 64, r], C("ones")[:, 0:HD], wgt[:, s_ % 4, r], start=first,
                             stop=(s_ % ST == ST - 1)).then_inc(used, 1)

            @st.block.scalar
            def _(act):
                for c in range(2):
                    act.wait_ge(conv_ready, c + 1)
                    A.activation(xc[:, c, :], conv[:, c, :], ACT.Silu, bias=col(c1, "conv_b", c)).then_inc(xc_ready, 1)
                act.wait_ge(gate_in, 1)
                A.activation(soft[0:36, :], absf[0:36, :], ACT.Exp, scale=-1.0).then_inc(gate_out, 1)
                act.wait_ge(gate_out, 1)
                A.activation(soft[0:36, :], soft[0:36, :], ACT.Ln, bias=C("one", 36)).then_inc(gate_out, 1)
                for j in range(4):
                    act.wait_ge(maps_done, j + 1)
                    A.activation(qk[:, j // 2, j % 2, :], ps[j][:, :], ACT.Copy, scale=HD ** -0.5 if j < 2 else 1.0) \
                     .then_inc(maps_copied, 1)
                act.wait_ge(gate_in, 2)
                A.activation(M[0:36, :], M[0:36, :], ACT.Exp, scale=-1.0).then_inc(gate_out, 1)
                act.wait_ge(cols_done, 1)
                A.activation(acol.rearrange("p j c -> p (j c)"), ps[7][:, 0:144], ACT.Copy).then_inc(cols_ready, 1)
                for s_, (g, j) in enumerate(steps):
                    p, d, e = groups[g]
                    first = s_ % ST == 0
                    if first and d == 0 and e == 0:
                        for m in range(8):
                            act.wait_ge(qk_done, 8 * p + m + 1)
                            A.activation(qks[:, m // ST, m % ST, :], ps[m % 2][:, :], ACT.Copy).then_inc(qk_copied, 1)
                    if first and e == 0:
                        act.wait_ge(t_spread, g // 2 + 1)
                        if g:
                            act.wait_ge(dir_ready, g // 2)
                        A.activation(thr, ps[7][:, :], ACT.Copy).then_inc(thr_ready, 1)
                    act.wait_ge(arg_ready, s_ + 1)
                    A.activation(wgt[:, s_ % 4, span(g, j)], wgt[:, s_ % 4, span(g, j)], ACT.Exp).then_inc(exp_ready, 1)

            @st.block.vector
            def _(dve):
                order = Order(dve, st.sem("dve_order"))
                for c in range(2):
                    w_ = lambda k: col(c1, "conv_w", 5 * c + k)
                    order.done(V.tensor_scalar(conv[:, c, :], mx[:, c, 0:S], w_(0), None, ALU.mult))
                    for k in range(1, 5):
                        ins = V.scalar_tensor_tensor(out=conv[:, c, :], in0=mx[:, c, k:k + S], scalar=w_(k),
                                                     in1=conv[:, c, :], op0=ALU.mult, op1=ALU.add)
                        if k < 4:
                            order.done(ins)
                    ins.then_inc(conv_ready, 1)
                R = slice(0, 36)
                V.scalar_tensor_tensor(out=absf[R, :], in0=gf[R, :], scalar=-1.0, in1=gf[R, :], op0=ALU.mult, op1=ALU.max).then_inc(gate_in, 1)
                dve.wait_ge(gate_out, 2)
                order.done(V.scalar_tensor_tensor(out=lf[R, :], in0=gf[R, :], scalar=0.0, in1=soft[R, :], op0=ALU.min, op1=ALU.subtract))
                order.done(V.memset(absf[R, :], 1.0))
                order.done(V.tensor_tensor_scan(F[R, :], absf[R, :], lf[R, :], 0.0, ALU.mult, ALU.add))
                order.done(V.tensor_tensor(a[R, :], gi[R, :], F[R, :], ALU.subtract))
                order.done(V.tensor_tensor_scan(lf[R, :], absf[R, :], a[R, :], 0.0, ALU.mult, ALU.max))
                V.tensor_tensor(M[R, :], F[R, :], lf[R, :], ALU.add).then_inc(gate_in, 1)
                dve.wait_ge(gate_in, 2)
                order.done(V.tensor_scalar(F[R, :], lf[R, :], -1.0, None, ALU.mult))
                for m, (dst, src) in enumerate(((rows_a, a), (rows_m, F), (rows_t, M))):
                    if m == 2:
                        dve.wait_ge(gate_out, 3)
                    V.tensor_copy(dst[0:32, :], src[0:32, :]).then_inc(zeroed, 1)
                    dve.wait_ge(zeroed, m + 1)
                    V.tensor_copy(dst[32:36, :], src[32:36, ::-1]).then_inc(rows_ready, 1)
                dve.wait_ge(cols_ready, 1)
                for s_ in range(len(steps) + 1):
                    if s_ < len(steps):
                        g, j = steps[s_]
                        p, d, e = groups[g]
                        r = span(g, j)
                        if s_ % ST == 0:
                            dve.wait_ge(m_spread, g + 1)
                        if s_ >= 4:
                            dve.wait_ge(used, s_ - 3)
                        rc = 32 * d + 2 * p + e
                        V.tensor_scalar(wgt[:, s_ % 4, r], ps[2 + g % 2][:, r], acol[:, j, rc:rc + 1], 0.0, ALU.add, ALU.min) \
                         .then_inc(arg_ready, 1)
                    if s_ >= 1:
                        g, j = steps[s_ - 1]
                        p, d, e = groups[g]
                        r = span(g, j)
                        dve.wait_ge(exp_ready, s_)
                        if (s_ - 1) % 16 == 0:
                            dve.wait_ge(qk_copied, 8 * p + 8)
                        wx = wgt[:, (s_ - 1) % 4, :]
                        order.done(V.tensor_tensor(wx[:, r], wx[:, r], qks[:, e, j, r], ALU.mult))
                        dg = slice(j * P, (j + 1) * P)
                        V.tensor_tensor(wx[:, dg], wx[:, dg], C("upto") if d == 0 else C("from"), ALU.mult) \
                         .then_inc(wgt_ready, 1)
                        if s_ % (2 * ST) == 0:
                            gd = s_ // (2 * ST)
                            dve.wait_ge(used, s_)
                            dve.wait_ge(thr_ready, gd)
                            order.done(V.scalar_tensor_tensor(out=den, in0=ps[6][:, :], scalar=-1.0, in1=thr,
                                                              op0=ALU.mult, op1=ALU.max))
                            order.done(V.tensor_tensor(den, ps[6][:, :], den, ALU.max))
                            order.done(V.reciprocal(den, den))
                            if d == 0:
                                V.tensor_tensor(hsum[:, p, :], ps[5][:, :], den, ALU.mult).then_inc(dir_ready, 1)
                                dve.wait_ge(dir_ready, gd)
                            else:
                                order.done(V.tensor_tensor(hdir, ps[5][:, :], den, ALU.mult))
                                V.tensor_tensor(hsum[:, p, :], hsum[:, p, :], hdir, ALU.add).then_inc(dir_ready, 1)
                                dve.wait_ge(dir_ready, gd)

        with Stage() as st:
            norms = [Norm(st, f"nh{p}", [hsum[:, p, :]], [outn[:, p, :]], [col(c1, "head_norm", p)], HD, finish, ps[p][:, :],
                          lhs="heads") for p in range(2)]
            sig_ready, skipped = st.sem("sig_ready"), st.sem("skipped")

            @st.block.tensor
            def _(pe):
                for x in norms:
                    x.pe(pe)

            @st.block.scalar
            def _(act):
                for x in norms:
                    x.act(act)
                A.activation(sig.rearrange("p a s -> p (a s)"), mo.rearrange("p a s -> p (a s)"), ACT.Sigmoid).then_inc(sig_ready, 1)

            @st.block.vector
            def _(dve):
                for p, x in enumerate(norms):
                    x.dve(dve)
                for p, x in enumerate(norms):
                    dve.wait_ge(x.ready, 1)
                    V.scalar_tensor_tensor(out=outn[:, p, :], in0=xc[:, p, :], scalar=col(c1, "skip", p), in1=outn[:, p, :],
                                           op0=ALU.mult, op1=ALU.add).then_inc(skipped, 1)
                dve.wait_ge(sig_ready, 1)
                dve.wait_ge(skipped, 2)
                V.tensor_tensor(y[:, 4:6, :].rearrange("p a s -> p (a s)"), outn.rearrange("p a s -> p (a s)"),
                                sig.rearrange("p a s -> p (a s)"), ALU.mult)

    modc = mod[:, 0, :]
    gain_m, gain_f = mod[:, 1, 0:8], mod[:, 1, 8:16]
    lbc = mod[:, 1, 16:22]

    def adaptive(l):
        sp_ = Space()
        QN = 1536
        w = sp_.get(4, QN)
        acc = sp_.get(6 * D)
        cond = sp_.get(8)
        with Stage() as st:
            landed = [st.sem(f"w_landed{j}") for j in range(4)]
            cond_ready, used, summed = st.sem("cond_ready"), st.sem("used"), st.sem("summed")
            p_landed = st.sem("p_landed")

            @st.block.sync
            def _(sp):
                sp.dma_start(par[:, 0:n2], t["par2"][l, :, :]).then_inc(p_landed, 16)
                for k in range(DT):
                    for q in range(4):
                        if k:
                            sp.wait_ge(used, 4 * k + q - 3)
                        sp.dma_start(w[:, q, :], t["ada"][l, k, :, q * QN:(q + 1) * QN]).then_inc(landed[q], 16)

            @st.block.scalar
            def _(act):
                at = cg["cond"][0]
                A.activation(cond, parg[:, at:at + 8], ACT.Silu).then_inc(cond_ready, 1)

            @st.block.vector
            def _(dve):
                order = Order(dve, st.sem("dve_order"))
                order.done(V.tensor_copy(lbc, lbt[:, bass.ds(l, 1), :, :].rearrange("p a b c -> p (a b c)")))
                dve.wait_ge(cond_ready, 1)
                for k in range(DT):
                    for q in range(4):
                        dve.wait_ge(landed[q], 16 * (k + 1))
                        a = acc[:, q * QN:(q + 1) * QN]
                        if k == 0:
                            V.tensor_scalar(a, w[:, q, :], cond[:, k:k + 1], None, ALU.mult).then_inc(used, 1)
                        else:
                            dve.wait_ge(used, 4 * k + q - 3)
                            V.scalar_tensor_tensor(out=a, in0=w[:, q, :], scalar=cond[:, k:k + 1], in1=a,
                                                   op0=ALU.mult, op1=ALU.add).then_inc(used, 1)
                dve.wait_ge(summed, 1)
                dve.wait_ge(p_landed, 16)
                ab = c2["ada_b"][0]
                order.done(V.tensor_tensor(modc, ps[0][:, 0:48], par[:, ab:ab + 48], ALU.add))
                for dst, name, at in ((gain_m, "norm_mix", 8), (gain_f, "norm_ffn", 32)):
                    g0 = c2[name][0]
                    order.done(V.scalar_tensor_tensor(out=dst, in0=modc[:, at:at + 8], scalar=1.0, in1=par[:, g0:g0 + 8],
                                                      op0=ALU.add, op1=ALU.mult))

            @st.block.tensor
            def _(pe):
                pe.wait_ge(used, 4 * DT)
                for j in range(48):
                    mm = T.matmul(ps[0][:, j:j + 1], acc[:, j * P:(j + 1) * P], C("ones")[:, 0:1], start=True, stop=True)
                mm.then_inc(summed, 1)

    m2 = Space(DT * S)
    aq = m2.get(4, S)
    ak = m2.get(P + S)
    bq, bf, bg = m2.get(2, S), m2.get(2, S), m2.get(2, S)
    cx = m2.get(6, S + 3)
    cgt = m2.get(2, S)
    cb, ca = m2.get(S), m2.get(S)
    vn = m2.get(ST, 384)
    M2_END = m2.at

    def mixer2_project(l):
        sp_ = Space(M2_END)
        SLOTS = 10
        w = sp_.get(SLOTS, DT, P)
        wg = sp_.get(DT, 8)
        wr = sp_.get(DT, 384)
        dst = ([aq[:, k, :] for k in range(4)] + [ak[:, P:P + S]] + [bq[:, k, :] for k in range(2)]
               + [bf[:, k, :] for k in range(2)] + [bg[:, k, :] for k in range(2)]
               + [cx[:, k, 3:3 + S] for k in range(6)] + [cgt[:, k, :] for k in range(2)])
        NT = len(dst)
        with Stage() as st:
            norm = Norm(st, "norm", [h[:, k, :] for k in range(DT)], [n[:, k, :] for k in range(DT)],
                        [gain_m[:, k:k + 1] for k in range(DT)], D, sp_, ps[6][:, :],
                        shifts=[modc[:, k:k + 1] for k in range(DT)])
            landed = [st.sem(f"w_landed{j}") for j in range(SLOTS + 2)]
            done, copied = st.sem("done"), st.sem("copied")

            @st.block.sync
            def _(sp):
                for j in range(NT):
                    if j >= SLOTS:
                        sp.wait_ge(done, j - SLOTS + 1)
                    sp.dma_start(w[:, j % SLOTS, :, :].rearrange("p k m -> p (k m)"), t["in2_t"][l, j, :, :]) \
                      .then_inc(landed[j % SLOTS], 16)
                    if j == SLOTS - 1:
                        sp.dma_start(wg.rearrange("p k m -> p (k m)"), t["in2_g"][l, :, :]).then_inc(landed[SLOTS], 16)
                        sp.dma_start(wr.rearrange("p k m -> p (k m)"), t["in2_r"][l, :, :]).then_inc(landed[SLOTS + 1], 16)

            @st.block.gpsimd
            def _(pool):
                G.memset(ak[:, 0:P], 0.0)
                G.memset(cx[:, :, 0:3], 0.0)

            @st.block.tensor
            def _(pe):
                norm.pe(pe)
                pe.wait_ge(norm.ready, DT)
                for j in range(NT + 6):
                    if j >= 4:
                        pe.wait_ge(copied, j - 3)
                    bank = ps[j % 4]
                    if j < NT:
                        pe.wait_ge(landed[j % SLOTS], 16 * (j // SLOTS + 1))
                        mm = products(bank[:, :], lambda k: w[:, j % SLOTS, k, :], lambda k: n[:, k, :], DT)
                    elif j < NT + 2:
                        c = j - NT
                        pe.wait_ge(landed[SLOTS], 16)
                        mm = products(bank[0:4, :], lambda k: wg[:, k, 4 * c:4 * c + 4], lambda k: n[:, k, :], DT)
                    else:
                        c = j - NT - 2
                        pe.wait_ge(landed[SLOTS + 1], 16)
                        mm = products(bank[:, 0:384], lambda k: n[:, k, c * P:(c + 1) * P], lambda k: wr[:, k, :], DT)
                    mm.then_inc(done, 1)

            @st.block.scalar
            def _(act):
                norm.act(act)
                for j in range(NT + 6):
                    act.wait_ge(done, j + 1)
                    bank = ps[j % 4]
                    if j < NT:
                        A.activation(dst[j], bank[:, :], ACT.Copy).then_inc(copied, 1)
                    elif j < NT + 2:
                        A.activation((cb if j == NT else ca)[0:4, :], bank[0:4, :], ACT.Copy).then_inc(copied, 1)
                    else:
                        A.activation(vn[:, j - NT - 2, :], bank[:, 0:384], ACT.Copy).then_inc(copied, 1)

            @st.block.vector
            def _(dve):
                norm.dve(dve)

    def mixer2_window(l):
        sp_ = Space(M2_END)
        tmp = sp_.get(S)
        sc = sp_.get(2, ST, 2 * P)
        pT = sp_.get(2, ST, 2, P)
        top, nmax, total, esink, inv = [sp_.get(8, ST) for _ in range(5)]
        heads = [(j, f) for j in range(4) for f in range(2)]
        x = [aq[:, j, :] for j in range(4)] + [ak[:, P:P + S]]
        with Stage() as st:
            norms = [Norm(st, f"n{r}", [x[r]], [x[r]], [col(c2, "q_norm" if r < 4 else "k_norm")], HD, sp_, ps[r][:, :],
                          lhs="heads") for r in range(5)]
            turned, rotated = st.sem("turned"), st.sem("rotated")
            scores_ready, negmax_ready, exp_ready = st.sem("scores_ready"), st.sem("negmax_ready"), st.sem("exp_ready")
            masked, probs_ready = st.sem("masked"), st.sem("probs_ready")
            pT_ready, pT_copied, y_ready, y_copied = (st.sem("pT_ready"), st.sem("pT_copied"), st.sem("y_ready"),
                                                      st.sem("y_copied"))

            @st.block.tensor
            def _(pe):
                for r in range(5):
                    norms[r].pe(pe)
                for r in range(5):
                    pe.wait_ge(norms[r].ready, 1)
                    if r >= 3:
                        pe.wait_ge(rotated, r - 2)
                    T.matmul(ps[5 + r % 3][:, :], C("rot_win"), x[r], start=True, stop=True).then_inc(turned, 1)
                pe.wait_ge(rotated, 5)
                for m in range(10):
                    if m < 8:
                        j, f = heads[m]
                        b = 64 * f
                        if m >= 2:
                            pe.wait_ge(masked, 2 * m - 2)
                        for q in range(ST):
                            mm = T.matmul(ps[2 * (m % 2) + q // 2][:, (q % 2) * 256:(q % 2) * 256 + 256],
                                          aq[b:b + 64, j, q * P:(q + 1) * P], ak[b:b + 64, q * P:(q + 2) * P],
                                          start=True, stop=True)
                        mm.then_inc(scores_ready, 1)
                    if 1 <= m <= 8:
                        g = m - 1
                        pe.wait_ge(probs_ready, ST * m)
                        if g:
                            pe.wait_ge(pT_copied, 2 * g)
                        for q in range(ST):
                            for a in range(2):
                                mm = T.transpose(ps[4 + q // 2][:, (q % 2) * 256 + a * P:(q % 2) * 256 + (a + 1) * P],
                                                 sc[:, g % 2, q, a * P:(a + 1) * P], C("ident"))
                        mm.then_inc(pT_ready, 1)
                    if m >= 2:
                        g = m - 2
                        j, f = heads[g]
                        b = 64 * f
                        pe.wait_ge(pT_copied, 2 * g + 2)
                        if g >= 2:
                            pe.wait_ge(y_copied, g - 1)
                        for q in range(ST):
                            for a in range(0 if q else 1, 2):
                                mm = T.matmul(ps[6 + g % 2][b:b + 64, q * P:(q + 1) * P],
                                              vn[:, q - 1 + a, f * HD:(f + 1) * HD], pT[:, g % 2, q, a, :],
                                              start=(a == 0 or q == 0), stop=(a == 1))
                        mm.then_inc(y_ready, 1)

            @st.block.scalar
            def _(act):
                for r in range(5):
                    norms[r].act(act)
                sk = c2["sinks"][0]
                for m in range(10):
                    if m < 8:
                        act.wait_ge(negmax_ready, m + 1)
                        for q in range(ST):
                            A.activation(sc[:, m % 2, q, :], sc[:, m % 2, q, :], ACT.Exp, bias=nmax[:, m, q:q + 1],
                                         accum_out=total[:, m, q:q + 1])
                        A.activation(esink[:, m, :], nmax[:, m, :], ACT.Exp, bias=par[:, sk + m:sk + m + 1]) \
                         .then_inc(exp_ready, 1)
                    if 1 <= m <= 8:
                        g = m - 1
                        act.wait_ge(pT_ready, m)
                        if g >= 2:
                            act.wait_ge(y_ready, g - 1)
                        for a in range(2):
                            A.activation(pT[:, g % 2, 2 * a:2 * a + 2, :, :].rearrange("p q a k -> p (q a k)"),
                                         ps[4 + a][:, :], ACT.Copy).then_inc(pT_copied, 1)
                    if m >= 2:
                        g = m - 2
                        j, f = heads[g]
                        act.wait_ge(y_ready, g + 1)
                        A.activation(y[64 * f:64 * f + 64, j, :], ps[6 + g % 2][64 * f:64 * f + 64, :], ACT.Copy) \
                         .then_inc(y_copied, 1)

            @st.block.vector
            def _(dve):
                order = Order(dve, st.sem("dve_order"))
                for r in range(5):
                    norms[r].dve(dve)
                for r in range(5):
                    dve.wait_ge(turned, r + 1)
                    rotate(dve, order, x[r], ps[5 + r % 3][:, :], 2, tmp).then_inc(rotated, 1)
                    dve.wait_ge(rotated, r + 1)
                sk = c2["sinks"][0]
                for m in range(9):
                    if m < 8:
                        dve.wait_ge(scores_ready, m + 1)
                        if m >= 2:
                            dve.wait_ge(pT_ready, m - 1)
                        for a in range(2):
                            V.scalar_tensor_tensor(out=sc[:, m % 2, 2 * a:2 * a + 2, :].rearrange("p q k -> p (q k)"),
                                                   in0=ps[2 * (m % 2) + a][:, :], scalar=HD ** -0.5,
                                                   in1=C("window", None, 256 * a, 256 * a + 512),
                                                   op0=ALU.mult, op1=ALU.add).then_inc(masked, 1)
                        dve.wait_ge(masked, 2 * m + 2)
                        order.done(V.reduce_max(top[:, m, :], sc[:, m % 2, :, :], AX.X))
                        V.tensor_scalar(nmax[:, m, :], top[:, m, :], par[:, sk + m:sk + m + 1], -1.0, ALU.max, ALU.mult) \
                         .then_inc(negmax_ready, 1)
                    if m >= 1:
                        g = m - 1
                        dve.wait_ge(exp_ready, m)
                        order.done(V.tensor_tensor(inv[:, g, :], total[:, g, :], esink[:, g, :], ALU.add))
                        order.done(V.reciprocal(inv[:, g, :], inv[:, g, :]))
                        for q in range(ST):
                            V.tensor_scalar(sc[:, g % 2, q, :], sc[:, g % 2, q, :], inv[:, g, q:q + 1], None, ALU.mult) \
                             .then_inc(probs_ready, 1)

    def head_output(st, sp_, tag, src, gain, gate, y_at, tmp):
        norms = [Norm(st, f"{tag}{c}", [src[:, c, :]], [src[:, c, :]], [gain], HD, sp_, ps[c][:, :], lhs="heads")
                 for c in range(2)]
        gate_ready = st.sem(tag + "_gate")

        def pe_(pe):
            for x in norms:
                x.pe(pe)

        def act_(act):
            for x in norms:
                x.act(act)
            A.activation(tmp, gate, ACT.Silu).then_inc(gate_ready, 1)

        def dve_(dve):
            for x in norms:
                x.dve(dve)
            dve.wait_ge(gate_ready, 1)
            for c, x in enumerate(norms):
                dve.wait_ge(x.ready, 1)
                V.tensor_tensor(y[:, y_at + c, :], src[:, c, :], tmp[:, c, :], ALU.mult)

        return pe_, act_, dve_

    def mixer2_hgrn(l):
        sp_ = Space(M2_END)
        az, sp2, B, mxv, lf, kk = [sp_.get(2, S) for _ in range(6)]
        cum = sp_.get(2, S)
        E = sp_.get(2, S)
        X = sp_.get(2, S)
        diag = sp_.get(H, ST, P)
        off = sp_.get(H, 6 * P)
        et = sp_.get(2, ST)
        qd, kd, far = sp_.get(2, S), sp_.get(2, S), sp_.get(2, 2, P)
        o = sp_.get(2, S)
        flat = lambda a: a.rearrange("p c s -> p (c s)")
        NL = len(LEVELS)
        steps = [(v, c) for v in range(NL) for c in range(2)]

        def halves(a, c, L):
            v = a[:, c, :].rearrange("p (b a k) -> p b a k", a=2, k=L)
            return v[:, :, 0, :], v[:, :, 1, :]

        with Stage() as st:
            f_in, f_out = st.sem("f_in"), st.sem("f_out")
            diff_ready, decay_ready, x_ready = st.sem("diff_ready"), st.sem("decay_ready"), st.sem("x_ready")
            own_done, own_copied = st.sem("own_done"), st.sem("own_copied")
            lev_done, lev_copied = st.sem("lev_done"), st.sem("lev_copied")
            tail_in, tail_exp, tail_ready = st.sem("tail_in"), st.sem("tail_exp"), st.sem("tail_ready")
            off_done, off_copied, o_done = st.sem("off_done"), st.sem("off_copied"), st.sem("o_done")

            @st.block.scalar
            def _(act):
                act.wait_ge(f_in, 1)
                A.activation(flat(sp2), flat(az), ACT.Exp, scale=-1.0).then_inc(f_out, 1)
                act.wait_ge(f_out, 1)
                A.activation(flat(sp2), flat(sp2), ACT.Ln, bias=C("one")).then_inc(f_out, 1)
                act.wait_ge(f_in, 2)
                A.activation(flat(az), flat(az), ACT.Exp).then_inc(f_out, 1)
                act.wait_ge(f_out, 3)
                A.activation(flat(az), flat(az), ACT.Ln, bias=C("one")).then_inc(f_out, 1)
                A.activation(flat(kk), flat(bf), ACT.Sigmoid, scale=-1.0).then_inc(f_out, 1)
                for i in range(len(steps)):
                    act.wait_ge(diff_ready, 2 * i + 2)
                    A.activation(E[:, i % 2, :], E[:, i % 2, :], ACT.Exp).then_inc(decay_ready, 1)
                act.wait_ge(tail_in, 2)
                A.activation(flat(kd), flat(kd), ACT.Exp).then_inc(tail_exp, 1)
                A.activation(flat(qd), flat(cum), ACT.Exp).then_inc(tail_exp, 1)
                A.activation(et, cum.rearrange("p c (j k) -> p c j k", k=P)[:, :, :, P - 1], ACT.Exp).then_inc(tail_exp, 1)
                for hd in range(H):
                    act.wait_ge(off_done, hd + 1)
                    b0 = 4 * (hd % 2)
                    A.activation(off[:, hd, 0:512], ps[b0][:, :], ACT.Copy).then_inc(off_copied, 1)
                    A.activation(off[:, hd, 512:768], ps[b0 + 1][:, 0:256], ACT.Copy).then_inc(off_copied, 1)
                for c in range(2):
                    act.wait_ge(o_done, c + 1)
                    A.activation(o[:, c, :], ps[2 + 4 * c][:, :], ACT.Copy)

            @st.block.vector
            def _(dve):
                order = Order(dve, st.sem("dve_order"))
                ln_lb, ln_1m, one_m = lbc[:, 0:2], lbc[:, 2:4], lbc[:, 4:6]
                V.scalar_tensor_tensor(out=flat(az), in0=flat(bf), scalar=-1.0, in1=flat(bf), op0=ALU.mult, op1=ALU.max) \
                 .then_inc(f_in, 1)
                dve.wait_ge(f_out, 2)
                order.done(V.scalar_tensor_tensor(out=flat(B), in0=flat(bf), scalar=0.0, in1=flat(sp2), op0=ALU.min, op1=ALU.subtract))
                for c in range(2):
                    order.done(V.tensor_scalar(B[:, c, :], B[:, c, :], ln_1m[:, c:c + 1], None, ALU.add))
                    order.done(V.tensor_scalar(mxv[:, c, :], B[:, c, :], ln_lb[:, c:c + 1], None, ALU.max))
                    order.done(V.scalar_tensor_tensor(out=az[:, c, :], in0=B[:, c, :], scalar=ln_lb[:, c:c + 1],
                                                      in1=mxv[:, c, :], op0=ALU.min, op1=ALU.subtract))
                V.memset(et, 0.0).then_inc(f_in, 1)
                dve.wait_ge(f_out, 4)
                order.done(V.tensor_tensor(flat(lf), flat(mxv), flat(az), ALU.add))
                for c in range(2):
                    order.done(V.tensor_tensor_scan(cum[:, c, :], C("restart"), lf[:, c, :], 0.0, ALU.mult, ALU.add))
                dve.wait_ge(f_out, 5)
                for c in range(2):
                    ins = V.tensor_scalar(kk[:, c, :], kk[:, c, :], one_m[:, c:c + 1], None, ALU.mult)
                    order.tick(ins)
                dve.wait_ge(order.sem, order.count)
                V.memset(et, 0.0).then_inc(x_ready, 1)
                for hd in range(H):
                    dve.wait_ge(own_done, hd + 1)
                    V.tensor_tensor(diag[:, hd, :, :], ps[hd][:, :].rearrange("p (j k) -> p j k", k=P),
                                    C("ident").unsqueeze(1).to_broadcast([P, ST, P]), ALU.mult).then_inc(own_copied, 1)
                dve.wait_ge(own_copied, H)
                for i in range(len(steps) + 2):
                    if i < len(steps):
                        v, c = steps[i]
                        L = LEVELS[v]
                        c0, c1_ = halves(cum, c, L)
                        e0, e1 = halves(E[:, i % 2:i % 2 + 1, :], 0, L)
                        mid = c0[:, :, L - 1:L].to_broadcast([P, S // (2 * L), L])
                        if i >= 2:
                            dve.wait_ge(x_ready, 2 * i - 1)
                        V.tensor_tensor(e0, mid, c0, ALU.subtract).then_inc(diff_ready, 1)
                        V.tensor_tensor(e1, c1_, mid, ALU.subtract).then_inc(diff_ready, 1)
                    if 1 <= i <= len(steps):
                        g = i - 1
                        v, c = steps[g]
                        L = LEVELS[v]
                        e0, e1 = halves(E[:, g % 2:g % 2 + 1, :], 0, L)
                        x0, x1 = halves(X[:, g % 2:g % 2 + 1, :], 0, L)
                        k0, _ = halves(kk, c, L)
                        _, q1 = halves(bq, c, L)
                        dve.wait_ge(decay_ready, i)
                        if g >= 2:
                            dve.wait_ge(lev_done, 2 * g - 2)
                        V.tensor_tensor(x0, e0, k0, ALU.mult).then_inc(x_ready, 1)
                        V.tensor_tensor(x1, e1, q1, ALU.mult).then_inc(x_ready, 1)
                    if i >= 2:
                        g = i - 2
                        v, c = steps[g]
                        lev = C("levels", None, v * P, (v + 1) * P).bitcast(I32)
                        for e in range(2):
                            hd = 2 * c + e
                            dve.wait_ge(lev_done, 2 * g + e + 1)
                            if v:
                                dve.wait_ge(lev_copied, 2 * (g - 2) + e + 1)
                            V.copy_predicated(diag[:, hd, :, :], lev.unsqueeze(1).to_broadcast([P, ST, P]),
                                              ps[4 + 2 * (g % 2) + e][:, :].rearrange("p (j k) -> p j k", k=P)) \
                             .then_inc(lev_copied, 1)
                for c in range(2):
                    cv = cum[:, c, :].rearrange("p (j k) -> p j k", k=P)
                    V.tensor_tensor(kd[:, c, :].rearrange("p (j k) -> p j k", k=P), cv[:, :, P - 1:P].to_broadcast([P, ST, P]),
                                    cv, ALU.subtract).then_inc(tail_in, 1)
                dve.wait_ge(tail_exp, 3)
                order.done(V.tensor_tensor(flat(kd), flat(kd), flat(kk), ALU.mult))
                order.done(V.tensor_tensor(flat(qd), flat(qd), flat(bq), ALU.mult))
                for c in range(2):
                    V.tensor_scalar(far[:, c, 0, :], kd[:, c, 0:P], et[:, c, 1:2], None, ALU.mult).then_inc(tail_ready, 1)
                    V.tensor_scalar(far[:, c, 1, :], qd[:, c, 3 * P:S], et[:, c, 2:3], None, ALU.mult).then_inc(tail_ready, 1)

            @st.block.tensor
            def _(pe):
                pe.wait_ge(x_ready, 1)
                for hd in range(H):
                    r = slice(64 * (hd % 2), 64 * (hd % 2) + 64)
                    for j in range(ST):
                        q = slice(j * P, (j + 1) * P)
                        mm = T.matmul(ps[hd][:, q], kk[r, hd // 2, q], bq[r, hd // 2, q], start=True, stop=True)
                    mm.then_inc(own_done, 1)
                for g, (v, c) in enumerate(steps):
                    pe.wait_ge(x_ready, 2 * g + 3)
                    for e in range(2):
                        if g >= 2:
                            pe.wait_ge(lev_copied, 2 * (g - 2) + e + 1)
                        r = slice(64 * e, 64 * e + 64)
                        for j in range(ST):
                            q = slice(j * P, (j + 1) * P)
                            mm = T.matmul(ps[4 + 2 * (g % 2) + e][:, q], X[r, g % 2, q], X[r, g % 2, q], start=True, stop=True)
                        mm.then_inc(lev_done, 1)
                pe.wait_ge(tail_ready, 4)
                pe.wait_ge(lev_copied, 4 * NL)
                for hd in range(H):
                    c, e = divmod(hd, 2)
                    r = slice(64 * e, 64 * e + 64)
                    b0 = 4 * (hd % 2)
                    if hd >= 2:
                        pe.wait_ge(off_copied, 2 * (hd - 2) + 2)
                    T.matmul(ps[b0][:, 0:P], kd[r, c, 0:P], qd[r, c, P:2 * P], start=True, stop=True)
                    T.matmul(ps[b0][:, P:2 * P], kd[r, c, 2 * P:3 * P], qd[r, c, 3 * P:S], start=True, stop=True)
                    for a, (lhs, bank, at) in enumerate(((far[r, c, 0, :], ps[b0], 2 * P), (kd[r, c, P:2 * P], ps[b0 + 1], 0))):
                        T.matmul(bank[:, at:at + P], lhs, qd[r, c, 2 * P:3 * P], start=True, stop=True)
                        mm = T.matmul(bank[:, at + P:at + 2 * P], lhs, far[r, c, 1, :], start=True, stop=True)
                    mm.then_inc(off_done, 1)
                for hd in range(H):
                    c, e = divmod(hd, 2)
                    pe.wait_ge(off_copied, 2 * hd + 2)
                    out = ps[2 + 4 * c][64 * e:64 * e + 64, :]
                    v_ = lambda j: vn[:, j, P + hd * HD:P + (hd + 1) * HD]
                    T.matmul(out[:, 0:P], v_(0), diag[:, hd, 0, :], start=True, stop=True)
                    T.matmul(out[:, P:2 * P], v_(0), off[:, hd, 0:P], start=True, stop=False)
                    T.matmul(out[:, P:2 * P], v_(1), diag[:, hd, 1, :], start=False, stop=True)
                    T.matmul(out[:, 2 * P:S], v_(0), off[:, hd, 2 * P:4 * P], start=True, stop=False)
                    T.matmul(out[:, 2 * P:S], v_(1), off[:, hd, 4 * P:6 * P], start=False, stop=False)
                    T.matmul(out[:, 2 * P:3 * P], v_(2), diag[:, hd, 2, :], start=False, stop=False)
                    T.matmul(out[:, 3 * P:S], v_(2), off[:, hd, P:2 * P], start=False, stop=False)
                    mm = T.matmul(out[:, 3 * P:S], v_(3), diag[:, hd, 3, :], start=False, stop=True)
                    if e:
                        mm.then_inc(o_done, 1)

        with Stage() as st:
            p_, a_, v_ = head_output(st, Space(M2_END), "hg", o, col(c2, "hgrn_norm"), bg, 4, qd)
            st.block.tensor(p_)
            st.block.scalar(a_)
            st.block.vector(v_)

    def mixer2_delta(l):
        sp_ = Space(M2_END)
        cv = sp_.get(6, S)
        late = sp_.at
        rowg, rowG, rs1, rs2 = [sp_.get(S) for _ in range(4)]
        rowc = sp_.get(S)
        cols = sp_.get(ST, 68)
        ecol = sp_.get(ST, 12)
        gm, Lm, tb = sp_.get(S), sp_.get(S), sp_.get(S)
        AT, qkT = sp_.get(H, ST, P), sp_.get(H, ST, P)
        Tn, Tt = sp_.get(H, ST, P), sp_.get(H, ST, P)
        low = sp_.get(2, ST, P)
        Xs = sp_.get(2, ST, P)
        nega = sp_.get(2)
        kN = n[:, 0:2, :].rearrange("p a (b c) -> p (a b) c", c=256)
        vN = n[:, 2:4, :].rearrange("p a (b c) -> p (a b) c", c=256)
        kdec = n[:, 4:6, :].rearrange("p a (b c) -> p (a b) c", c=256)
        U = n[:, 6:8, :].rearrange("p a (b c) -> p (a b) c", c=256)
        qd = cx[:, 0:2, 0:S]
        WT = cx[:, 2:4, 0:S]
        eGB = cx[:, 4:6, 0:S]
        flat = lambda a: a.rearrange("p c s -> p (c s)")
        chunks = lambda a: a.rearrange("p (j k) -> p j k", k=P)

        def headcols(i):
            return ecol[:, :, 4 * i:4 * i + 4].unsqueeze(3).to_broadcast([P, ST, H, HD])

        with Stage() as st:
            conv_ready, silu_ready = st.sem("conv_ready"), st.sem("silu_ready")
            norms = [Norm(st, f"n{c}", [cv[:, c, :]], [cv[:, c, :]], [HD ** -0.5 if c < 2 else 1.0], 1.0, Space(late + 3 * S + c * 4 * S),
                          ps[c][:, :], lhs="heads") for c in range(4)]
            g_in, g_out = st.sem("g_in"), st.sem("g_out")

            @st.block.tensor
            def _(pe):
                for x in norms:
                    x.pe(pe)

            @st.block.scalar
            def _(act):
                for c in range(6):
                    act.wait_ge(conv_ready, c + 1)
                    A.activation(cv[:, c, :], cv[:, c, :], ACT.Silu).then_inc(silu_ready, 1)
                act.wait_ge(silu_ready, 6)
                for x in norms:
                    x.act(act)

            @st.block.vector
            def _(dve):
                order = Order(dve, st.sem("dve_order"))
                for c in range(6):
                    w_ = lambda k: col(c2, "conv_w", 4 * c + k)
                    order.done(V.tensor_scalar(cv[:, c, :], cx[:, c, 0:S], w_(0), None, ALU.mult))
                    for k in range(1, 4):
                        ins = V.scalar_tensor_tensor(out=cv[:, c, :], in0=cx[:, c, k:k + S], scalar=w_(k), in1=cv[:, c, :],
                                                     op0=ALU.mult, op1=ALU.add)
                        if k < 3:
                            order.done(ins)
                    ins.then_inc(conv_ready, 1)
                for x in norms:
                    x.dve(dve)

        R = slice(0, 4)
        with Stage() as st:
            g_in, g_out, rows_ready = st.sem("g_in"), st.sem("g_out"), st.sem("rows_ready")
            zeroed, cols_done, cols_ready = st.sem("zeroed"), st.sem("cols_done"), st.sem("cols_ready")
            spread, scan_ready, decay_ready, head_ready = (st.sem("spread"), st.sem("scan_ready"), st.sem("decay_ready"),
                                                           st.sem("head_ready"))
            nat_done, nat_copied, eg_done, eg_ready = (st.sem("nat_done"), st.sem("nat_copied"), st.sem("eg_done"),
                                                       st.sem("eg_ready"))
            ecols_ready = st.sem("ecols_ready")

            @st.block.gpsimd
            def _(pool):
                G.memset(rowc[0:68, :], 0.0).then_inc(zeroed, 1)

            @st.block.scalar
            def _(act):
                act.wait_ge(zeroed, 1)
                A.activation(rowc[R, :], cb[R, :], ACT.Sigmoid).then_inc(g_out, 1)
                A.activation(nega[R, 0:1], col(c2, "a_log", 0, 4), ACT.Exp).then_inc(g_out, 1)
                A.activation(rowg[R, :], ca[R, :], ACT.Identity, bias=col(c2, "dt_bias", 0, 4)).then_inc(g_out, 1)
                act.wait_ge(g_in, 1)
                A.activation(rs1[R, :], rs1[R, :], ACT.Exp, scale=-1.0).then_inc(g_out, 1)
                act.wait_ge(g_out, 4)
                A.activation(rs1[R, :], rs1[R, :], ACT.Ln, bias=C("one", 4)).then_inc(g_out, 1)
                act.wait_ge(cols_done, 1)
                A.activation(cols.rearrange("p j c -> p (j c)"), ps[7][:, 0:ST * 68], ACT.Copy).then_inc(cols_ready, 1)
                act.wait_ge(cols_ready, 1)
                A.activation(ecol[:, :, 0:4], cols[:, :, 32:36], ACT.Exp).then_inc(cols_ready, 1)
                A.activation(ecol[:, :, 4:8], cols[:, :, 64:68], ACT.Exp).then_inc(cols_ready, 1)
                for c in range(2):
                    act.wait_ge(eg_done, c + 1)
                    A.activation(eGB[:, c, :], ps[4 + c][:, :], ACT.Exp).then_inc(eg_ready, 1)
                for j in range(4):
                    act.wait_ge(nat_done, j + 1)
                    A.activation((kN if j < 2 else vN)[:, 2 * (j % 2):2 * (j % 2) + 2, :].rearrange("p a c -> p (a c)"),
                                 ps[6 + j % 2][:, :], ACT.Copy).then_inc(nat_copied, 1)
                for hd in range(H):
                    act.wait_ge(scan_ready, hd + 1)
                    A.activation(Lm, gm, ACT.Exp).then_inc(decay_ready, 1)

            @st.block.tensor
            def _(pe):
                pe.wait_ge(rows_ready, 1)
                for j in range(ST):
                    mm = T.transpose(ps[7][:, 68 * j:68 * j + 68], rowc[0:68, j * P:(j + 1) * P], C("ident")[0:68, 0:68])
                mm.then_inc(cols_done, 1)
                for c in range(2):
                    T.matmul(ps[4 + c][:, :], C("selp", 4, c * P, (c + 1) * P), rowG[R, :], start=True, stop=True).then_inc(eg_done, 1)
                pe.wait_ge(cols_ready, 1)
                for j in range(4):
                    if j >= 2:
                        pe.wait_ge(nat_copied, j - 1)
                    for a in range(2):
                        for p in range(2):
                            ch = 2 * (j % 2) + a
                            mm = T.transpose(ps[6 + j % 2][:, a * 256 + p * P:a * 256 + (p + 1) * P],
                                             cv[:, 2 + 2 * (j // 2) + p, ch * P:(ch + 1) * P], C("ident"))
                    mm.then_inc(nat_done, 1)
                for hd in range(H):
                    r = slice(64 * (hd % 2), 64 * (hd % 2) + 64)
                    if hd:
                        pe.wait_ge(head_ready, 2 * hd)
                    T.matmul(ps[0][:, :], C("sel", 4, hd * P, (hd + 1) * P), rowg[R, :], start=True, stop=True)
                    T.matmul(ps[1][:, :], C("sel", 4, hd * P, (hd + 1) * P), rowc[R, :], start=True, stop=True)
                    for b, at in ((2, 2), (3, 0)):
                        for j in range(ST):
                            q = slice(j * P, (j + 1) * P)
                            mm = T.matmul(ps[b][:, q], cv[r, 2 + hd // 2, q], cv[r, at + hd // 2, q], start=True, stop=True)
                    mm.then_inc(spread, 1)

            @st.block.vector
            def _(dve):
                order = Order(dve, st.sem("dve_order"))
                dve.wait_ge(g_out, 3)
                V.scalar_tensor_tensor(out=rs1[R, :], in0=rowg[R, :], scalar=-1.0, in1=rowg[R, :], op0=ALU.mult, op1=ALU.max) \
                 .then_inc(g_in, 1)
                dve.wait_ge(g_out, 5)
                order.done(V.scalar_tensor_tensor(out=rs2[R, :], in0=rowg[R, :], scalar=0.0, in1=rs1[R, :], op0=ALU.max, op1=ALU.add))
                order.done(V.tensor_scalar(rowg[R, :], rs2[R, :], nega[R, 0:1], -1.0, ALU.mult, ALU.mult))
                order.done(V.tensor_tensor_scan(rowG[R, :], C("restart", 4), rowg[R, :], 0.0, ALU.mult, ALU.add))
                gv = chunks(rowG[R, :])
                order.done(V.tensor_copy(rowc[32:36, :], rowG[R, :]))
                V.tensor_tensor(chunks(rowc[64:68, :]), gv[:, :, P - 1:P].to_broadcast([4, ST, P]), gv, ALU.subtract) \
                 .then_inc(rows_ready, 1)
                dve.wait_ge(cols_ready, 3)
                order.done(V.tensor_tensor(ecol[:, :, 8:12], ecol[:, :, 0:4], cols[:, :, 0:4], ALU.mult))
                dve.wait_ge(eg_ready, 2)
                order.done(V.tensor_tensor(qd, cv[:, 0:2, :], eGB, ALU.mult))
                dve.wait_ge(nat_copied, 4)
                hv = lambda a: a.rearrange("p j (e c) -> p j e c", c=HD)
                order.done(V.tensor_tensor(hv(kdec), hv(kN), headcols(1), ALU.mult))
                order.done(V.tensor_tensor(hv(kN), hv(kN), headcols(2), ALU.mult))
                order.done(V.tensor_tensor(hv(vN), hv(vN), cols[:, :, 0:4].unsqueeze(3).to_broadcast([P, ST, H, HD]), ALU.mult))
                for hd in range(H):
                    dve.wait_ge(spread, hd + 1)
                    if hd:
                        dve.wait_ge(decay_ready, hd)
                    order.done(V.tensor_tensor(gm, ps[0][:, :], C("strict4"), ALU.mult))
                    V.tensor_tensor_scan(gm, C("strict4"), gm, 0.0, ALU.mult, ALU.add).then_inc(scan_ready, 1)
                    dve.wait_ge(decay_ready, hd + 1)
                    order.done(V.tensor_tensor(tb, Lm, C("strict4"), ALU.mult))
                    order.done(V.tensor_tensor(tb, tb, ps[1][:, :], ALU.mult))
                    order.done(V.tensor_tensor(chunks(Lm), chunks(Lm), C("upto").unsqueeze(1).to_broadcast([P, ST, P]), ALU.mult))
                    V.tensor_tensor(AT[:, hd, :, :].rearrange("p j k -> p (j k)"), tb, ps[2][:, :], ALU.mult).then_inc(head_ready, 1)
                    V.tensor_tensor(qkT[:, hd, :, :].rearrange("p j k -> p (j k)"), Lm, ps[3][:, :], ALU.mult).then_inc(head_ready, 1)
                    dve.wait_ge(head_ready, 2 * hd + 2)

        steps = [(v, hd) for v in range(len(LEVELS)) for hd in range(H)]
        NS = len(steps)
        with Stage() as st:
            eye_ready, low_ready, x_done, x_ready = st.sem("eye_ready"), st.sem("low_ready"), st.sem("x_done"), st.sem("x_ready")
            yz_done, updated = st.sem("yz_done"), st.sem("updated")

            @st.block.gpsimd
            def _(pool):
                for i, (v, hd) in enumerate(steps):
                    if i >= 2:
                        pool.wait_ge(x_done, i - 1)
                    G.tensor_tensor(low[:, i % 2, :, :], AT[:, hd, :, :],
                                    C("levels", None, v * P, (v + 1) * P).unsqueeze(1).to_broadcast([P, ST, P]), ALU.mult) \
                     .then_inc(low_ready, 1)

            @st.block.scalar
            def _(act):
                for i in range(NS):
                    act.wait_ge(x_done, i + 1)
                    if i >= 2:
                        act.wait_ge(yz_done, 2 * (i - 2) + 2)
                    A.activation(Xs[:, i % 2, :, :].rearrange("p j k -> p (j k)"), ps[i % 2][:, :], ACT.Copy).then_inc(x_ready, 1)

            @st.block.tensor
            def _(pe):
                pe.wait_ge(eye_ready, 2 * H)
                for i in range(NS + 1):
                    if i < NS:
                        v, hd = steps[i]
                        pe.wait_ge(low_ready, i + 1)
                        if v:
                            pe.wait_ge(updated, 2 * (i - H) + 2)
                        if i >= 2:
                            pe.wait_ge(x_ready, i - 1)
                        for j in range(ST):
                            mm = T.matmul(ps[i % 2][:, j * P:(j + 1) * P], low[:, i % 2, j, :], Tn[:, hd, j, :], start=True, stop=True)
                        mm.then_inc(x_done, 1)
                    if i >= 1:
                        g = i - 1
                        v, hd = steps[g]
                        pe.wait_ge(x_ready, g + 1)
                        if g >= 2:
                            pe.wait_ge(updated, 2 * (g - 2) + 2)
                        for j in range(ST):
                            mm = T.matmul(ps[2 + g % 2][:, j * P:(j + 1) * P], Tt[:, hd, j, :], Xs[:, g % 2, j, :], start=True, stop=True)
                        mm.then_inc(yz_done, 1)
                        for j in range(ST):
                            mm = T.matmul(ps[4 + g % 2][:, j * P:(j + 1) * P], Xs[:, g % 2, j, :], Tt[:, hd, j, :], start=True, stop=True)
                        mm.then_inc(yz_done, 1)

            @st.block.vector
            def _(dve):
                eye = C("ident").unsqueeze(1).to_broadcast([P, ST, P])
                for hd in range(H):
                    V.tensor_copy(Tn[:, hd, :, :], eye).then_inc(eye_ready, 1)
                    V.tensor_copy(Tt[:, hd, :, :], eye).then_inc(eye_ready, 1)
                dve.wait_ge(eye_ready, 2 * H)
                for i, (v, hd) in enumerate(steps):
                    if v:
                        dve.wait_ge(updated, 2 * (i - H) + 2)
                    for a, X_ in enumerate((Tn, Tt)):
                        dve.wait_ge(yz_done, 2 * i + 2)
                        f = X_[:, hd, :, :].rearrange("p j k -> p (j k)")
                        V.tensor_tensor(f, f, ps[2 + 2 * a + i % 2][:, :], ALU.subtract).then_inc(updated, 1)

        state = rowg[:, 0:2 * HD].rearrange("p (a c) -> p a c", c=HD)
        vnew = rowG[:, 0:H * HD].rearrange("p (a c) -> p a c", c=HD)
        o = low[:, 0:2, :, :].rearrange("p a j k -> p a (j k)")
        with Stage() as st:
            u_done, u_copied, w_done, w_copied = st.sem("u_done"), st.sem("u_copied"), st.sem("w_done"), st.sem("w_copied")
            zeroed, ws_done, v_ready, s_done, s_ready = (st.sem("zeroed"), st.sem("ws_done"), st.sem("v_ready"), st.sem("s_done"),
                                                         st.sem("s_ready"))
            o_done = st.sem("o_done")

            @st.block.gpsimd
            def _(pool):
                G.memset(state, 0.0).then_inc(zeroed, 1)

            @st.block.tensor
            def _(pe):
                for j in range(ST):
                    for hd in range(H):
                        mm = T.matmul(ps[j // 2][:, (j % 2) * 256 + hd * HD:(j % 2) * 256 + (hd + 1) * HD], Tt[:, hd, j, :],
                                      vN[:, j, hd * HD:(hd + 1) * HD], start=True, stop=True)
                mm.then_inc(u_done, 1)
                for hd in range(H):
                    for j in range(ST):
                        mm = T.matmul(ps[2 + hd // 2][64 * (hd % 2):64 * (hd % 2) + 64, j * P:(j + 1) * P],
                                      kN[:, j, hd * HD:(hd + 1) * HD], Tt[:, hd, j, :], start=True, stop=True)
                mm.then_inc(w_done, 1)
                pe.wait_ge(w_copied, 2)
                pe.wait_ge(u_copied, 2)
                pe.wait_ge(zeroed, 1)
                for j in range(ST):
                    q = slice(j * P, (j + 1) * P)
                    if j:
                        pe.wait_ge(s_ready, 2 * j)
                    for hd in range(H):
                        r = slice(64 * (hd % 2), 64 * (hd % 2) + 64)
                        mm = T.matmul(ps[4 * (1 - hd % 2)][:, (hd // 2) * HD:(hd // 2 + 1) * HD], WT[r, hd // 2, q], state[r, hd // 2, :],
                                      start=True, stop=True)
                        if hd >= 2:
                            mm.then_inc(ws_done, 1)
                    pe.wait_ge(v_ready, 2 * j + 2)
                    for hd in range(H):
                        r = slice(64 * (hd % 2), 64 * (hd % 2) + 64)
                        mm = T.matmul(ps[5][r, (hd // 2) * HD:(hd // 2 + 1) * HD], kdec[:, j, hd * HD:(hd + 1) * HD], vnew[:, hd, :],
                                      start=True, stop=True)
                    for hd in range(H):
                        r = slice(64 * (hd % 2), 64 * (hd % 2) + 64)
                        out = ps[6 + hd // 2][r, q]
                        T.matmul(out, state[r, hd // 2, :], qd[r, hd // 2, q], start=True, stop=False)
                        mm = T.matmul(out, vnew[:, hd, :], qkT[:, hd, j, :], start=False, stop=True)
                    mm.then_inc(s_done, 1)

            @st.block.scalar
            def _(act):
                act.wait_ge(u_done, 1)
                for a in range(2):
                    A.activation(U[:, 2 * a:2 * a + 2, :].rearrange("p a c -> p (a c)"), ps[a][:, :], ACT.Copy).then_inc(u_copied, 1)
                act.wait_ge(w_done, 1)
                for c in range(2):
                    A.activation(WT[:, c, :], ps[2 + c][:, :], ACT.Copy).then_inc(w_copied, 1)
                act.wait_ge(s_done, ST)
                for c in range(2):
                    A.activation(o[:, c, :], ps[6 + c][:, :], ACT.Copy).then_inc(o_done, 1)

            @st.block.vector
            def _(dve):
                dve.wait_ge(u_copied, 2)
                for j in range(ST):
                    dve.wait_ge(ws_done, 2 * j + 2)
                    if j:
                        dve.wait_ge(s_done, j)
                    for e in range(2):
                        V.tensor_tensor(vnew.rearrange("p (a e) c -> p a e c", e=2)[:, :, e, :],
                                        U[:, j, :].rearrange("p (a e c) -> p a e c", e=2, c=HD)[:, :, e, :],
                                        ps[4 * (1 - e)][:, 0:2 * HD].rearrange("p (a c) -> p a c", c=HD), ALU.subtract) \
                         .then_inc(v_ready, 1)
                    dve.wait_ge(s_done, j + 1)
                    for c in range(2):
                        V.scalar_tensor_tensor(out=state[:, c, :], in0=state[:, c, :], scalar=eGB[:, c, (j + 1) * P - 1:(j + 1) * P],
                                               in1=ps[5][:, c * HD:(c + 1) * HD], op0=ALU.mult, op1=ALU.add).then_inc(s_ready, 1)

        with Stage() as st:
            p_, a_, v_ = head_output(st, Space(late + 10 * S), "gd", o, col(c2, "gdn_norm"), cgt, 6, qd)
            st.block.tensor(p_)
            st.block.scalar(a_)
            st.block.vector(v_)

    load_inputs()
    with nc.Fori(0, DEPTH) as l:
        load_parameters(l, "par1", n1)
        feed_forward(l, t["ffn1_gu"], t["ffn1_dn"], [col(c1, "ffn1_norm", k) for k in range(DT)])
        mixer1_project(l)
        mixer1_attention(l)
        mixer1_mlstm(l)
        mixer1_fourier(l)
        project_out(l, t["out1"])
        feed_forward(l, t["ffn2_gu"], t["ffn2_dn"], [col(c1, "ffn2_norm", k) for k in range(DT)])
        embed_layer(l)
    final_norm()
    with nc.Fori(0, DEPTH) as l:
        adaptive(l)
        mixer2_project(l)
        mixer2_window(l)
        mixer2_hgrn(l)
        mixer2_delta(l)
        project_out(l, t["out2"], [modc[:, 16 + k:17 + k] for k in range(DT)])
        feed_forward(l, t["ffn3_gu"], t["ffn3_dn"], [gain_f[:, k:k + 1] for k in range(DT)],
                     [modc[:, 24 + k:25 + k] for k in range(DT)], [modc[:, 40 + k:41 + k] for k in range(DT)])
    with Stage() as st:
        @st.block.sync
        def _(sp):
            sp.dma_start(t["out"].rearrange("(k p) s -> p k s", p=P), h[:, :, :]).then_inc(st.sem("stored"), 16)
            sp.wait_ge(st.sem("stored"), 16)


def tiles(w, cols=None):
    L, K, N = w.shape
    return np.ascontiguousarray(w.reshape(L, K // P, P, N // P, P).transpose(0, 3, 2, 1, 4)
                                .reshape(L, N // P, P, K))


def rows(w):
    L, K, N = w.shape
    return np.ascontiguousarray(w.reshape(L, K // P, P, N).transpose(0, 2, 1, 3).reshape(L, P, -1))


def column(v):
    return v.reshape(v.shape[0], -1, P).transpose(0, 2, 1)


def padded(a, rows_at, width):
    out = np.zeros((a.shape[0], P, 1), a.dtype)
    for g, r in enumerate(rows_at):
        out[:, r:r + width, 0] = a[:, g]
    return out


def pairs(w):
    out = np.zeros((w.shape[0], P, 2, P), w.dtype)
    for g in range(4):
        b = 64 * (g % 2)
        out[:, b:b + 64, g // 2, b:b + 64] = w[:, g]
    return out.reshape(w.shape[0], P, 2 * P)


def lay_out(x):
    L = DEPTH
    f = {}
    f["x"] = np.ascontiguousarray(x["x"][0].T)
    f["p"] = np.ascontiguousarray(x["p"][:, 0].transpose(0, 2, 1))
    f["pos"] = np.ascontiguousarray(x["positions"]).astype(np.int32)
    f["pos2"] = np.ascontiguousarray(x["positions_2"]).astype(np.int32)
    for name in ("ffn1", "ffn2"):
        f[name + "_gu"] = np.stack([tiles(x[name + "_w_gate"]), tiles(x[name + "_w_up"])], 3).reshape(L, FT, P, 2 * D)
        f[name + "_dn"] = tiles(x[name + "_w_down"])
    f["ffn3_gu"] = np.stack([tiles(x["w_gate_2"]), tiles(x["w_up_2"])], 3).reshape(L, FT, P, 2 * D)
    f["ffn3_dn"] = tiles(x["w_down_2"])

    w = x["w_in"]
    o = np.cumsum([0, 384, 256, 64, 256, 256, 256, 16, 256])
    cq, ckv, kr, mx, mv, mo, mif, fin = [w[:, :, o[i]:o[i + 1]] for i in range(8)]
    f["in1_t"] = tiles(np.concatenate([cq, ckv, mx, mo, kr, kr], 2))
    gates = np.zeros((L, D, 2, 36), np.float32)
    for g in range(2):
        for d in range(2):
            gates[:, :, g, 32 * d:32 * d + H] = mif[:, :, 8 * g + 4 * d:8 * g + 4 * d + 4]
    f["in1_g"] = rows(gates.reshape(L, D, 72))
    f["in1_r"] = rows(np.concatenate([mv, fin], 2))
    uq = x["mla_w_uq"].reshape(L, 384, 4, 192)
    f["uq"] = rows(np.concatenate([uq[..., :128].reshape(L, 384, 512), uq[..., 128:].reshape(L, 384, 256)], 2))
    ukv = x["mla_w_ukv"].reshape(L, 256, 4, 256)
    f["ukv"] = rows(np.concatenate([ukv[..., :128].reshape(L, 256, 512), ukv[..., 128:].reshape(L, 256, 512)], 2))
    f["mqk"] = np.ascontiguousarray(np.concatenate([pairs(x["mlstm_w_q"]), pairs(x["mlstm_w_k"])], 2))
    f["fnw"] = pairs(x["fnet_w"])
    f["out1"] = tiles(x["w_out"])
    f["pleg"] = tiles(x["ple_w_gate"])
    f["plep"] = rows(x["ple_w_proj"])
    f["par1"] = np.ascontiguousarray(np.concatenate([
        column(x["ffn1_norm"]), column(x["mix_norm"]), column(x["mla_q_norm"]), column(x["mla_kv_norm"]),
        x["mlstm_conv_w"].reshape(L, 5, 2, P).transpose(0, 3, 2, 1).reshape(L, P, 10), column(x["mlstm_conv_b"]),
        padded(x["mlstm_i_bias"], (0, 32), H), padded(x["mlstm_f_bias"], (0, 32), H),
        column(x["mlstm_head_norm"]), column(x["mlstm_skip"]), column(x["fnet_b"]), column(x["ffn2_norm"]),
        column(x["ple_gate_norm"]), column(x["ple_post_norm"])], 2))

    w = x["w_in_2"]
    o = np.cumsum([0, 512, 128, 128, 256, 256, 256, 256, 768, 256, 4, 4])
    aq, ak, av, bq, bf, bv, bg, cc, cgt, cb, ca = [w[:, :, o[i]:o[i + 1]] for i in range(11)]
    order = [0, 4, 1, 5, 2, 6, 3, 7]
    aq = aq.reshape(L, D, 8, HD)[:, :, order].reshape(L, D, 512)
    f["in2_t"] = tiles(np.concatenate([aq, ak, bq, bf, bg, cc, cgt], 2))
    f["in2_g"] = rows(np.concatenate([cb, ca], 2))
    f["in2_r"] = rows(np.concatenate([av, bv], 2))
    wo = x["w_out_2"]
    f["out2"] = tiles(np.concatenate([wo[:, :512].reshape(L, 8, HD, D)[:, order].reshape(L, 512, D), wo[:, 512:]], 1))
    f["ada"] = np.ascontiguousarray(x["ada_w_2"].reshape(L, DT, P, 6 * D))
    two = lambda v: np.concatenate([v, v], 1)[:, :, None]
    sinks = np.broadcast_to(x["attn_sinks_2"][:, None, order], (L, P, 8))
    f["par2"] = np.ascontiguousarray(np.concatenate([
        column(x["norm_mix_2"]), two(x["attn_q_norm_2"]), two(x["attn_k_norm_2"]), sinks, two(x["hgrn_out_norm_2"]),
        x["gdn_conv_w_2"].reshape(L, 4, 6, P).transpose(0, 3, 2, 1).reshape(L, P, 24),
        padded(x["gdn_a_log_2"][:, None], (0,), H), padded(x["gdn_dt_bias_2"][:, None], (0,), H),
        two(x["gdn_out_norm_2"]), column(x["norm_ffn_2"]), column(x["ada_b_2"])], 2))
    f["parg"] = np.ascontiguousarray(np.concatenate([
        column(x["final_norm"][None])[0], column(x["c_2"])[0],
        column(x["hgrn_lb_logits_2"]).transpose(1, 0, 2).reshape(P, 4)], 1))

    i = np.arange(S)
    ang = 2 * np.pi * ((i[:, None] * i[None, :]) % S) / S
    unit = 1.0 / math.sqrt(S * HD)
    dft = np.stack([np.cos(ang) * unit, np.sin(ang) * unit]).astype(np.float32)
    f["dft"] = np.ascontiguousarray(dft.reshape(2, ST, P, S).transpose(2, 0, 1, 3).reshape(P, 2 * ST * S))
    return f


def kernel(**inputs):
    import concourse.bacc as bacc
    from concourse.bass_utils import run_bass_kernel_spmd as run

    arrays = lay_out({k: np.asarray(v) for k, v in inputs.items()})
    arrays["cst"], where = pack(constant_columns())
    nc = bacc.Bacc("TRN2", target_bir_lowering=False, num_devices=1)
    t = {k: nc.dram_tensor("in_" + k, a.shape, mybir.dt.from_np(a.dtype), kind="ExternalInput").ap()
         for k, a in arrays.items()}
    t["out"] = nc.dram_tensor("out", (D, S), F32, kind="ExternalOutput").ap()
    build(nc, t, where)
    r = run(nc, [{"in_" + k: a for k, a in arrays.items()}], core_ids=[0])
    return np.ascontiguousarray(r.results[0]["out"].T)[None]
```

```python
import math
from contextlib import ExitStack

import numpy as np

import concourse.bass as bass
from concourse import mybir

F32 = mybir.dt.float32
F32R = mybir.dt.float32r
I32 = mybir.dt.int32
ALU = mybir.AluOpType
ACT = mybir.ActivationFunctionType
AX = mybir.AxisListType

P = 128
S = 512
ST = S // P
D = 1024
DT = D // P
FF = 2816
FT = FF // P
DEPTH = 2
HD = 64
H = 4
EPS = 1e-6
BIG = 1e30
LEVELS = [1 << e for e in range(7)]
MLA_SCALE = (128 + 64) ** -0.5


def constant_columns():
    f = np.float32
    i = np.arange(P)
    same64 = (i[:, None] // 64 == i[None, :] // 64)
    out = {"ident": np.eye(P, dtype=f), "ones": np.ones((P, P), f), "heads": same64.astype(f)}

    def rotation(width):
        r = np.zeros((P, P), f)
        for base in (0, 64):
            for m in range(width // 2):
                r[base + m + width // 2, base + m] = -1.0
                r[base + m, base + m + width // 2] = 1.0
        return r

    out["rot_mla"] = rotation(64)
    out["rot_win"] = rotation(16)
    out["upto"] = (i[:, None] <= i[None, :]).astype(f)
    out["from"] = (i[:, None] >= i[None, :]).astype(f)
    out["strict4"] = np.tile((i[:, None] < i[None, :]).astype(f), (1, ST))
    lev = [((i[:, None] // (2 * L) == i[None, :] // (2 * L)) & (i[:, None] % (2 * L) < L)
            & (i[None, :] % (2 * L) >= L)).astype(f) for L in LEVELS]
    out["levels"] = np.concatenate(lev, 1)
    q, k = i[:, None], np.arange(2 * P)[None, :]
    delta = q + P - k
    rest = np.where((delta >= 0) & (delta < P), 0.0, -BIG).astype(f)
    first = np.where(k >= P, rest, -BIG).astype(f)
    out["window"] = np.concatenate([first, rest, rest], 1)
    out["restart"] = np.tile((np.arange(S) % P != 0).astype(f), (P, 1))
    c = np.arange(HD)
    ang = 2 * np.pi * ((c[:, None] * c[None, :]) % HD) / HD
    z = np.zeros((P, P), f)
    dc, ds = z.copy(), z.copy()
    for b in (0, HD):
        dc[b:b + HD, b:b + HD] = np.cos(ang)
        ds[b:b + HD, b:b + HD] = -np.sin(ang)
    out["dft_c"], out["dft_s"] = dc, ds
    sel = np.zeros((36, 8, P), f)
    selp = np.zeros((36, 4, P), f)
    for d in range(2):
        for h in range(H):
            sel[32 * d + h, 4 * d + h] = 1.0
            selp[32 * d + h, 2 * d + h // 2, 64 * (h % 2):64 * (h % 2) + 64] = 1.0
    out["sel"] = sel.reshape(36, -1)
    out["selp"] = selp.reshape(36, -1)
    inv1 = np.zeros((P, 1), f)
    inv2 = np.zeros((P, 1), f)
    for b in (0, 64):
        t = 1.0 / (10000.0 ** (np.arange(0, 64, 2) / 64.0))
        inv1[b:b + 32, 0] = t
        inv1[b + 32:b + 64, 0] = t
        t = 500000.0 ** (-np.arange(8) * 2.0 / 16.0)
        inv2[b:b + 8, 0] = t
        inv2[b + 8:b + 16, 0] = t
    out["inv_mla"], out["inv_win"] = inv1, inv2
    out["eps"] = np.full((P, 1), EPS, f)
    out["one"] = np.full((P, 1), 1.0, f)
    return out


def pack(columns):
    at, where = 0, {}
    for name, a in columns.items():
        where[name] = (at, a.shape[1], a.shape[0])
        at += a.shape[1]
    whole = np.zeros((P, at), np.float32)
    for name, a in columns.items():
        whole[:a.shape[0], where[name][0]:where[name][0] + a.shape[1]] = a
    return whole, where


PAR1 = {"ffn1_norm": 8, "mix_norm": 8, "q_norm": 3, "kv_norm": 2, "conv_w": 10, "conv_b": 2, "i_bias": 1,
        "f_bias": 1, "head_norm": 2, "skip": 2, "fnet_b": 2, "ffn2_norm": 8, "gate_norm": 8, "post_norm": 8}
PAR2 = {"norm_mix": 8, "q_norm": 1, "k_norm": 1, "sinks": 8, "hgrn_norm": 1, "conv_w": 24, "a_log": 1,
        "dt_bias": 1, "gdn_norm": 1, "norm_ffn": 8, "ada_b": 48}
PARG = {"final_norm": 8, "cond": 8, "lb": 4}


def columns_of(table):
    at, out = 0, {}
    for name, n in table.items():
        out[name] = (at, n)
        at += n
    return out, at


def build(nc, t, where):
    ctx = ExitStack()
    with ctx:
        program(nc, t, where, ctx)


def program(nc, t, where, ctx):
    def sb(name, shape, dt=F32):
        return ctx.enter_context(nc.sbuf_tensor(name, shape, dt))

    h = sb("stream", [P, DT, S])
    cst = sb("consts", [P, t["cst"].shape[1]])
    c1, n1 = columns_of(PAR1)
    c2, n2 = columns_of(PAR2)
    cg, ng = columns_of(PARG)
    par = sb("par", [P, max(n1, n2)])
    parg = sb("parg", [P, ng])
    rope = sb("rope", [P, 4, S])
    mod = sb("mod", [P, DEPTH, 48])
    ada = sb("ada", [P, DEPTH, 48])
    lbt = sb("lbt", [P, DEPTH, 3, 2])
    ps = [ctx.enter_context(nc.psum_tensor(f"ps{i}", [P, S], F32)) for i in range(8)]

    V, A, T, G = nc.vector, nc.scalar, nc.tensor, nc.gpsimd

    class Stage:
        last = None
        count = 0

        def __init__(self):
            self.held = ExitStack()
            self.sems = {}
            Stage.count += 1

        def sem(self, name):
            if name not in self.sems:
                self.sems[name] = self.held.enter_context(nc.semaphore(f"{name}_{Stage.count}"))
            return self.sems[name]

        def clear(self, sp):
            for sem in self.sems.values():
                sp.sem_clear(sem)

        def __enter__(self):
            self.manager = nc.Block()
            self.block = self.manager.__enter__()
            if Stage.last:
                self.block.sync(Stage.last.clear)
            return self

        def __exit__(self, *e):
            r = self.manager.__exit__(*e)
            if Stage.last:
                Stage.last.held.close()
            Stage.last = self
            return r

        @staticmethod
        def clear_last():
            with nc.Block() as cleared:
                cleared.sync(Stage.last.clear)
            Stage.last.held.close()
            Stage.last = None

    class Order:

        def __init__(self, eng, sem):
            self.eng, self.sem, self.count = eng, sem, 0

        def tick(self, ins):
            ins.then_inc(self.sem, 1)
            self.count += 1
            return self.count

        def done(self, ins):
            self.tick(ins)
            self.eng.wait_ge(self.sem, self.count)

    class Scope(ExitStack):
        made = 0

        def sb(self, name, shape, dt=F32):
            Scope.made += 1
            return self.enter_context(nc.sbuf_tensor(f"{name}_{Scope.made}", shape, dt))

        def space(self, size):
            return Space(self.sb("work", [P, size]), size)

    class Space:

        def __init__(self, tensor, size, at=0):
            self.tensor, self.size, self.at = tensor, size, at

        def copy(self):
            return Space(self.tensor, self.size, self.at)

        def get(self, *shape):
            size = int(np.prod(shape))
            assert self.at + size <= self.size, (self.at + size, self.size)
            a = self.tensor[:, self.at:self.at + size]
            self.at += size
            names = "abcd"[:len(shape)]
            if len(shape) > 1:
                a = a.rearrange(f"p ({' '.join(names)}) -> p {' '.join(names)}",
                                **dict(zip(names[1:], shape[1:])))
            return a

    def C(name, rows=None, a=0, b=None):
        at, width, r = where[name]
        return cst[0:(rows or r), at + a:at + (width if b is None else b)]

    def cond(k):
        return col(cg, "cond", k)

    def col(table, name, k=0, rows=P):
        at, width = table[name]
        src = parg if table is cg else par
        return src[0:rows, at + k:at + k + 1]

    V, A, T, G = nc.vector, nc.scalar, nc.tensor, nc.gpsimd

    def products(bank, lhs, rhs, kt):
        for k in range(kt):
            mm = T.matmul(bank, lhs(k), rhs(k), start=(k == 0), stop=(k == kt - 1))
        return mm

    def split_products(bank, lhs_hi, lhs_lo, rhs_hi, rhs_lo, kt, before=None):
        for k in range(kt):
            if before:
                before(k)
            T.matmul(bank, lhs_hi(k), rhs_hi(k), start=(k == 0), stop=False)
            T.matmul(bank, lhs_hi(k), rhs_lo(k), start=False, stop=False)
            mm = T.matmul(bank, lhs_lo(k), rhs_hi(k), start=False, stop=(k == kt - 1))
        return mm

    ITEM = 2 * DT * P

    class Weights:

        def __init__(self, st, scope):
            self.raw = scope.sb("raw", [P, 2, ITEM])
            self.hi = scope.sb("w_hi", [P, 2, ITEM], F32R)
            self.lo = scope.sb("w_lo", [P, 2, ITEM], F32R)
            self.landed = [st.sem(f"w_landed{b}") for b in range(2)]
            self.hi_ready, self.lo_ready, self.used = st.sem("w_hi_ready"), st.sem("w_lo_ready"), st.sem("w_used")

        def load(self, sp, b, n, src, first=False):
            if not first:
                sp.wait_ge(self.lo_ready, 2 * n + (b - 1))
            sp.dma_start(self.raw[:, b, 0:src.shape[-1]], src).then_inc(self.landed[b], 16)

        def high(self, act, b, n, size, first=False):
            act.wait_ge(self.landed[b], 16 * n + 16)
            if not first:
                act.wait_ge(self.used, 2 * n + (b - 1))
            A.activation(self.hi[:, b, 0:size], self.raw[:, b, 0:size], ACT.Copy).then_inc(self.hi_ready, 1)

        def low(self, dve, b, n, size):
            dve.wait_ge(self.hi_ready, 2 * n + (b + 1))
            V.tensor_tensor(self.lo[:, b, 0:size], self.raw[:, b, 0:size], self.hi[:, b, 0:size].bitcast(F32), ALU.subtract) \
             .then_inc(self.lo_ready, 1)

        def wait(self, pe, b, n):
            pe.wait_ge(self.lo_ready, 2 * n + (b + 1))

    class Split:

        def __init__(self, scope, name, kt):
            self.hi = scope.sb(name + "_hi", [P, kt, S], F32R)
            self.lo = scope.sb(name + "_lo", [P, kt, S], F32R)

    class Norm:

        def __init__(self, st, name, src, dst, gains, width, space, bank, lhs="ones", shifts=None):
            self.src, self.dst, self.gains, self.width, self.lhs = src, dst, gains, width, lhs
            self.shifts = shifts
            self.k = len(src)
            self.bank = bank
            self.sq = space.get(2, S)
            self.acc = space.get(S)
            self.root = self.acc if self.k > 1 else self.sq[:, 1, :]
            self.rstd = space.get(S)
            self.squares = st.sem(name + "_squares")
            self.added = st.sem(name + "_added")
            self.summed = st.sem(name + "_summed")
            self.rooted = st.sem(name + "_rooted")
            self.inverted = st.sem(name + "_inverted")
            self.ready = st.sem(name + "_ready")
            self.split = isinstance(dst, Split)
            if self.split:
                self.tmp = space.get(2, S)
                self.whole = space.get(2, S) if shifts else self.tmp
                self.scaled, self.high = st.sem(name + "_scaled"), st.sem(name + "_high")

        def square(self, act):
            for k in range(self.k):
                if k >= 2:
                    act.wait_ge(self.added, max(1, k - 2))
                A.activation(self.sq[:, k % 2, :], self.src[k], ACT.Square).then_inc(self.squares, 1)

        def add(self, dve):
            for k in range(1, self.k):
                dve.wait_ge(self.squares, k + 1)
                if k >= 2:
                    dve.wait_ge(self.added, k - 1)
                V.tensor_tensor(self.acc, self.sq[:, 0, :] if k == 1 else self.acc, self.sq[:, k % 2, :], ALU.add) \
                 .then_inc(self.added, 1)

        def act(self, act):
            self.square(act)
            self.act_finish(act)

        def act_finish(self, act):
            act.wait_ge(self.summed, 1)
            A.activation(self.root, self.bank, ACT.Sqrt, scale=1.0 / self.width, bias=C("eps")) \
             .then_inc(self.rooted, 1)
            if self.split:
                for k in range(self.k):
                    act.wait_ge(self.scaled, k + 1)
                    if self.shifts:
                        if k >= 2:
                            act.wait_ge(self.ready, k - 1)
                        A.activation(self.whole[:, k % 2, :], self.tmp[:, k % 2, :], ACT.Identity, bias=self.shifts[k])
                        A.activation(self.dst.hi[:, k, :], self.tmp[:, k % 2, :], ACT.Identity, bias=self.shifts[k]) \
                         .then_inc(self.high, 1)
                    else:
                        A.activation(self.dst.hi[:, k, :], self.tmp[:, k % 2, :], ACT.Copy).then_inc(self.high, 1)

        def pe(self, pe):
            if self.k > 1:
                pe.wait_ge(self.added, self.k - 1)
            else:
                pe.wait_ge(self.squares, 1)
            T.matmul(self.bank, C(self.lhs), self.acc if self.k > 1 else self.sq[:, 0, :], start=True, stop=True) \
             .then_inc(self.summed, 1)

        def dve(self, dve):
            self.add(dve)
            self.dve_finish(dve)

        def dve_finish(self, dve):
            dve.wait_ge(self.rooted, 1)
            V.reciprocal(self.rstd, self.root).then_inc(self.inverted, 1)
            dve.wait_ge(self.inverted, 1)
            for k in range(self.k + 1):
                if k < self.k:
                    if self.split and k >= 2:
                        dve.wait_ge(self.ready, k - 1)
                    V.scalar_tensor_tensor(out=self.tmp[:, k % 2, :] if self.split else self.dst[k], in0=self.src[k],
                                           scalar=self.gains[k], in1=self.rstd, op0=ALU.mult, op1=ALU.mult) \
                     .then_inc(self.scaled if self.split else self.ready, 1)
                if self.split and k >= 1:
                    dve.wait_ge(self.high, k)
                    V.tensor_tensor(self.dst.lo[:, k - 1, :], self.whole[:, (k - 1) % 2, :],
                                    self.dst.hi[:, k - 1, :].bitcast(F32), ALU.subtract).then_inc(self.ready, 1)

        def tile_wait(self, pe):
            return lambda k: pe.wait_ge(self.ready, k + 1)

    HALVES = [(0, 12), (12, 10)]
    AC = 768
    AN = 3 * D // AC

    def feed_forward(l, w_gu, w_dn, gains, shifts=None, gate_at=None, ada_half=None):
        scope = Scope()
        x = Split(scope, "x", DT)
        hid = Split(scope, "hid", max(c for _, c in HALVES))
        sp_ = scope.space(2 * 2 * S + (8 if shifts else 6) * S)
        sil, hf = sp_.get(2, S), sp_.get(2, S)
        phases, n0 = [], 0
        for t0, nt in HALVES:
            phases.append((True, t0, nt, n0, nt // 2, ITEM))
            phases.append((False, t0, nt, n0 + nt // 2, DT // 2, nt * P))
            n0 += nt // 2 + DT // 2
        sizes = [z for *_, count, z in phases for _ in range(count)]
        with Stage() as st:
            w = Weights(st, scope)
            norm = Norm(st, "norm", [h[:, k, :] for k in range(DT)], x, gains, D, sp_, ps[6][:, :], shifts=shifts)
            gate_done, silu_ready = st.sem("gate_done"), st.sem("silu_ready")
            if ada_half is not None:
                aw = scope.sb("ada_w", [P, 2, AC])
                acc = sp_.tensor[:, 4 * S:4 * S + 3 * D]
                a_landed, a_scaled, a_added, a_used, a_summed = [st.sem(n) for n in ("a_landed", "a_scaled", "a_added", "a_used",
                                                                                    "a_summed")]

                def load_ada(sp, n, first=False):
                    if not first:
                        sp.wait_ge(a_used, n)
                    sp.dma_start(aw.rearrange("p a n -> p (a n)"), t["ada"][l, n + AN * DT // 2 * ada_half, :, :]).then_inc(a_landed, 16)

                @st.block.gpsimd
                def _(pool):
                    pool.wait_ge(norm.ready, DT)
                    added = 0
                    for n in range(AN * DT // 2):
                        c, k0 = divmod(2 * n, DT)
                        a = acc[:, c * AC:(c + 1) * AC]
                        pool.wait_ge(a_landed, 16 * n + 16)
                        for e in range(2):
                            G.tensor_scalar(aw[:, e, :], aw[:, e, :], cond(k0 + e), None, ALU.mult).then_inc(a_scaled, 1)
                        for e in range(2):
                            pool.wait_ge(a_scaled, 2 * n + e + 1)
                            if n or e:
                                pool.wait_ge(a_added, 2 * n + e)
                            if k0 + e == 0:
                                ins = G.tensor_copy(a, aw[:, 0, :])
                            else:
                                ins = G.tensor_tensor(a, a, aw[:, e, :], ALU.add)
                            ins.then_inc(a_added, 1)
                        pool.wait_ge(a_added, 2 * n + 2)
                        pool.sem_inc(a_used, 1)
            hf_ready, hid_high, hid_ready, h_updated = (st.sem("hf_ready"), st.sem("hid_high"), st.sem("hid_ready"),
                                                        st.sem("h_updated"))

            @st.block.sync
            def _(sp):
                for gu, t0, nt, n0, count, size in phases:
                    def load(i, first=False):
                        for b in range(2):
                            src = w_gu[l, 2 * i + (t0 + b), :, :] if gu else w_dn[l, 2 * i + b, :, t0 * P:(t0 + nt) * P]
                            w.load(sp, b, i + n0, src, first)
                    first = 1 if n0 == 0 else 0
                    if first:
                        load(0, True)
                        if ada_half is not None:
                            load_ada(sp, 0, True)
                    last = count
                    if ada_half is not None:
                        last = min(count, AN * DT // 2 - n0)
                    with sp.Fori(first, last) as i:
                        load(i)
                        if ada_half is not None:
                            load_ada(sp, i + n0)
                    if last < count:
                        with sp.Fori(last, count) as i:
                            load(i)

            @st.block.tensor
            def _(pe):
                norm.pe(pe)
                for half, (gu, t0, nt, n0, count, size) in enumerate(phases):
                    def up(i, before=None):
                        for b in range(2):
                            w.wait(pe, b, i + n0)
                            pe.wait_ge(hid_ready, 2 * i + (t0 + b + 1))
                            wt = lambda part, a: lambda k: part[:, b, (a * DT + k) * P:(a * DT + k + 1) * P]
                            for a in range(2):
                                split_products(ps[2 * b + a][:, :], wt(w.hi, a), wt(w.lo, a), lambda k: x.hi[:, k, :],
                                               lambda k: x.lo[:, k, :], DT, before).then_inc(w.used if a else gate_done, 1)
                                before = None

                    def down(i):
                        for b in range(2):
                            w.wait(pe, b, i + n0)
                            pe.wait_ge(h_updated, 2 * i + (DT * (half // 2) + b + 1))
                            split_products(ps[4 + b][:, :], lambda k: w.hi[:, b, k * P:(k + 1) * P],
                                           lambda k: w.lo[:, b, k * P:(k + 1) * P], lambda k: hid.hi[:, k, :],
                                           lambda k: hid.lo[:, k, :], nt).then_inc(w.used, 1)

                    if gu and n0 == 0:
                        up(0, norm.tile_wait(pe))
                        with pe.Fori(1, count) as i:
                            up(i)
                    elif gu:
                        with pe.Fori(0, count) as i:
                            up(i)
                    else:
                        pe.wait_ge(hid_ready, 2 + t0 + nt)
                        with pe.Fori(0, count) as i:
                            down(i)
                if ada_half is not None:
                    pe.wait_ge(a_added, DT * AN)
                    for j in range(24):
                        mm = T.matmul(ps[7][:, j:j + 1], acc[:, j * P:(j + 1) * P], C("ones")[:, 0:1], start=True, stop=True)
                    mm.then_inc(a_summed, 1)

            @st.block.scalar
            def _(act):
                norm.square(act)
                for b in range(2):
                    w.high(act, b, 0, ITEM, True)
                norm.act_finish(act)
                A.activation(sil[:, 0, 0:1], C("one"), ACT.Silu).then_inc(st.sem("table"), 1)
                act.wait_ge(st.sem("table"), 1)
                for gu, t0, nt, n0, count, size in phases:
                    def step(i, ahead):
                        for b in range(2):
                            if gu:
                                act.wait_ge(gate_done, 2 * i + (t0 + b + 1))
                                act.wait_ge(hid_ready, 2 * i + (t0 + b + 1))
                                A.activation(sil[:, b, :], ps[2 * b][:, :], ACT.Silu).then_inc(silu_ready, 1)
                            if ahead:
                                w.high(act, b, i + (n0 + 1), ahead)
                    with act.Fori(0, count - 1) as i:
                        step(i, size)
                    step(count - 1, sizes[n0 + count] if n0 + count < len(sizes) else 0)

            @st.block.vector
            def _(dve):
                dve.sem_inc(hid_ready, 2)
                dve.sem_inc(h_updated, 2)
                norm.add(dve)
                for b in range(2):
                    w.low(dve, b, 0, ITEM)
                norm.dve_finish(dve)
                for half, (gu, t0, nt, n0, count, size) in enumerate(phases):
                    def step(i, ahead):
                        for b in range(2):
                            if gu:
                                j = 2 * i + (t0 + b)
                                at = lambda part: part[:, bass.ds(2 * i + b, 1), :].rearrange("p a s -> p (a s)")
                                dve.wait_ge(silu_ready, j + 1)
                                dve.wait_ge(w.used, 2 * i + (2 * n0 + b + 1))
                                V.tensor_tensor(hf[:, b, :], sil[:, b, :], ps[2 * b + 1][:, :], ALU.mult).then_inc(hf_ready, 1)
                                dve.wait_ge(hf_ready, j + 1)
                                V.tensor_copy(at(hid.hi), hf[:, b, :]).then_inc(hid_high, 1)
                                dve.wait_ge(hid_high, j + 1)
                                V.tensor_tensor(at(hid.lo), hf[:, b, :], at(hid.hi).bitcast(F32), ALU.subtract).then_inc(hid_ready, 1)
                                dve.wait_ge(hid_ready, j + 3)
                            else:
                                dve.wait_ge(w.used, 2 * i + (2 * n0 + b + 1))
                                hx = h[:, bass.ds(2 * i + b, 1), :].rearrange("p a s -> p (a s)")
                                V.scalar_tensor_tensor(out=hx, in0=ps[4 + b][:, :],
                                                       scalar=0.5 if gate_at is None else mod[:, 0, bass.ds(2 * i + (gate_at + b), 1)],
                                                       in1=hx, op0=ALU.mult, op1=ALU.add).then_inc(h_updated, 1)
                            if ahead:
                                w.low(dve, b, i + (n0 + 1), ahead)
                    with dve.Fori(0, count - 1) as i:
                        step(i, size)
                    step(count - 1, sizes[n0 + count] if n0 + count < len(sizes) else 0)
                if ada_half is not None:
                    dve.wait_ge(a_summed, 1)
                    V.tensor_copy(ada[:, bass.ds(l, 1), 24 * ada_half:24 * ada_half + 24].rearrange("p a c -> p (a c)"), ps[7][:, 0:24])
        scope.close()

    def load_inputs():
        scope = Scope()
        sp_ = scope.space(10 * S)
        posi = scope.sb("positions", [P, 2 * S], I32)[:, :]
        pos, turns, ang, red = sp_.get(2, S), sp_.get(S), sp_.get(S), sp_.get(S)
        shifted, over = sp_.get(S), sp_.get(S)
        lbx = sp_.get(16)
        c_hi = 6.28125
        c_mid = float(np.float32(2 * math.pi - c_hi))
        c_lo = float(2 * math.pi - c_hi - c_mid)
        magic = 1.5 * 2.0 ** 23
        top = 3.1415925
        with Stage() as st:
            landed, table_ready, reduced = st.sem("landed"), st.sem("table_ready"), st.sem("reduced")
            bounds_in, bounds_out = st.sem("bounds_in"), st.sem("bounds_out")

            @st.block.sync
            def _(sp):
                sp.dma_start(cst[:, :], t["cst"]).then_inc(landed, 16)
                sp.dma_start(parg[:, :], t["parg"]).then_inc(landed, 16)
                sp.dma_start(posi[:, 0:S], t["pos"].partition_broadcast(P)).then_inc(landed, 16)
                sp.dma_start(posi[:, S:2 * S], t["pos2"].partition_broadcast(P)).then_inc(landed, 16)
                sp.dma_start(h[:, :, :], t["x"].rearrange("(k p) s -> p k s", p=P)).then_inc(landed, 16)
                sp.wait_ge(landed, 80)

            @st.block.vector
            def _(dve):
                order = Order(dve, st.sem("dve_order"))
                dve.wait_ge(landed, 80)
                order.done(V.tensor_copy(pos.rearrange("p a s -> p (a s)"), posi))
                for r, inv in enumerate(("inv_mla", "inv_win")):
                    order.done(V.tensor_scalar(ang, pos[:, r, :], C(inv), None, ALU.mult))
                    order.done(V.tensor_scalar(turns, ang, 1.0 / (2 * math.pi), magic, ALU.mult, ALU.add))
                    order.done(V.tensor_scalar(turns, turns, magic, None, ALU.subtract))
                    order.done(V.scalar_tensor_tensor(out=red, in0=turns, scalar=-c_hi, in1=ang, op0=ALU.mult, op1=ALU.add))
                    order.done(V.scalar_tensor_tensor(out=red, in0=turns, scalar=-c_mid, in1=red, op0=ALU.mult, op1=ALU.add))
                    order.done(V.scalar_tensor_tensor(out=red, in0=turns, scalar=-c_lo, in1=red, op0=ALU.mult, op1=ALU.add))
                    order.done(V.tensor_scalar(shifted, red, math.pi / 2, None, ALU.add))
                    order.done(V.tensor_scalar(over, shifted, math.pi, -2 * math.pi, ALU.is_gt, ALU.mult))
                    order.done(V.tensor_tensor(shifted, shifted, over, ALU.add))
                    order.done(V.tensor_scalar(rope[:, 2 * r, :], shifted, top, -top, ALU.min, ALU.max))
                    V.tensor_scalar(rope[:, 2 * r + 1, :], red, top, -top, ALU.min, ALU.max).then_inc(reduced, 1)
                l0 = parg[:, cg["lb"][0]:cg["lb"][0] + 2]
                l1 = parg[:, cg["lb"][0] + 2:cg["lb"][0] + 4]
                top_ = lbx[:, 0:2]
                order.done(V.tensor_tensor(top_, l0, l1, ALU.max))
                order.done(V.tensor_tensor(lbx[:, 2:4], l0, top_, ALU.subtract))
                order.done(V.tensor_tensor(lbx[:, 4:6], l1, top_, ALU.subtract))
                V.tensor_copy(lbx[:, 12:14], lbx[:, 4:6]).then_inc(bounds_in, 1)
                dve.wait_ge(bounds_out, 1)
                order.done(V.tensor_tensor(lbx[:, 10:12], lbx[:, 6:8], lbx[:, 8:10], ALU.add))
                order.done(V.reciprocal(lbx[:, 12:14], lbx[:, 10:12]))
                V.tensor_copy(lbx[:, 14:16], lbx[:, 10:12]).then_inc(bounds_in, 1)
                order.done(V.memset(lbt[:, 0, 0, :], -BIG))
                order.done(V.memset(lbt[:, 0, 1, :], 0.0))
                order.done(V.memset(lbt[:, 0, 2, :], 1.0))
                order.done(V.tensor_tensor(lbt[:, 1, 2, :], lbx[:, 6:8], lbx[:, 12:14], ALU.mult))
                dve.wait_ge(bounds_out, 2)
                order.done(V.tensor_tensor(lbt[:, 1, 0, :], lbx[:, 4:6], lbx[:, 14:16], ALU.subtract))
                order.done(V.tensor_tensor(lbt[:, 1, 1, :], lbx[:, 2:4], lbx[:, 14:16], ALU.subtract))

            @st.block.scalar
            def _(act):
                for r in range(2):
                    act.wait_ge(reduced, r + 1)
                    for j in range(2):
                        A.activation(rope[:, 2 * r + j, :], rope[:, 2 * r + j, :], ACT.Sin).then_inc(table_ready, 1)
                at = cg["cond"][0]
                A.activation(parg[:, at:at + DT], parg[:, at:at + DT], ACT.Silu)
                act.wait_ge(bounds_in, 1)
                A.activation(lbx[:, 6:10], lbx[:, 2:6], ACT.Exp).then_inc(bounds_out, 1)
                act.wait_ge(bounds_in, 2)
                A.activation(lbx[:, 14:16], lbx[:, 14:16], ACT.Ln).then_inc(bounds_out, 1)
        scope.close()

    def load_parameters(l, name, width):
        with Stage() as st:
            @st.block.sync
            def _(sp):
                sp.dma_start(par[:, 0:width], t[name][l, :, :]).then_inc(st.sem("landed"), 16)
                sp.wait_ge(st.sem("landed"), 16)

    WORK = 24400

    def mixer1_buffers(scope):
        m = scope.space(16700)
        y = m.get(DT, S)
        cq, ckv, kr = m.get(3, S), m.get(2, S), m.get(S)
        mx = m.get(2, S + 4)
        mo = m.get(2, S)
        gi, gf = m.get(S), m.get(S)
        vz = m.get(ST, S)
        uq, ukv = m.get(3, 768), m.get(2, 1024)
        return y, cq, ckv, kr, mx, mo, gi, gf, vz, uq, ukv

    def mixer1_project(l, m):
        y, cq, ckv, kr, mx, mo, gi, gf, vz, uq, ukv = m
        scope = Scope()
        x = Split(scope, "x", DT)
        sp_ = scope.space(6 * S)
        dst = [cq[:, 0, :], cq[:, 1, :], cq[:, 2, :], ckv[:, 0, :], ckv[:, 1, :], mx[:, 0, 2:2 + S], mx[:, 1, 2:2 + S],
               mo[:, 0, :], mo[:, 1, :], kr]
        sizes = [ITEM] * 5 + [D] + [ITEM] * 2
        with Stage() as st:
            w = Weights(st, scope)
            norm = Norm(st, "norm", [h[:, k, :] for k in range(DT)], x,
                        [col(c1, "mix_norm", k) for k in range(DT)], D, sp_, ps[6][:, :])
            next_landed = st.sem("next_landed")
            done, copied = st.sem("done"), st.sem("copied")

            @st.block.sync
            def _(sp):
                for g in range(8):
                    src = t["in1_t"][l, g, :, :] if g < 5 else t["in1_g"][l, :, :] if g == 5 else t["in1_r"][l, g - 6, :, :]
                    w.load(sp, g % 2, g // 2, src, g < 2)
                    if g == 1:
                        sp.dma_start(uq.rearrange("p k m -> p (k m)"), t["uq"][l, :, :]).then_inc(next_landed, 16)
                        sp.dma_start(ukv.rearrange("p k m -> p (k m)"), t["ukv"][l, :, :]).then_inc(next_landed, 16)
                sp.wait_ge(next_landed, 32)

            @st.block.gpsimd
            def _(pool):
                G.memset(mx[:, :, 0:2], 0.0)
                G.memset(mx[:, :, S + 2:S + 4], 0.0)

            @st.block.tensor
            def _(pe):
                norm.pe(pe)
                before = norm.tile_wait(pe)
                for g in range(6):
                    b = g % 2
                    w.wait(pe, b, g // 2)
                    for a in range(2 if g < 5 else 1):
                        j = 2 * g + a
                        if j >= 4:
                            pe.wait_ge(copied, j - 3)
                        wt = lambda part: lambda k: part[:, b, (a * DT + k) * P:(a * DT + k + 1) * P]
                        split_products(ps[j % 4][:, :], wt(w.hi), wt(w.lo), lambda k: x.hi[:, k, :], lambda k: x.lo[:, k, :],
                                       DT, before).then_inc(done if a == 0 and g < 5 else w.used, 1)
                        before = None
                for g in (6, 7):
                    b = g % 2
                    w.wait(pe, b, g // 2)
                    for j in range(ST):
                        q = slice(j * P, (j + 1) * P)
                        wt = lambda part: lambda k: part[:, b, k * 256:(k + 1) * 256]
                        mm = split_products(ps[4 + j][:, (g - 6) * 256:(g - 5) * 256], lambda k: x.hi[:, k, q], lambda k: x.lo[:, k, q],
                                            wt(w.hi), wt(w.lo), DT)
                    mm.then_inc(w.used, 1)

            @st.block.scalar
            def _(act):
                norm.square(act)
                for b in range(2):
                    w.high(act, b, 0, sizes[b], True)
                norm.act_finish(act)
                for g in range(8):
                    for a in range(2):
                        j = 2 * g + a
                        if g < 5:
                            act.wait_ge(w.used if a else done, g + 1)
                            A.activation(dst[j], ps[j % 4][:, :], ACT.Copy).then_inc(copied, 1)
                    if g == 5:
                        act.wait_ge(w.used, 6)
                        bank = ps[2]
                        for rows_, bias, r in ((gi, "i_bias", 0), (gf, "f_bias", 64)):
                            A.activation(rows_[0:32, :], bank[r:r + 32, :], ACT.Identity, bias=col(c1, bias)[0:32, :])
                            A.activation(rows_[32:36, :], bank[r + 32:r + 36, ::-1], ACT.Identity, bias=col(c1, bias)[32:36, :])
                    if g + 2 < 8:
                        w.high(act, g % 2, g // 2 + 1, sizes[g + 2])
                act.wait_ge(w.used, 8)
                for j in range(ST):
                    A.activation(vz[:, j, :], ps[4 + j][:, :], ACT.Copy)

            @st.block.vector
            def _(dve):
                norm.add(dve)
                for b in range(2):
                    w.low(dve, b, 0, sizes[b])
                norm.dve_finish(dve)
                for g in range(2, 8):
                    w.low(dve, g % 2, g // 2, sizes[g])
        scope.close()

    def rotate(dve, order, x, turned, cos_sin, tmp):
        V.tensor_tensor(x, x, rope[:, cos_sin, :], ALU.mult)
        order.done(V.tensor_tensor(tmp, turned, rope[:, cos_sin + 1, :], ALU.mult))
        return V.tensor_tensor(x, x, tmp, ALU.add)

    def mixer1_attention(l, m):
        y, cq, ckv, kr, mx, mo, gi, gf, vz, uq, ukv = m
        scope = Scope()
        sp_ = scope.space(WORK)
        cqn, ckvn = sp_.get(3, S), sp_.get(2, S)
        qn, qr, kn, vn = sp_.get(H, S), sp_.get(2, S), sp_.get(H, S), sp_.get(ST, S)
        tmp = sp_.get(S)
        prob = sp_.get(2, S)
        pT = sp_.get(2, ST, S)
        top, nmax, total, inv = sp_.get(16), sp_.get(16), sp_.get(16), sp_.get(16)
        N = H * ST
        turned_src = [qr[:, 0, :], qr[:, 1, :], kr]
        with Stage() as st:
            nq = Norm(st, "nq", [cq[:, k, :] for k in range(3)], [cqn[:, k, :] for k in range(3)],
                      [col(c1, "q_norm", k) for k in range(3)], 384, sp_, ps[6][:, :])
            nk = Norm(st, "nk", [ckv[:, k, :] for k in range(2)], [ckvn[:, k, :] for k in range(2)],
                      [col(c1, "kv_norm", k) for k in range(2)], 256, sp_, ps[7][:, :])
            done, copied = st.sem("done"), st.sem("copied")
            turned, rotated = st.sem("turned"), st.sem("rotated")
            scores_ready, negmax_ready, exp_ready = st.sem("scores_ready"), st.sem("negmax_ready"), st.sem("exp_ready")
            probs_ready, pT_ready, pT_copied = st.sem("probs_ready"), st.sem("pT_ready"), st.sem("pT_copied")
            y_ready, y_copied = st.sem("y_ready"), st.sem("y_copied")

            @st.block.tensor
            def _(pe):
                nq.pe(pe)
                nk.pe(pe)
                pe.wait_ge(nq.ready, 3)
                for j in range(14):
                    if j == 6:
                        pe.wait_ge(nk.ready, 2)
                    if j >= 4:
                        pe.wait_ge(copied, j - 3)
                    bank = ps[j % 4][:, :]
                    if j < 6:
                        mm = products(bank, lambda k: uq[:, k, j * P:(j + 1) * P], lambda k: cqn[:, k, :], 3)
                    elif j < 10:
                        mm = products(bank, lambda k: ukv[:, k, (j - 6) * P:(j - 5) * P], lambda k: ckvn[:, k, :], 2)
                    else:
                        mm = products(bank, lambda k: ckvn[:, k, (j - 10) * P:(j - 9) * P], lambda k: ukv[:, k, 512:1024], 2)
                    mm.then_inc(done, 1)
                pe.wait_ge(copied, 14)
                for r in range(3):
                    T.matmul(ps[4 + r][:, :], C("rot_mla"), turned_src[r], start=True, stop=True).then_inc(turned, 1)
                pe.wait_ge(rotated, 3)
                for m in range(N + 1):
                    if m < N:
                        hd, i = divmod(m, ST)
                        q = slice(i * P, (i + 1) * P)
                        b = 64 * (hd % 2)
                        if m >= 2:
                            pe.wait_ge(exp_ready, m - 1)
                        T.matmul(ps[m % 2][:, :], qn[:, hd, q], kn[:, hd, :], start=True, stop=False)
                        T.matmul(ps[m % 2][:, :], qr[b:b + 64, hd // 2, q], kr[b:b + 64, :], start=False, stop=True) \
                         .then_inc(scores_ready, 1)
                    if m >= 1:
                        g = m - 1
                        hd, i = divmod(g, ST)
                        pe.wait_ge(probs_ready, g + 1)
                        if g >= 2:
                            pe.wait_ge(pT_copied, g - 1)
                        for k in range(ST):
                            mm = T.transpose(ps[2 + g % 2][:, k * P:(k + 1) * P], prob[:, g % 2, k * P:(k + 1) * P],
                                             C("ident"))
                        mm.then_inc(pT_ready, 1)
                        if i == ST - 1:
                            pe.wait_ge(pT_copied, g + 1)
                            if hd >= 2:
                                pe.wait_ge(y_copied, hd - 1)
                            products(ps[4 + hd % 2][:, :], lambda k: vn[:, k, hd * P:(hd + 1) * P],
                                     lambda k: pT[:, hd % 2, k, :], ST).then_inc(y_ready, 1)

            @st.block.scalar
            def _(act):
                nq.act(act)
                nk.act(act)
                for j in range(14):
                    act.wait_ge(done, j + 1)
                    dst = (qn[:, j, :] if j < 4 else qr[:, j - 4, :] if j < 6 else kn[:, j - 6, :] if j < 10
                           else vn[:, j - 10, :])
                    A.activation(dst, ps[j % 4][:, :], ACT.Copy).then_inc(copied, 1)
                for m in range(N):
                    act.wait_ge(negmax_ready, m + 1)
                    if m >= 2:
                        act.wait_ge(pT_ready, m - 1)
                    A.activation(prob[:, m % 2, :], ps[m % 2][:, :], ACT.Exp, scale=MLA_SCALE,
                                 bias=nmax[:, m:m + 1], accum_out=total[:, m:m + 1]).then_inc(exp_ready, 1)
                    if m % ST == 1 and m >= ST:
                        hd = m // ST - 1
                        act.wait_ge(y_ready, hd + 1)
                        A.activation(y[:, hd, :], ps[4 + hd % 2][:, :], ACT.Copy).then_inc(y_copied, 1)
                act.wait_ge(y_ready, H)
                A.activation(y[:, H - 1, :], ps[4 + (H - 1) % 2][:, :], ACT.Copy).then_inc(y_copied, 1)

            @st.block.vector
            def _(dve):
                order = Order(dve, st.sem("dve_order"))
                nq.dve(dve)
                nk.dve(dve)
                for r in range(3):
                    dve.wait_ge(turned, r + 1)
                    rotate(dve, order, turned_src[r], ps[4 + r][:, :], 0, tmp).then_inc(rotated, 1)
                    dve.wait_ge(rotated, r + 1)
                for m in range(N + 2):
                    if m >= 2:
                        hd, i = divmod(m - 2, ST)
                        dve.wait_ge(pT_ready, m - 1)
                        if i == 0 and hd >= 2:
                            dve.wait_ge(y_ready, hd - 1)
                        V.tensor_copy(pT[:, hd % 2, :, i * P:(i + 1) * P],
                                      ps[2 + m % 2][:, :].rearrange("p (k q) -> p k q", k=ST)).then_inc(pT_copied, 1)
                    if m < N:
                        dve.wait_ge(scores_ready, m + 1)
                        order.done(V.reduce_max(top[:, m:m + 1], ps[m % 2][:, :], AX.X))
                        V.tensor_scalar(nmax[:, m:m + 1], top[:, m:m + 1], -MLA_SCALE, None, ALU.mult) \
                         .then_inc(negmax_ready, 1)
                    if 1 <= m <= N:
                        g = m - 1
                        dve.wait_ge(exp_ready, g + 1)
                        order.done(V.reciprocal(inv[:, g:g + 1], total[:, g:g + 1]))
                        V.tensor_scalar(prob[:, g % 2, :], prob[:, g % 2, :], inv[:, g:g + 1], None, ALU.mult) \
                         .then_inc(probs_ready, 1)
        scope.close()

    def mixer1_fourier(l, m):
        y, cq, ckv, kr, mx, mo, gi, gf, vz, uq, ukv = m
        scope = Scope()
        sp_ = scope.space(WORK)
        dft = sp_.get(2, ST, S)
        part = sp_.get(2, 2, S)
        spec = sp_.get(2, S)
        fw = sp_.get(2, P)
        with Stage() as st:
            landed, w_landed = st.sem("landed"), st.sem("w_landed")
            done, copied = st.sem("done"), st.sem("copied")

            @st.block.sync
            def _(sp):
                sp.dma_start(dft.rearrange("p a j s -> p (a j s)"), t["dft"]).then_inc(landed, 16)
                sp.dma_start(fw.rearrange("p a m -> p (a m)"), t["fnw"][l, :, :]).then_inc(w_landed, 16)

            @st.block.tensor
            def _(pe):
                pe.wait_ge(landed, 16)
                for j in range(4):
                    c, a = divmod(j, 2)
                    products(ps[j][:, :], lambda k: vz[:, k, 256 + c * P:256 + (c + 1) * P], lambda k: dft[:, a, k, :], ST) \
                        .then_inc(done, 1)
                for c in range(2):
                    pe.wait_ge(copied, 2 * c + 2)
                    products(ps[4 + c][:, :], lambda k: C("dft_s") if k else C("dft_c"), lambda k: part[:, c, k, :], 2) \
                        .then_inc(done, 1)
                pe.wait_ge(w_landed, 16)
                for c in range(2):
                    pe.wait_ge(copied, 5 + c)
                    T.matmul(ps[6 + c][:, :], fw[:, c, :], spec[:, c, :], start=True, stop=True).then_inc(done, 1)

            @st.block.scalar
            def _(act):
                for j in range(8):
                    act.wait_ge(done, j + 1)
                    if j < 4:
                        A.activation(part[:, j // 2, j % 2, :], ps[j][:, :], ACT.Copy).then_inc(copied, 1)
                    elif j < 6:
                        A.activation(spec[:, j - 4, :], ps[j][:, :], ACT.Copy).then_inc(copied, 1)
                    else:
                        A.activation(y[:, j, :], ps[j][:, :], ACT.Identity, bias=col(c1, "fnet_b", j - 6)).then_inc(copied, 1)
        scope.close()

    def project_out(l, w_dram, y, gate=None):
        scope = Scope()
        x = Split(scope, "x", DT)
        with Stage() as st:
            w = Weights(st, scope)
            y_high, y_low, done, added = st.sem("y_high"), st.sem("y_low"), st.sem("done"), st.sem("added")

            @st.block.sync
            def _(sp):
                for g in range(4):
                    w.load(sp, g % 2, g // 2, w_dram[l, g, :, :], g < 2)

            @st.block.tensor
            def _(pe):
                before = lambda k: pe.wait_ge(y_low, k + 1)
                for g in range(4):
                    b = g % 2
                    w.wait(pe, b, g // 2)
                    for a in range(2):
                        j = 2 * g + a
                        if j >= 4:
                            pe.wait_ge(added, j - 3)
                        wt = lambda part: lambda k: part[:, b, (a * DT + k) * P:(a * DT + k + 1) * P]
                        split_products(ps[j % 4][:, :], wt(w.hi), wt(w.lo), lambda k: x.hi[:, k, :], lambda k: x.lo[:, k, :],
                                       DT, before).then_inc(w.used if a else done, 1)
                        before = None

            @st.block.scalar
            def _(act):
                for k in range(DT):
                    A.activation(x.hi[:, k, :], y[:, k, :], ACT.Copy).then_inc(y_high, 1)
                    if k < 2:
                        w.high(act, k, 0, ITEM, True)
                for g in (2, 3):
                    w.high(act, g % 2, 1, ITEM)

            @st.block.vector
            def _(dve):
                for k in range(DT):
                    dve.wait_ge(y_high, k + 1)
                    V.tensor_tensor(x.lo[:, k, :], y[:, k, :], x.hi[:, k, :].bitcast(F32), ALU.subtract).then_inc(y_low, 1)
                    if k < 2:
                        w.low(dve, k, 0, ITEM)
                for j in range(DT):
                    dve.wait_ge(w.used if j % 2 else done, j // 2 + 1)
                    V.scalar_tensor_tensor(out=h[:, j, :], in0=ps[j % 4][:, :], scalar=1.0 if gate is None else gate[j],
                                           in1=h[:, j, :], op0=ALU.mult, op1=ALU.add).then_inc(added, 1)
                    if j in (1, 3):
                        w.low(dve, j // 2, 1, ITEM)
        scope.close()

    def embed_layer(l):
        scope = Scope()
        x = Split(scope, "x", DT)
        sp_ = scope.space(4096 + 1024 + 2048 + 1024 + 10 * S)
        e = sp_.get(DT, S)
        pt = sp_.get(2, S)
        wp = sp_.get(2, D)
        sig = sp_.get(2, S)
        with Stage() as st:
            w = Weights(st, scope)
            p_landed = st.sem("p_landed")
            e_done, e_copied, done, sig_ready = st.sem("e_done"), st.sem("e_copied"), st.sem("done"), st.sem("sig_ready")
            gated, added = st.sem("gated"), st.sem("added")
            ng_ = Norm(st, "norm", [h[:, k, :] for k in range(DT)], x,
                       [col(c1, "gate_norm", k) for k in range(DT)], D, sp_, ps[6][:, :])
            ne = Norm(st, "ne", [e[:, k, :] for k in range(DT)], [e[:, k, :] for k in range(DT)],
                      [col(c1, "post_norm", k) for k in range(DT)], D, sp_, ps[7][:, :])

            @st.block.sync
            def _(sp):
                sp.dma_start(pt, t["p"][l, :, :].rearrange("(k p) s -> p k s", p=P)).then_inc(p_landed, 16)
                sp.dma_start(wp.rearrange("p k m -> p (k m)"), t["plep"][l, :, :]).then_inc(p_landed, 16)
                for g in range(4):
                    w.load(sp, g % 2, g // 2, t["pleg"][l, g, :, :], g < 2)

            @st.block.tensor
            def _(pe):
                ng_.pe(pe)
                pe.wait_ge(p_landed, 32)
                for j in range(DT):
                    if j >= 4:
                        pe.wait_ge(e_copied, j - 3)
                    products(ps[j % 4][:, :], lambda k: wp[:, k, j * P:(j + 1) * P], lambda k: pt[:, k, :], 2).then_inc(e_done, 1)
                pe.wait_ge(e_copied, DT)
                ne.pe(pe)
                before = ng_.tile_wait(pe)
                for g in range(4):
                    b = g % 2
                    w.wait(pe, b, g // 2)
                    for a in range(2):
                        j = 2 * g + a
                        if j >= 4:
                            pe.wait_ge(sig_ready, j - 3)
                        wt = lambda part: lambda k: part[:, b, (a * DT + k) * P:(a * DT + k + 1) * P]
                        split_products(ps[j % 4][:, :], wt(w.hi), wt(w.lo), lambda k: x.hi[:, k, :], lambda k: x.lo[:, k, :],
                                       DT, before).then_inc(w.used if a else done, 1)
                        before = None

            @st.block.scalar
            def _(act):
                ng_.square(act)
                for b in range(2):
                    w.high(act, b, 0, ITEM, True)
                ng_.act_finish(act)
                for j in range(DT):
                    act.wait_ge(e_done, j + 1)
                    A.activation(e[:, j, :], ps[j % 4][:, :], ACT.Copy).then_inc(e_copied, 1)
                act.wait_ge(e_copied, DT)
                ne.act(act)
                for j in range(DT):
                    act.wait_ge(w.used if j % 2 else done, j // 2 + 1)
                    if j >= 2:
                        act.wait_ge(gated, j - 1)
                    A.activation(sig[:, j % 2, :], ps[j % 4][:, :], ACT.Sigmoid).then_inc(sig_ready, 1)
                    if j in (1, 3):
                        w.high(act, j // 2, 1, ITEM)

            @st.block.vector
            def _(dve):
                ng_.add(dve)
                for b in range(2):
                    w.low(dve, b, 0, ITEM)
                ng_.dve_finish(dve)
                ne.dve(dve)
                dve.wait_ge(ne.ready, DT)
                for j in range(DT):
                    dve.wait_ge(sig_ready, j + 1)
                    V.tensor_tensor(e[:, j, :], e[:, j, :], sig[:, j % 2, :], ALU.mult).then_inc(gated, 1)
                    dve.wait_ge(gated, j + 1)
                    V.tensor_tensor(h[:, j, :], h[:, j, :], e[:, j, :], ALU.add).then_inc(added, 1)
                    if j in (1, 3):
                        w.low(dve, j // 2, 1, ITEM)
        scope.close()

    def final_norm():
        scope = Scope()
        sp_ = scope.space(4 * S)
        with Stage() as st:
            norm = Norm(st, "norm", [h[:, k, :] for k in range(DT)], [h[:, k, :] for k in range(DT)],
                        [col(cg, "final_norm", k) for k in range(DT)], D, sp_, ps[6][:, :])
            st.block.tensor(norm.pe)
            st.block.scalar(norm.act)
            st.block.vector(norm.dve)
        scope.close()

    def mixer1_mlstm(l, m):
        y, cq, ckv, kr, mx, mo, gi, gf, vz, uq, ukv = m
        scope = Scope()
        sp_ = scope.space(WORK)
        conv = sp_.get(2, S)
        xc = sp_.get(2, S)
        qk = sp_.get(2, 2, S)
        ws = sp_.get(2, 2, P)
        absf, soft, lf, F, a, M = [sp_.get(S) for _ in range(6)]
        rows_a, rows_m, rows_t = sp_.get(S), sp_.get(S), sp_.get(S)
        acol = sp_.get(ST, 36)
        finish = sp_.copy()
        qks = sp_.get(2, ST, S)
        wgt = sp_.get(4, S)
        thr = sp_.get(S)
        den, hdir = sp_.get(S), sp_.get(S)
        hsum = sp_.get(2, S)
        outn, sig = sp_.get(2, S), sp_.get(2, S)
        groups = [(p, d, e) for p in range(2) for d in range(2) for e in range(2)]
        steps = [(g, j) for g in range(8) for j in (range(ST) if groups[g][1] == 0 else range(ST - 1, -1, -1))]

        def head(a_, p, e, cols):
            return qk[64 * e:64 * e + 64, a_, p, cols]

        def span(g, j):
            return slice(j * P, S) if groups[g][1] == 0 else slice(0, (j + 1) * P)

        with Stage() as st:
            landed = st.sem("landed")
            conv_ready, xc_ready = st.sem("conv_ready"), st.sem("xc_ready")
            gate_in, gate_out = st.sem("gate_in"), st.sem("gate_out")
            rows_ready, cols_done, cols_ready = st.sem("rows_ready"), st.sem("cols_done"), st.sem("cols_ready")
            maps_done, maps_copied = st.sem("maps_done"), st.sem("maps_copied")
            qk_done, qk_copied = st.sem("qk_done"), st.sem("qk_copied")
            m_spread, arg_ready, exp_ready, wgt_ready = (st.sem("m_spread"), st.sem("arg_ready"), st.sem("exp_ready"),
                                                         st.sem("wgt_ready"))
            used, t_spread, thr_ready, dir_ready = st.sem("used"), st.sem("t_spread"), st.sem("thr_ready"), st.sem("dir_ready")
            zeroed = st.sem("zeroed")

            @st.block.sync
            def _(sp):
                sp.dma_start(ws.rearrange("p a b m -> p (a b m)"), t["mqk"][l, :, :]).then_inc(landed, 16)

            @st.block.tensor
            def _(pe):
                pe.wait_ge(landed, 16)
                for j in range(4):
                    a_, p = divmod(j, 2)
                    pe.wait_ge(xc_ready, p + 1)
                    T.matmul(ps[j][:, :], ws[:, a_, p, :], xc[:, p, :], start=True, stop=True).then_inc(maps_done, 1)
                pe.wait_ge(rows_ready, 1)
                for j in range(ST):
                    mm = T.transpose(ps[7][:, 36 * j:36 * j + 36], rows_a[0:36, j * P:(j + 1) * P], C("ident")[0:36, 0:36])
                mm.then_inc(cols_done, 1)
                pe.wait_ge(maps_copied, 4)
                pe.wait_ge(rows_ready, 3)
                for s_, (g, j) in enumerate(steps):
                    p, d, e = groups[g]
                    b = 64 * e
                    first = s_ % ST == 0
                    if first and d == 0 and e == 0:
                        for m in range(8):
                            hh, jj = divmod(m, ST)
                            mj = 8 * p + m
                            if p and m == 0:
                                pe.wait_ge(wgt_ready, 16)
                            if mj >= 2:
                                pe.wait_ge(qk_copied, mj - 1)
                            T.matmul(ps[m % 2][:, :], head(1, p, hh, slice(jj * P, (jj + 1) * P)), head(0, p, hh, slice(0, S)),
                                     start=True, stop=True).then_inc(qk_done, 1)
                    if first:
                        for g_ in ([0, 1] if g == 0 else [g + 1] if g < 7 else []):
                            p_, d_, e_ = groups[g_]
                            if g_ >= 2:
                                pe.wait_ge(arg_ready, ST * (g_ - 1))
                            c_ = 4 * d_ + 2 * p_ + e_
                            T.matmul(ps[2 + g_ % 2][:, :], C("sel", 36, c_ * P, (c_ + 1) * P), rows_m[0:36, :],
                                     start=True, stop=True).then_inc(m_spread, 1)
                        if e == 0:
                            if g == 0:
                                pe.wait_ge(cols_ready, 1)
                            else:
                                pe.wait_ge(dir_ready, g // 2)
                            T.matmul(ps[7][:, :], C("selp", 36, (2 * d + p) * P, (2 * d + p + 1) * P), rows_t[0:36, :],
                                     start=True, stop=True).then_inc(t_spread, 1)
                    pe.wait_ge(wgt_ready, s_ + 1)
                    r = span(g, j)
                    hd = 2 * p + e
                    T.matmul(ps[5][b:b + 64, r], vz[:, j, hd * HD:(hd + 1) * HD], wgt[:, s_ % 4, r], start=first,
                             stop=(s_ % ST == ST - 1))
                    T.matmul(ps[6][b:b + 64, r], C("ones")[:, 0:HD], wgt[:, s_ % 4, r], start=first,
                             stop=(s_ % ST == ST - 1)).then_inc(used, 1)

            @st.block.scalar
            def _(act):
                for c in range(2):
                    act.wait_ge(conv_ready, c + 1)
                    A.activation(xc[:, c, :], conv[:, c, :], ACT.Silu, bias=col(c1, "conv_b", c)).then_inc(xc_ready, 1)
                act.wait_ge(gate_in, 1)
                A.activation(soft[0:36, :], absf[0:36, :], ACT.Exp, scale=-1.0).then_inc(gate_out, 1)
                act.wait_ge(gate_out, 1)
                A.activation(soft[0:36, :], soft[0:36, :], ACT.Ln, bias=C("one", 36)).then_inc(gate_out, 1)
                for j in range(4):
                    act.wait_ge(maps_done, j + 1)
                    A.activation(qk[:, j // 2, j % 2, :], ps[j][:, :], ACT.Copy, scale=HD ** -0.5 if j < 2 else 1.0) \
                     .then_inc(maps_copied, 1)
                act.wait_ge(gate_in, 2)
                A.activation(M[0:36, :], M[0:36, :], ACT.Exp, scale=-1.0).then_inc(gate_out, 1)
                act.wait_ge(cols_done, 1)
                A.activation(acol.rearrange("p j c -> p (j c)"), ps[7][:, 0:144], ACT.Copy).then_inc(cols_ready, 1)
                for s_, (g, j) in enumerate(steps):
                    p, d, e = groups[g]
                    first = s_ % ST == 0
                    if first and d == 0 and e == 0:
                        for m in range(8):
                            act.wait_ge(qk_done, 8 * p + m + 1)
                            A.activation(qks[:, m // ST, m % ST, :], ps[m % 2][:, :], ACT.Copy).then_inc(qk_copied, 1)
                    if first and e == 0:
                        act.wait_ge(t_spread, g // 2 + 1)
                        if g:
                            act.wait_ge(dir_ready, g // 2)
                        A.activation(thr, ps[7][:, :], ACT.Copy).then_inc(thr_ready, 1)
                    act.wait_ge(arg_ready, s_ + 1)
                    A.activation(wgt[:, s_ % 4, span(g, j)], wgt[:, s_ % 4, span(g, j)], ACT.Exp).then_inc(exp_ready, 1)

            @st.block.vector
            def _(dve):
                order = Order(dve, st.sem("dve_order"))
                for c in range(2):
                    w_ = lambda k: col(c1, "conv_w", 5 * c + k)
                    order.done(V.tensor_scalar(conv[:, c, :], mx[:, c, 0:S], w_(0), None, ALU.mult))
                    for k in range(1, 5):
                        ins = V.scalar_tensor_tensor(out=conv[:, c, :], in0=mx[:, c, k:k + S], scalar=w_(k),
                                                     in1=conv[:, c, :], op0=ALU.mult, op1=ALU.add)
                        if k < 4:
                            order.done(ins)
                    ins.then_inc(conv_ready, 1)
                R = slice(0, 36)
                V.scalar_tensor_tensor(out=absf[R, :], in0=gf[R, :], scalar=-1.0, in1=gf[R, :], op0=ALU.mult, op1=ALU.max).then_inc(gate_in, 1)
                dve.wait_ge(gate_out, 2)
                order.done(V.scalar_tensor_tensor(out=lf[R, :], in0=gf[R, :], scalar=0.0, in1=soft[R, :], op0=ALU.min, op1=ALU.subtract))
                order.done(V.memset(absf[R, :], 1.0))
                order.done(V.tensor_tensor_scan(F[R, :], absf[R, :], lf[R, :], 0.0, ALU.mult, ALU.add))
                order.done(V.tensor_tensor(a[R, :], gi[R, :], F[R, :], ALU.subtract))
                order.done(V.tensor_tensor_scan(lf[R, :], absf[R, :], a[R, :], 0.0, ALU.mult, ALU.max))
                V.tensor_tensor(M[R, :], F[R, :], lf[R, :], ALU.add).then_inc(gate_in, 1)
                dve.wait_ge(gate_in, 2)
                order.done(V.tensor_scalar(F[R, :], lf[R, :], -1.0, None, ALU.mult))
                for m, (dst, src) in enumerate(((rows_a, a), (rows_m, F), (rows_t, M))):
                    if m == 2:
                        dve.wait_ge(gate_out, 3)
                    V.tensor_copy(dst[0:32, :], src[0:32, :]).then_inc(zeroed, 1)
                    dve.wait_ge(zeroed, m + 1)
                    V.tensor_copy(dst[32:36, :], src[32:36, ::-1]).then_inc(rows_ready, 1)
                dve.wait_ge(cols_ready, 1)
                for s_ in range(len(steps) + 1):
                    if s_ < len(steps):
                        g, j = steps[s_]
                        p, d, e = groups[g]
                        r = span(g, j)
                        if s_ % ST == 0:
                            dve.wait_ge(m_spread, g + 1)
                        if s_ >= 4:
                            dve.wait_ge(used, s_ - 3)
                        rc = 32 * d + 2 * p + e
                        V.tensor_scalar(wgt[:, s_ % 4, r], ps[2 + g % 2][:, r], acol[:, j, rc:rc + 1], 0.0, ALU.add, ALU.min) \
                         .then_inc(arg_ready, 1)
                    if s_ >= 1:
                        g, j = steps[s_ - 1]
                        p, d, e = groups[g]
                        r = span(g, j)
                        dve.wait_ge(exp_ready, s_)
                        if (s_ - 1) % 16 == 0:
                            dve.wait_ge(qk_copied, 8 * p + 8)
                        wx = wgt[:, (s_ - 1) % 4, :]
                        order.done(V.tensor_tensor(wx[:, r], wx[:, r], qks[:, e, j, r], ALU.mult))
                        dg = slice(j * P, (j + 1) * P)
                        V.tensor_tensor(wx[:, dg], wx[:, dg], C("upto") if d == 0 else C("from"), ALU.mult) \
                         .then_inc(wgt_ready, 1)
                        if s_ % (2 * ST) == 0:
                            gd = s_ // (2 * ST)
                            dve.wait_ge(used, s_)
                            dve.wait_ge(thr_ready, gd)
                            order.done(V.scalar_tensor_tensor(out=den, in0=ps[6][:, :], scalar=-1.0, in1=thr,
                                                              op0=ALU.mult, op1=ALU.max))
                            order.done(V.tensor_tensor(den, ps[6][:, :], den, ALU.max))
                            order.done(V.reciprocal(den, den))
                            if d == 0:
                                V.tensor_tensor(hsum[:, p, :], ps[5][:, :], den, ALU.mult).then_inc(dir_ready, 1)
                                dve.wait_ge(dir_ready, gd)
                            else:
                                order.done(V.tensor_tensor(hdir, ps[5][:, :], den, ALU.mult))
                                V.tensor_tensor(hsum[:, p, :], hsum[:, p, :], hdir, ALU.add).then_inc(dir_ready, 1)
                                dve.wait_ge(dir_ready, gd)

        with Stage() as st:
            norms = [Norm(st, f"nh{p}", [hsum[:, p, :]], [outn[:, p, :]], [col(c1, "head_norm", p)], HD, finish, ps[p][:, :],
                          lhs="heads") for p in range(2)]
            sig_ready, skipped = st.sem("sig_ready"), st.sem("skipped")

            @st.block.tensor
            def _(pe):
                for x in norms:
                    x.pe(pe)

            @st.block.scalar
            def _(act):
                for x in norms:
                    x.act(act)
                A.activation(sig.rearrange("p a s -> p (a s)"), mo.rearrange("p a s -> p (a s)"), ACT.Sigmoid).then_inc(sig_ready, 1)

            @st.block.vector
            def _(dve):
                for p, x in enumerate(norms):
                    x.dve(dve)
                for p, x in enumerate(norms):
                    dve.wait_ge(x.ready, 1)
                    V.scalar_tensor_tensor(out=outn[:, p, :], in0=xc[:, p, :], scalar=col(c1, "skip", p), in1=outn[:, p, :],
                                           op0=ALU.mult, op1=ALU.add).then_inc(skipped, 1)
                dve.wait_ge(sig_ready, 1)
                dve.wait_ge(skipped, 2)
                V.tensor_tensor(y[:, 4:6, :].rearrange("p a s -> p (a s)"), outn.rearrange("p a s -> p (a s)"),
                                sig.rearrange("p a s -> p (a s)"), ALU.mult)
        scope.close()

    modc = mod[:, 0, :]
    gain_m, gain_f = mod[:, 1, 0:8], mod[:, 1, 8:16]
    lbc = mod[:, 1, 16:22]

    def adaptive(l):
        with Stage() as st:
            p_landed = st.sem("p_landed")

            @st.block.sync
            def _(sp):
                sp.dma_start(par[:, 0:n2], t["par2"][l, :, :]).then_inc(p_landed, 16)

            @st.block.vector
            def _(dve):
                order = Order(dve, st.sem("dve_order"))
                order.done(V.tensor_copy(lbc, lbt[:, bass.ds(l, 1), :, :].rearrange("p a b c -> p (a b c)")))
                dve.wait_ge(p_landed, 16)
                ab = c2["ada_b"][0]
                order.done(V.tensor_tensor(modc, ada[:, bass.ds(l, 1), :].rearrange("p a c -> p (a c)"), par[:, ab:ab + 48], ALU.add))
                for dst, name, at in ((gain_m, "norm_mix", 8), (gain_f, "norm_ffn", 32)):
                    g0 = c2[name][0]
                    order.done(V.scalar_tensor_tensor(out=dst, in0=modc[:, at:at + 8], scalar=1.0, in1=par[:, g0:g0 + 8],
                                                      op0=ALU.add, op1=ALU.mult))

    def mixer2_buffers(scope):
        m = scope.space(16700)
        y = m.get(DT, S)
        aq = m.get(4, S)
        ak = m.get(P + S)
        bq, bf, bg = m.get(2, S), m.get(2, S), m.get(2, S)
        cx = m.get(6, S + 3)
        cgt = m.get(2, S)
        cb, ca = m.get(S), m.get(S)
        vn = m.get(ST, 384)
        return y, aq, ak, bq, bf, bg, cx, cgt, cb, ca, vn

    def mixer2_project(l, m):
        y, aq, ak, bq, bf, bg, cx, cgt, cb, ca, vn = m
        scope = Scope()
        x = Split(scope, "x", DT)
        sp_ = scope.space(8 * S)
        dst = ([aq[:, k, :] for k in range(4)] + [ak[:, P:P + S]] + [bq[:, k, :] for k in range(2)]
               + [bf[:, k, :] for k in range(2)] + [bg[:, k, :] for k in range(2)]
               + [cx[:, k, 3:3 + S] for k in range(6)] + [cgt[:, k, :] for k in range(2)])
        sizes = [ITEM] * 10 + [DT * 192] * 2
        with Stage() as st:
            w = Weights(st, scope)
            norm = Norm(st, "norm", [h[:, k, :] for k in range(DT)], x,
                        [gain_m[:, k:k + 1] for k in range(DT)], D, sp_, ps[6][:, :],
                        shifts=[modc[:, k:k + 1] for k in range(DT)])
            done, copied = st.sem("done"), st.sem("copied")

            @st.block.sync
            def _(sp):
                for g in range(12):
                    w.load(sp, g % 2, g // 2, t["in2_t"][l, g, :, :] if g < 10 else t["in2_r"][l, g - 10, :, :], g < 2)

            @st.block.gpsimd
            def _(pool):
                G.memset(ak[:, 0:P], 0.0)
                G.memset(cx[:, :, 0:3], 0.0)

            @st.block.tensor
            def _(pe):
                norm.pe(pe)
                before = norm.tile_wait(pe)
                for g in range(10):
                    b = g % 2
                    w.wait(pe, b, g // 2)
                    for a in range(2):
                        j = 2 * g + a
                        if j >= 4:
                            pe.wait_ge(copied, j - 3)
                        wt = lambda part: lambda k: part[:, b, (a * DT + k) * P:(a * DT + k + 1) * P]
                        split_products(ps[j % 4][:, :], wt(w.hi), wt(w.lo), lambda k: x.hi[:, k, :], lambda k: x.lo[:, k, :],
                                       DT, before).then_inc(w.used if a else done, 1)
                        before = None
                for g in (10, 11):
                    b = g % 2
                    w.wait(pe, b, g // 2)
                    for j in range(ST):
                        q = slice(j * P, (j + 1) * P)
                        wt = lambda part: lambda k: part[:, b, k * 192:(k + 1) * 192]
                        mm = split_products(ps[4 + j][:, (g - 10) * 192:(g - 9) * 192], lambda k: x.hi[:, k, q],
                                            lambda k: x.lo[:, k, q], wt(w.hi), wt(w.lo), DT)
                    mm.then_inc(w.used, 1)

            @st.block.scalar
            def _(act):
                norm.square(act)
                for b in range(2):
                    w.high(act, b, 0, sizes[b], True)
                norm.act_finish(act)
                for g in range(12):
                    for a in range(2 if g < 10 else 0):
                        j = 2 * g + a
                        act.wait_ge(w.used if a else done, g + 1)
                        bank = ps[j % 4]
                        if j < 19:
                            A.activation(dst[j], bank[:, :], ACT.Copy).then_inc(copied, 1)
                        else:
                            A.activation(cb[0:4, :], bank[0:4, :], ACT.Copy)
                            A.activation(ca[0:4, :], bank[32:36, :], ACT.Copy).then_inc(copied, 1)
                    if g + 2 < 12:
                        w.high(act, g % 2, g // 2 + 1, sizes[g + 2])
                act.wait_ge(w.used, 12)
                for j in range(ST):
                    A.activation(vn[:, j, :], ps[4 + j][:, 0:384], ACT.Copy)

            @st.block.vector
            def _(dve):
                norm.add(dve)
                for b in range(2):
                    w.low(dve, b, 0, sizes[b])
                norm.dve_finish(dve)
                for g in range(2, 12):
                    w.low(dve, g % 2, g // 2, sizes[g])
        scope.close()

    def mixer2_window(l, m):
        y, aq, ak, bq, bf, bg, cx, cgt, cb, ca, vn = m
        scope = Scope()
        sp_ = scope.space(WORK)
        tmp = sp_.get(S)
        sc = sp_.get(2, ST, 2 * P)
        pT = sp_.get(2, ST, 2, P)
        top, nmax, total, esink, inv = [sp_.get(8, ST) for _ in range(5)]
        heads = [(j, f) for j in range(4) for f in range(2)]
        x = [aq[:, j, :] for j in range(4)] + [ak[:, P:P + S]]
        with Stage() as st:
            norms = [Norm(st, f"n{r}", [x[r]], [x[r]], [col(c2, "q_norm" if r < 4 else "k_norm")], HD, sp_, ps[r][:, :],
                          lhs="heads") for r in range(5)]
            turned, rotated = st.sem("turned"), st.sem("rotated")
            scores_ready, negmax_ready, exp_ready = st.sem("scores_ready"), st.sem("negmax_ready"), st.sem("exp_ready")
            masked, probs_ready = st.sem("masked"), st.sem("probs_ready")
            pT_ready, pT_copied, y_ready, y_copied = (st.sem("pT_ready"), st.sem("pT_copied"), st.sem("y_ready"),
                                                      st.sem("y_copied"))

            @st.block.tensor
            def _(pe):
                for r in range(5):
                    norms[r].pe(pe)
                for r in range(5):
                    pe.wait_ge(norms[r].ready, 1)
                    if r >= 3:
                        pe.wait_ge(rotated, r - 2)
                    T.matmul(ps[5 + r % 3][:, :], C("rot_win"), x[r], start=True, stop=True).then_inc(turned, 1)
                pe.wait_ge(rotated, 5)
                for m in range(10):
                    if m < 8:
                        j, f = heads[m]
                        b = 64 * f
                        if m >= 2:
                            pe.wait_ge(masked, 2 * m - 2)
                        for q in range(ST):
                            mm = T.matmul(ps[2 * (m % 2) + q // 2][:, (q % 2) * 256:(q % 2) * 256 + 256],
                                          aq[b:b + 64, j, q * P:(q + 1) * P], ak[b:b + 64, q * P:(q + 2) * P],
                                          start=True, stop=True)
                        mm.then_inc(scores_ready, 1)
                    if 1 <= m <= 8:
                        g = m - 1
                        pe.wait_ge(probs_ready, ST * m)
                        if g:
                            pe.wait_ge(pT_copied, 2 * g)
                        for q in range(ST):
                            for a in range(2):
                                mm = T.transpose(ps[4 + q // 2][:, (q % 2) * 256 + a * P:(q % 2) * 256 + (a + 1) * P],
                                                 sc[:, g % 2, q, a * P:(a + 1) * P], C("ident"))
                        mm.then_inc(pT_ready, 1)
                    if m >= 2:
                        g = m - 2
                        j, f = heads[g]
                        b = 64 * f
                        pe.wait_ge(pT_copied, 2 * g + 2)
                        if g >= 2:
                            pe.wait_ge(y_copied, g - 1)
                        for q in range(ST):
                            for a in range(0 if q else 1, 2):
                                mm = T.matmul(ps[6 + g % 2][b:b + 64, q * P:(q + 1) * P],
                                              vn[:, q - 1 + a, f * HD:(f + 1) * HD], pT[:, g % 2, q, a, :],
                                              start=(a == 0 or q == 0), stop=(a == 1))
                        mm.then_inc(y_ready, 1)

            @st.block.scalar
            def _(act):
                for r in range(5):
                    norms[r].act(act)
                sk = c2["sinks"][0]
                for m in range(10):
                    if m < 8:
                        act.wait_ge(negmax_ready, m + 1)
                        for q in range(ST):
                            A.activation(sc[:, m % 2, q, :], sc[:, m % 2, q, :], ACT.Exp, bias=nmax[:, m, q:q + 1],
                                         accum_out=total[:, m, q:q + 1])
                        A.activation(esink[:, m, :], nmax[:, m, :], ACT.Exp, bias=par[:, sk + m:sk + m + 1]) \
                         .then_inc(exp_ready, 1)
                    if 1 <= m <= 8:
                        g = m - 1
                        act.wait_ge(pT_ready, m)
                        if g >= 2:
                            act.wait_ge(y_ready, g - 1)
                        for a in range(2):
                            A.activation(pT[:, g % 2, 2 * a:2 * a + 2, :, :].rearrange("p q a k -> p (q a k)"),
                                         ps[4 + a][:, :], ACT.Copy).then_inc(pT_copied, 1)
                    if m >= 2:
                        g = m - 2
                        j, f = heads[g]
                        act.wait_ge(y_ready, g + 1)
                        A.activation(y[64 * f:64 * f + 64, j, :], ps[6 + g % 2][64 * f:64 * f + 64, :], ACT.Copy) \
                         .then_inc(y_copied, 1)

            @st.block.vector
            def _(dve):
                order = Order(dve, st.sem("dve_order"))
                for r in range(5):
                    norms[r].dve(dve)
                for r in range(5):
                    dve.wait_ge(turned, r + 1)
                    rotate(dve, order, x[r], ps[5 + r % 3][:, :], 2, tmp).then_inc(rotated, 1)
                    dve.wait_ge(rotated, r + 1)
                sk = c2["sinks"][0]
                for m in range(9):
                    if m < 8:
                        dve.wait_ge(scores_ready, m + 1)
                        if m >= 2:
                            dve.wait_ge(pT_ready, m - 1)
                        for a in range(2):
                            V.scalar_tensor_tensor(out=sc[:, m % 2, 2 * a:2 * a + 2, :].rearrange("p q k -> p (q k)"),
                                                   in0=ps[2 * (m % 2) + a][:, :], scalar=HD ** -0.5,
                                                   in1=C("window", None, 256 * a, 256 * a + 512),
                                                   op0=ALU.mult, op1=ALU.add).then_inc(masked, 1)
                        dve.wait_ge(masked, 2 * m + 2)
                        order.done(V.reduce_max(top[:, m, :], sc[:, m % 2, :, :], AX.X))
                        V.tensor_scalar(nmax[:, m, :], top[:, m, :], par[:, sk + m:sk + m + 1], -1.0, ALU.max, ALU.mult) \
                         .then_inc(negmax_ready, 1)
                    if m >= 1:
                        g = m - 1
                        dve.wait_ge(exp_ready, m)
                        order.done(V.tensor_tensor(inv[:, g, :], total[:, g, :], esink[:, g, :], ALU.add))
                        order.done(V.reciprocal(inv[:, g, :], inv[:, g, :]))
                        for q in range(ST):
                            V.tensor_scalar(sc[:, g % 2, q, :], sc[:, g % 2, q, :], inv[:, g, q:q + 1], None, ALU.mult) \
                             .then_inc(probs_ready, 1)
        scope.close()

    def head_output(st, sp_, tag, src, gain, gate, y, y_at, tmp):
        norms = [Norm(st, f"{tag}{c}", [src[:, c, :]], [src[:, c, :]], [gain], HD, sp_, ps[c][:, :], lhs="heads")
                 for c in range(2)]
        gate_ready = st.sem(tag + "_gate")

        def pe_(pe):
            for x in norms:
                x.pe(pe)

        def act_(act):
            for x in norms:
                x.act(act)
            A.activation(tmp, gate, ACT.Silu).then_inc(gate_ready, 1)

        def dve_(dve):
            for x in norms:
                x.dve(dve)
            dve.wait_ge(gate_ready, 1)
            for c, x in enumerate(norms):
                dve.wait_ge(x.ready, 1)
                V.tensor_tensor(y[:, y_at + c, :], src[:, c, :], tmp[:, c, :], ALU.mult)

        return pe_, act_, dve_

    def mixer2_hgrn(l, m):
        y, aq, ak, bq, bf, bg, cx, cgt, cb, ca, vn = m
        scope = Scope()
        sp_ = scope.space(WORK)
        finish = sp_.copy()
        az, sp2, B, mxv, lf, kk = [sp_.get(2, S) for _ in range(6)]
        cum = sp_.get(2, S)
        E = sp_.get(2, S)
        X = sp_.get(2, S)
        diag = sp_.get(H, ST, P)
        off = sp_.get(H, 6 * P)
        et = sp_.get(2, ST)
        qd, kd, far = sp_.get(2, S), sp_.get(2, S), sp_.get(2, 2, P)
        o = sp_.get(2, S)
        flat = lambda a: a.rearrange("p c s -> p (c s)")
        NL = len(LEVELS)
        steps = [(v, c) for v in range(NL) for c in range(2)]

        def halves(a, c, L):
            v = a[:, c, :].rearrange("p (b a k) -> p b a k", a=2, k=L)
            return v[:, :, 0, :], v[:, :, 1, :]

        with Stage() as st:
            f_in, f_out = st.sem("f_in"), st.sem("f_out")
            diff_ready, decay_ready, x_ready = st.sem("diff_ready"), st.sem("decay_ready"), st.sem("x_ready")
            own_done, own_copied = st.sem("own_done"), st.sem("own_copied")
            lev_done, lev_copied = st.sem("lev_done"), st.sem("lev_copied")
            tail_in, tail_exp, tail_ready = st.sem("tail_in"), st.sem("tail_exp"), st.sem("tail_ready")
            off_done, off_copied, o_done = st.sem("off_done"), st.sem("off_copied"), st.sem("o_done")

            @st.block.scalar
            def _(act):
                act.wait_ge(f_in, 1)
                A.activation(flat(sp2), flat(az), ACT.Exp, scale=-1.0).then_inc(f_out, 1)
                act.wait_ge(f_out, 1)
                A.activation(flat(sp2), flat(sp2), ACT.Ln, bias=C("one")).then_inc(f_out, 1)
                act.wait_ge(f_in, 2)
                A.activation(flat(az), flat(az), ACT.Exp).then_inc(f_out, 1)
                act.wait_ge(f_out, 3)
                A.activation(flat(az), flat(az), ACT.Ln, bias=C("one")).then_inc(f_out, 1)
                A.activation(flat(kk), flat(bf), ACT.Sigmoid, scale=-1.0).then_inc(f_out, 1)
                for i in range(len(steps)):
                    act.wait_ge(diff_ready, 2 * i + 2)
                    A.activation(E[:, i % 2, :], E[:, i % 2, :], ACT.Exp).then_inc(decay_ready, 1)
                act.wait_ge(tail_in, 2)
                A.activation(flat(kd), flat(kd), ACT.Exp).then_inc(tail_exp, 1)
                A.activation(flat(qd), flat(cum), ACT.Exp).then_inc(tail_exp, 1)
                A.activation(et, cum.rearrange("p c (j k) -> p c j k", k=P)[:, :, :, P - 1], ACT.Exp).then_inc(tail_exp, 1)
                for hd in range(H):
                    act.wait_ge(off_done, hd + 1)
                    b0 = 4 * (hd % 2)
                    A.activation(off[:, hd, 0:512], ps[b0][:, :], ACT.Copy).then_inc(off_copied, 1)
                    A.activation(off[:, hd, 512:768], ps[b0 + 1][:, 0:256], ACT.Copy).then_inc(off_copied, 1)
                for c in range(2):
                    act.wait_ge(o_done, c + 1)
                    A.activation(o[:, c, :], ps[2 + 4 * c][:, :], ACT.Copy)

            @st.block.vector
            def _(dve):
                order = Order(dve, st.sem("dve_order"))
                ln_lb, ln_1m, one_m = lbc[:, 0:2], lbc[:, 2:4], lbc[:, 4:6]
                V.scalar_tensor_tensor(out=flat(az), in0=flat(bf), scalar=-1.0, in1=flat(bf), op0=ALU.mult, op1=ALU.max) \
                 .then_inc(f_in, 1)
                dve.wait_ge(f_out, 2)
                order.done(V.scalar_tensor_tensor(out=flat(B), in0=flat(bf), scalar=0.0, in1=flat(sp2), op0=ALU.min, op1=ALU.subtract))
                for c in range(2):
                    order.done(V.tensor_scalar(B[:, c, :], B[:, c, :], ln_1m[:, c:c + 1], None, ALU.add))
                    order.done(V.tensor_scalar(mxv[:, c, :], B[:, c, :], ln_lb[:, c:c + 1], None, ALU.max))
                    order.done(V.scalar_tensor_tensor(out=az[:, c, :], in0=B[:, c, :], scalar=ln_lb[:, c:c + 1],
                                                      in1=mxv[:, c, :], op0=ALU.min, op1=ALU.subtract))
                V.memset(et, 0.0).then_inc(f_in, 1)
                dve.wait_ge(f_out, 4)
                order.done(V.tensor_tensor(flat(lf), flat(mxv), flat(az), ALU.add))
                for c in range(2):
                    order.done(V.tensor_tensor_scan(cum[:, c, :], C("restart"), lf[:, c, :], 0.0, ALU.mult, ALU.add))
                dve.wait_ge(f_out, 5)
                for c in range(2):
                    ins = V.tensor_scalar(kk[:, c, :], kk[:, c, :], one_m[:, c:c + 1], None, ALU.mult)
                    order.tick(ins)
                dve.wait_ge(order.sem, order.count)
                V.memset(et, 0.0).then_inc(x_ready, 1)
                for hd in range(H):
                    dve.wait_ge(own_done, hd + 1)
                    V.tensor_tensor(diag[:, hd, :, :], ps[hd][:, :].rearrange("p (j k) -> p j k", k=P),
                                    C("ident").unsqueeze(1).to_broadcast([P, ST, P]), ALU.mult).then_inc(own_copied, 1)
                dve.wait_ge(own_copied, H)
                for i in range(len(steps) + 2):
                    if i < len(steps):
                        v, c = steps[i]
                        L = LEVELS[v]
                        c0, c1_ = halves(cum, c, L)
                        e0, e1 = halves(E[:, i % 2:i % 2 + 1, :], 0, L)
                        mid = c0[:, :, L - 1:L].to_broadcast([P, S // (2 * L), L])
                        if i >= 2:
                            dve.wait_ge(x_ready, 2 * i - 1)
                        V.tensor_tensor(e0, mid, c0, ALU.subtract).then_inc(diff_ready, 1)
                        V.tensor_tensor(e1, c1_, mid, ALU.subtract).then_inc(diff_ready, 1)
                    if 1 <= i <= len(steps):
                        g = i - 1
                        v, c = steps[g]
                        L = LEVELS[v]
                        e0, e1 = halves(E[:, g % 2:g % 2 + 1, :], 0, L)
                        x0, x1 = halves(X[:, g % 2:g % 2 + 1, :], 0, L)
                        k0, _ = halves(kk, c, L)
                        _, q1 = halves(bq, c, L)
                        dve.wait_ge(decay_ready, i)
                        if g >= 2:
                            dve.wait_ge(lev_done, 2 * g - 2)
                        V.tensor_tensor(x0, e0, k0, ALU.mult).then_inc(x_ready, 1)
                        V.tensor_tensor(x1, e1, q1, ALU.mult).then_inc(x_ready, 1)
                    if i >= 2:
                        g = i - 2
                        v, c = steps[g]
                        lev = C("levels", None, v * P, (v + 1) * P).bitcast(I32)
                        for e in range(2):
                            hd = 2 * c + e
                            dve.wait_ge(lev_done, 2 * g + e + 1)
                            if v:
                                dve.wait_ge(lev_copied, 2 * (g - 2) + e + 1)
                            V.copy_predicated(diag[:, hd, :, :], lev.unsqueeze(1).to_broadcast([P, ST, P]),
                                              ps[4 + 2 * (g % 2) + e][:, :].rearrange("p (j k) -> p j k", k=P)) \
                             .then_inc(lev_copied, 1)
                for c in range(2):
                    cv = cum[:, c, :].rearrange("p (j k) -> p j k", k=P)
                    V.tensor_tensor(kd[:, c, :].rearrange("p (j k) -> p j k", k=P), cv[:, :, P - 1:P].to_broadcast([P, ST, P]),
                                    cv, ALU.subtract).then_inc(tail_in, 1)
                dve.wait_ge(tail_exp, 3)
                order.done(V.tensor_tensor(flat(kd), flat(kd), flat(kk), ALU.mult))
                order.done(V.tensor_tensor(flat(qd), flat(qd), flat(bq), ALU.mult))
                for c in range(2):
                    V.tensor_scalar(far[:, c, 0, :], kd[:, c, 0:P], et[:, c, 1:2], None, ALU.mult).then_inc(tail_ready, 1)
                    V.tensor_scalar(far[:, c, 1, :], qd[:, c, 3 * P:S], et[:, c, 2:3], None, ALU.mult).then_inc(tail_ready, 1)

            @st.block.tensor
            def _(pe):
                pe.wait_ge(x_ready, 1)
                for hd in range(H):
                    r = slice(64 * (hd % 2), 64 * (hd % 2) + 64)
                    for j in range(ST):
                        q = slice(j * P, (j + 1) * P)
                        mm = T.matmul(ps[hd][:, q], kk[r, hd // 2, q], bq[r, hd // 2, q], start=True, stop=True)
                    mm.then_inc(own_done, 1)
                for g, (v, c) in enumerate(steps):
                    pe.wait_ge(x_ready, 2 * g + 3)
                    for e in range(2):
                        if g >= 2:
                            pe.wait_ge(lev_copied, 2 * (g - 2) + e + 1)
                        r = slice(64 * e, 64 * e + 64)
                        for j in range(ST):
                            q = slice(j * P, (j + 1) * P)
                            mm = T.matmul(ps[4 + 2 * (g % 2) + e][:, q], X[r, g % 2, q], X[r, g % 2, q], start=True, stop=True)
                        mm.then_inc(lev_done, 1)
                pe.wait_ge(tail_ready, 4)
                pe.wait_ge(lev_copied, 4 * NL)
                for hd in range(H):
                    c, e = divmod(hd, 2)
                    r = slice(64 * e, 64 * e + 64)
                    b0 = 4 * (hd % 2)
                    if hd >= 2:
                        pe.wait_ge(off_copied, 2 * (hd - 2) + 2)
                    T.matmul(ps[b0][:, 0:P], kd[r, c, 0:P], qd[r, c, P:2 * P], start=True, stop=True)
                    T.matmul(ps[b0][:, P:2 * P], kd[r, c, 2 * P:3 * P], qd[r, c, 3 * P:S], start=True, stop=True)
                    for a, (lhs, bank, at) in enumerate(((far[r, c, 0, :], ps[b0], 2 * P), (kd[r, c, P:2 * P], ps[b0 + 1], 0))):
                        T.matmul(bank[:, at:at + P], lhs, qd[r, c, 2 * P:3 * P], start=True, stop=True)
                        mm = T.matmul(bank[:, at + P:at + 2 * P], lhs, far[r, c, 1, :], start=True, stop=True)
                    mm.then_inc(off_done, 1)
                for hd in range(H):
                    c, e = divmod(hd, 2)
                    pe.wait_ge(off_copied, 2 * hd + 2)
                    out = ps[2 + 4 * c][64 * e:64 * e + 64, :]
                    v_ = lambda j: vn[:, j, P + hd * HD:P + (hd + 1) * HD]
                    T.matmul(out[:, 0:P], v_(0), diag[:, hd, 0, :], start=True, stop=True)
                    T.matmul(out[:, P:2 * P], v_(0), off[:, hd, 0:P], start=True, stop=False)
                    T.matmul(out[:, P:2 * P], v_(1), diag[:, hd, 1, :], start=False, stop=True)
                    T.matmul(out[:, 2 * P:S], v_(0), off[:, hd, 2 * P:4 * P], start=True, stop=False)
                    T.matmul(out[:, 2 * P:S], v_(1), off[:, hd, 4 * P:6 * P], start=False, stop=False)
                    T.matmul(out[:, 2 * P:3 * P], v_(2), diag[:, hd, 2, :], start=False, stop=False)
                    T.matmul(out[:, 3 * P:S], v_(2), off[:, hd, P:2 * P], start=False, stop=False)
                    mm = T.matmul(out[:, 3 * P:S], v_(3), diag[:, hd, 3, :], start=False, stop=True)
                    if e:
                        mm.then_inc(o_done, 1)

        with Stage() as st:
            p_, a_, v_ = head_output(st, finish, "hg", o, col(c2, "hgrn_norm"), bg, y, 4, qd)
            st.block.tensor(p_)
            st.block.scalar(a_)
            st.block.vector(v_)
        scope.close()

    def mixer2_delta(l, m):
        y, aq, ak, bq, bf, bg, cx, cgt, cb, ca, vn = m
        scope = Scope()
        sp_ = scope.space(WORK)
        cv = sp_.get(6, S)
        early = sp_.copy()
        rowg, rowG, rs1, rs2 = [sp_.get(S) for _ in range(4)]
        rowc = sp_.get(S)
        cols = sp_.get(ST, 68)
        ecol = sp_.get(ST, 12)
        gm, Lm, tb = sp_.get(S), sp_.get(S), sp_.get(S)
        finish = sp_.copy()
        AT, qkT = sp_.get(H, ST, P), sp_.get(H, ST, P)
        Tn, Tt = sp_.get(H, ST, P), sp_.get(H, ST, P)
        low = sp_.get(2, ST, P)
        Xs = sp_.get(2, ST, P)
        nega = sp_.get(2)
        n = sp_.get(DT, S)
        kN = n[:, 0:2, :].rearrange("p a (b c) -> p (a b) c", c=256)
        vN = n[:, 2:4, :].rearrange("p a (b c) -> p (a b) c", c=256)
        kdec = n[:, 4:6, :].rearrange("p a (b c) -> p (a b) c", c=256)
        U = n[:, 6:8, :].rearrange("p a (b c) -> p (a b) c", c=256)
        qd = cx[:, 0:2, 0:S]
        WT = cx[:, 2:4, 0:S]
        eGB = cx[:, 4:6, 0:S]
        flat = lambda a: a.rearrange("p c s -> p (c s)")
        chunks = lambda a: a.rearrange("p (j k) -> p j k", k=P)

        def headcols(i):
            return ecol[:, :, 4 * i:4 * i + 4].unsqueeze(3).to_broadcast([P, ST, H, HD])

        with Stage() as st:
            conv_ready, silu_ready = st.sem("conv_ready"), st.sem("silu_ready")
            norms = [Norm(st, f"n{c}", [cv[:, c, :]], [cv[:, c, :]], [HD ** -0.5 if c < 2 else 1.0], 1.0, early,
                          ps[c][:, :], lhs="heads") for c in range(4)]
            g_in, g_out = st.sem("g_in"), st.sem("g_out")

            @st.block.tensor
            def _(pe):
                for x in norms:
                    x.pe(pe)

            @st.block.scalar
            def _(act):
                for c in range(6):
                    act.wait_ge(conv_ready, c + 1)
                    A.activation(cv[:, c, :], cv[:, c, :], ACT.Silu).then_inc(silu_ready, 1)
                act.wait_ge(silu_ready, 6)
                for x in norms:
                    x.act(act)

            @st.block.vector
            def _(dve):
                order = Order(dve, st.sem("dve_order"))
                for c in range(6):
                    w_ = lambda k: col(c2, "conv_w", 4 * c + k)
                    order.done(V.tensor_scalar(cv[:, c, :], cx[:, c, 0:S], w_(0), None, ALU.mult))
                    for k in range(1, 4):
                        ins = V.scalar_tensor_tensor(out=cv[:, c, :], in0=cx[:, c, k:k + S], scalar=w_(k), in1=cv[:, c, :],
                                                     op0=ALU.mult, op1=ALU.add)
                        if k < 3:
                            order.done(ins)
                    ins.then_inc(conv_ready, 1)
                for x in norms:
                    x.dve(dve)

        R = slice(0, 4)
        with Stage() as st:
            g_in, g_out, rows_ready = st.sem("g_in"), st.sem("g_out"), st.sem("rows_ready")
            zeroed, cols_done, cols_ready = st.sem("zeroed"), st.sem("cols_done"), st.sem("cols_ready")
            spread, scan_ready, decay_ready, head_ready = (st.sem("spread"), st.sem("scan_ready"), st.sem("decay_ready"),
                                                           st.sem("head_ready"))
            nat_done, nat_copied, eg_done, eg_ready = (st.sem("nat_done"), st.sem("nat_copied"), st.sem("eg_done"),
                                                       st.sem("eg_ready"))
            ecols_ready = st.sem("ecols_ready")

            @st.block.gpsimd
            def _(pool):
                G.memset(rowc[0:68, :], 0.0).then_inc(zeroed, 1)

            @st.block.scalar
            def _(act):
                act.wait_ge(zeroed, 1)
                A.activation(rowc[R, :], cb[R, :], ACT.Sigmoid).then_inc(g_out, 1)
                A.activation(nega[R, 0:1], col(c2, "a_log", 0, 4), ACT.Exp).then_inc(g_out, 1)
                A.activation(rowg[R, :], ca[R, :], ACT.Identity, bias=col(c2, "dt_bias", 0, 4)).then_inc(g_out, 1)
                act.wait_ge(g_in, 1)
                A.activation(rs1[R, :], rs1[R, :], ACT.Exp, scale=-1.0).then_inc(g_out, 1)
                act.wait_ge(g_out, 4)
                A.activation(rs1[R, :], rs1[R, :], ACT.Ln, bias=C("one", 4)).then_inc(g_out, 1)
                act.wait_ge(cols_done, 1)
                A.activation(cols.rearrange("p j c -> p (j c)"), ps[7][:, 0:ST * 68], ACT.Copy).then_inc(cols_ready, 1)
                act.wait_ge(cols_ready, 1)
                A.activation(ecol[:, :, 0:4], cols[:, :, 32:36], ACT.Exp).then_inc(cols_ready, 1)
                A.activation(ecol[:, :, 4:8], cols[:, :, 64:68], ACT.Exp).then_inc(cols_ready, 1)
                for c in range(2):
                    act.wait_ge(eg_done, c + 1)
                    A.activation(eGB[:, c, :], ps[4 + c][:, :], ACT.Exp).then_inc(eg_ready, 1)
                for j in range(4):
                    act.wait_ge(nat_done, j + 1)
                    A.activation((kN if j < 2 else vN)[:, 2 * (j % 2):2 * (j % 2) + 2, :].rearrange("p a c -> p (a c)"),
                                 ps[6 + j % 2][:, :], ACT.Copy).then_inc(nat_copied, 1)
                for hd in range(H):
                    act.wait_ge(scan_ready, hd + 1)
                    A.activation(Lm, gm, ACT.Exp).then_inc(decay_ready, 1)

            @st.block.tensor
            def _(pe):
                pe.wait_ge(rows_ready, 1)
                for j in range(ST):
                    mm = T.transpose(ps[7][:, 68 * j:68 * j + 68], rowc[0:68, j * P:(j + 1) * P], C("ident")[0:68, 0:68])
                mm.then_inc(cols_done, 1)
                for c in range(2):
                    T.matmul(ps[4 + c][:, :], C("selp", 4, c * P, (c + 1) * P), rowG[R, :], start=True, stop=True).then_inc(eg_done, 1)
                pe.wait_ge(cols_ready, 1)
                for j in range(4):
                    if j >= 2:
                        pe.wait_ge(nat_copied, j - 1)
                    for a in range(2):
                        for p in range(2):
                            ch = 2 * (j % 2) + a
                            mm = T.transpose(ps[6 + j % 2][:, a * 256 + p * P:a * 256 + (p + 1) * P],
                                             cv[:, 2 + 2 * (j // 2) + p, ch * P:(ch + 1) * P], C("ident"))
                    mm.then_inc(nat_done, 1)
                for hd in range(H):
                    r = slice(64 * (hd % 2), 64 * (hd % 2) + 64)
                    if hd:
                        pe.wait_ge(head_ready, 2 * hd)
                    T.matmul(ps[0][:, :], C("sel", 4, hd * P, (hd + 1) * P), rowg[R, :], start=True, stop=True)
                    T.matmul(ps[1][:, :], C("sel", 4, hd * P, (hd + 1) * P), rowc[R, :], start=True, stop=True)
                    for b, at in ((2, 2), (3, 0)):
                        for j in range(ST):
                            q = slice(j * P, (j + 1) * P)
                            mm = T.matmul(ps[b][:, q], cv[r, 2 + hd // 2, q], cv[r, at + hd // 2, q], start=True, stop=True)
                    mm.then_inc(spread, 1)

            @st.block.vector
            def _(dve):
                order = Order(dve, st.sem("dve_order"))
                dve.wait_ge(g_out, 3)
                V.scalar_tensor_tensor(out=rs1[R, :], in0=rowg[R, :], scalar=-1.0, in1=rowg[R, :], op0=ALU.mult, op1=ALU.max) \
                 .then_inc(g_in, 1)
                dve.wait_ge(g_out, 5)
                order.done(V.scalar_tensor_tensor(out=rs2[R, :], in0=rowg[R, :], scalar=0.0, in1=rs1[R, :], op0=ALU.max, op1=ALU.add))
                order.done(V.tensor_scalar(rowg[R, :], rs2[R, :], nega[R, 0:1], -1.0, ALU.mult, ALU.mult))
                order.done(V.tensor_tensor_scan(rowG[R, :], C("restart", 4), rowg[R, :], 0.0, ALU.mult, ALU.add))
                gv = chunks(rowG[R, :])
                order.done(V.tensor_copy(rowc[32:36, :], rowG[R, :]))
                V.tensor_tensor(chunks(rowc[64:68, :]), gv[:, :, P - 1:P].to_broadcast([4, ST, P]), gv, ALU.subtract) \
                 .then_inc(rows_ready, 1)
                dve.wait_ge(cols_ready, 3)
                order.done(V.tensor_tensor(ecol[:, :, 8:12], ecol[:, :, 0:4], cols[:, :, 0:4], ALU.mult))
                dve.wait_ge(eg_ready, 2)
                order.done(V.tensor_tensor(qd, cv[:, 0:2, :], eGB, ALU.mult))
                dve.wait_ge(nat_copied, 4)
                hv = lambda a: a.rearrange("p j (e c) -> p j e c", c=HD)
                order.done(V.tensor_tensor(hv(kdec), hv(kN), headcols(1), ALU.mult))
                order.done(V.tensor_tensor(hv(kN), hv(kN), headcols(2), ALU.mult))
                order.done(V.tensor_tensor(hv(vN), hv(vN), cols[:, :, 0:4].unsqueeze(3).to_broadcast([P, ST, H, HD]), ALU.mult))
                for hd in range(H):
                    dve.wait_ge(spread, hd + 1)
                    if hd:
                        dve.wait_ge(decay_ready, hd)
                    order.done(V.tensor_tensor(gm, ps[0][:, :], C("strict4"), ALU.mult))
                    V.tensor_tensor_scan(gm, C("strict4"), gm, 0.0, ALU.mult, ALU.add).then_inc(scan_ready, 1)
                    dve.wait_ge(decay_ready, hd + 1)
                    order.done(V.tensor_tensor(tb, Lm, C("strict4"), ALU.mult))
                    order.done(V.tensor_tensor(tb, tb, ps[1][:, :], ALU.mult))
                    order.done(V.tensor_tensor(chunks(Lm), chunks(Lm), C("upto").unsqueeze(1).to_broadcast([P, ST, P]), ALU.mult))
                    V.tensor_tensor(AT[:, hd, :, :].rearrange("p j k -> p (j k)"), tb, ps[2][:, :], ALU.mult).then_inc(head_ready, 1)
                    V.tensor_tensor(qkT[:, hd, :, :].rearrange("p j k -> p (j k)"), Lm, ps[3][:, :], ALU.mult).then_inc(head_ready, 1)
                    dve.wait_ge(head_ready, 2 * hd + 2)

        steps = [(v, hd) for v in range(len(LEVELS)) for hd in range(H)]
        NS = len(steps)
        with Stage() as st:
            eye_ready, low_ready, x_done, x_ready = st.sem("eye_ready"), st.sem("low_ready"), st.sem("x_done"), st.sem("x_ready")
            yz_done, updated = st.sem("yz_done"), st.sem("updated")

            @st.block.gpsimd
            def _(pool):
                for i, (v, hd) in enumerate(steps):
                    if i >= 2:
                        pool.wait_ge(x_done, i - 1)
                    G.tensor_tensor(low[:, i % 2, :, :], AT[:, hd, :, :],
                                    C("levels", None, v * P, (v + 1) * P).unsqueeze(1).to_broadcast([P, ST, P]), ALU.mult) \
                     .then_inc(low_ready, 1)

            @st.block.scalar
            def _(act):
                for i in range(NS):
                    act.wait_ge(x_done, i + 1)
                    if i >= 2:
                        act.wait_ge(yz_done, 2 * (i - 2) + 2)
                    A.activation(Xs[:, i % 2, :, :].rearrange("p j k -> p (j k)"), ps[i % 2][:, :], ACT.Copy).then_inc(x_ready, 1)

            @st.block.tensor
            def _(pe):
                pe.wait_ge(eye_ready, 2 * H)
                for i in range(NS + 1):
                    if i < NS:
                        v, hd = steps[i]
                        pe.wait_ge(low_ready, i + 1)
                        if v:
                            pe.wait_ge(updated, 2 * (i - H) + 2)
                        if i >= 2:
                            pe.wait_ge(x_ready, i - 1)
                        for j in range(ST):
                            mm = T.matmul(ps[i % 2][:, j * P:(j + 1) * P], low[:, i % 2, j, :], Tn[:, hd, j, :], start=True, stop=True)
                        mm.then_inc(x_done, 1)
                    if i >= 1:
                        g = i - 1
                        v, hd = steps[g]
                        pe.wait_ge(x_ready, g + 1)
                        if g >= 2:
                            pe.wait_ge(updated, 2 * (g - 2) + 2)
                        for j in range(ST):
                            mm = T.matmul(ps[2 + g % 2][:, j * P:(j + 1) * P], Tt[:, hd, j, :], Xs[:, g % 2, j, :], start=True, stop=True)
                        mm.then_inc(yz_done, 1)
                        for j in range(ST):
                            mm = T.matmul(ps[4 + g % 2][:, j * P:(j + 1) * P], Xs[:, g % 2, j, :], Tt[:, hd, j, :], start=True, stop=True)
                        mm.then_inc(yz_done, 1)

            @st.block.vector
            def _(dve):
                eye = C("ident").unsqueeze(1).to_broadcast([P, ST, P])
                for hd in range(H):
                    V.tensor_copy(Tn[:, hd, :, :], eye).then_inc(eye_ready, 1)
                    V.tensor_copy(Tt[:, hd, :, :], eye).then_inc(eye_ready, 1)
                dve.wait_ge(eye_ready, 2 * H)
                for i, (v, hd) in enumerate(steps):
                    if v:
                        dve.wait_ge(updated, 2 * (i - H) + 2)
                    for a, X_ in enumerate((Tn, Tt)):
                        dve.wait_ge(yz_done, 2 * i + 2)
                        f = X_[:, hd, :, :].rearrange("p j k -> p (j k)")
                        V.tensor_tensor(f, f, ps[2 + 2 * a + i % 2][:, :], ALU.subtract).then_inc(updated, 1)

        state = rowg[:, 0:2 * HD].rearrange("p (a c) -> p a c", c=HD)
        vnew = rowG[:, 0:H * HD].rearrange("p (a c) -> p a c", c=HD)
        o = low[:, 0:2, :, :].rearrange("p a j k -> p a (j k)")
        with Stage() as st:
            u_done, u_copied, w_done, w_copied = st.sem("u_done"), st.sem("u_copied"), st.sem("w_done"), st.sem("w_copied")
            zeroed, ws_done, v_ready, s_done, s_ready = (st.sem("zeroed"), st.sem("ws_done"), st.sem("v_ready"), st.sem("s_done"),
                                                         st.sem("s_ready"))
            o_done = st.sem("o_done")

            @st.block.gpsimd
            def _(pool):
                G.memset(state, 0.0).then_inc(zeroed, 1)

            @st.block.tensor
            def _(pe):
                for j in range(ST):
                    for hd in range(H):
                        mm = T.matmul(ps[j // 2][:, (j % 2) * 256 + hd * HD:(j % 2) * 256 + (hd + 1) * HD], Tt[:, hd, j, :],
                                      vN[:, j, hd * HD:(hd + 1) * HD], start=True, stop=True)
                mm.then_inc(u_done, 1)
                for hd in range(H):
                    for j in range(ST):
                        mm = T.matmul(ps[2 + hd // 2][64 * (hd % 2):64 * (hd % 2) + 64, j * P:(j + 1) * P],
                                      kN[:, j, hd * HD:(hd + 1) * HD], Tt[:, hd, j, :], start=True, stop=True)
                mm.then_inc(w_done, 1)
                pe.wait_ge(w_copied, 2)
                pe.wait_ge(u_copied, 2)
                pe.wait_ge(zeroed, 1)
                for j in range(ST):
                    q = slice(j * P, (j + 1) * P)
                    if j:
                        pe.wait_ge(s_ready, 2 * j)
                    for hd in range(H):
                        r = slice(64 * (hd % 2), 64 * (hd % 2) + 64)
                        mm = T.matmul(ps[4 * (1 - hd % 2)][:, (hd // 2) * HD:(hd // 2 + 1) * HD], WT[r, hd // 2, q], state[r, hd // 2, :],
                                      start=True, stop=True)
                        if hd >= 2:
                            mm.then_inc(ws_done, 1)
                    pe.wait_ge(v_ready, 2 * j + 2)
                    for hd in range(H):
                        r = slice(64 * (hd % 2), 64 * (hd % 2) + 64)
                        mm = T.matmul(ps[5][r, (hd // 2) * HD:(hd // 2 + 1) * HD], kdec[:, j, hd * HD:(hd + 1) * HD], vnew[:, hd, :],
                                      start=True, stop=True)
                    for hd in range(H):
                        r = slice(64 * (hd % 2), 64 * (hd % 2) + 64)
                        out = ps[6 + hd // 2][r, q]
                        T.matmul(out, state[r, hd // 2, :], qd[r, hd // 2, q], start=True, stop=False)
                        mm = T.matmul(out, vnew[:, hd, :], qkT[:, hd, j, :], start=False, stop=True)
                    mm.then_inc(s_done, 1)

            @st.block.scalar
            def _(act):
                act.wait_ge(u_done, 1)
                for a in range(2):
                    A.activation(U[:, 2 * a:2 * a + 2, :].rearrange("p a c -> p (a c)"), ps[a][:, :], ACT.Copy).then_inc(u_copied, 1)
                act.wait_ge(w_done, 1)
                for c in range(2):
                    A.activation(WT[:, c, :], ps[2 + c][:, :], ACT.Copy).then_inc(w_copied, 1)
                act.wait_ge(s_done, ST)
                for c in range(2):
                    A.activation(o[:, c, :], ps[6 + c][:, :], ACT.Copy).then_inc(o_done, 1)

            @st.block.vector
            def _(dve):
                dve.wait_ge(u_copied, 2)
                for j in range(ST):
                    dve.wait_ge(ws_done, 2 * j + 2)
                    if j:
                        dve.wait_ge(s_done, j)
                    for e in range(2):
                        V.tensor_tensor(vnew.rearrange("p (a e) c -> p a e c", e=2)[:, :, e, :],
                                        U[:, j, :].rearrange("p (a e c) -> p a e c", e=2, c=HD)[:, :, e, :],
                                        ps[4 * (1 - e)][:, 0:2 * HD].rearrange("p (a c) -> p a c", c=HD), ALU.subtract) \
                         .then_inc(v_ready, 1)
                    dve.wait_ge(s_done, j + 1)
                    for c in range(2):
                        V.scalar_tensor_tensor(out=state[:, c, :], in0=state[:, c, :], scalar=eGB[:, c, (j + 1) * P - 1:(j + 1) * P],
                                               in1=ps[5][:, c * HD:(c + 1) * HD], op0=ALU.mult, op1=ALU.add).then_inc(s_ready, 1)

        with Stage() as st:
            p_, a_, v_ = head_output(st, finish, "gd", o, col(c2, "gdn_norm"), cgt, y, 6, qd)
            st.block.tensor(p_)
            st.block.scalar(a_)
            st.block.vector(v_)
        scope.close()

    load_inputs()
    Stage.clear_last()
    with nc.Fori(0, DEPTH) as l:
        load_parameters(l, "par1", n1)
        feed_forward(l, t["ffn1_gu"], t["ffn1_dn"], [col(c1, "ffn1_norm", k) for k in range(DT)], ada_half=0)
        scope = Scope()
        m = mixer1_buffers(scope)
        mixer1_project(l, m)
        mixer1_attention(l, m)
        mixer1_mlstm(l, m)
        mixer1_fourier(l, m)
        project_out(l, t["out1"], m[0])
        scope.close()
        feed_forward(l, t["ffn2_gu"], t["ffn2_dn"], [col(c1, "ffn2_norm", k) for k in range(DT)], ada_half=1)
        embed_layer(l)
        Stage.clear_last()
    final_norm()
    Stage.clear_last()
    with nc.Fori(0, DEPTH) as l:
        adaptive(l)
        scope = Scope()
        m = mixer2_buffers(scope)
        mixer2_project(l, m)
        mixer2_window(l, m)
        mixer2_hgrn(l, m)
        mixer2_delta(l, m)
        project_out(l, t["out2"], m[0], [modc[:, 16 + k:17 + k] for k in range(DT)])
        scope.close()
        feed_forward(l, t["ffn3_gu"], t["ffn3_dn"], [gain_f[:, k:k + 1] for k in range(DT)],
                     [modc[:, 24 + k:25 + k] for k in range(DT)], 40)
        Stage.clear_last()
    with Stage() as st:
        @st.block.sync
        def _(sp):
            sp.dma_start(t["out"].rearrange("(k p) s -> p k s", p=P), h[:, :, :]).then_inc(st.sem("stored"), 16)
            sp.wait_ge(st.sem("stored"), 16)
    Stage.clear_last()


def tiles(w, cols=None):
    L, K, N = w.shape
    return np.ascontiguousarray(w.reshape(L, K // P, P, N // P, P).transpose(0, 3, 2, 1, 4)
                                .reshape(L, N // P, P, K))


def tile_pairs(w):
    a = tiles(w)
    L, n, _, K = a.shape
    return np.ascontiguousarray(a.reshape(L, n // 2, 2, P, K).transpose(0, 1, 3, 2, 4).reshape(L, n // 2, P, 2 * K))


def row_parts(w, n):
    L, K, N = w.shape
    return np.ascontiguousarray(w.reshape(L, K // P, P, n, N // n).transpose(0, 3, 2, 1, 4).reshape(L, n, P, -1))


def rows(w):
    L, K, N = w.shape
    return np.ascontiguousarray(w.reshape(L, K // P, P, N).transpose(0, 2, 1, 3).reshape(L, P, -1))


def column(v):
    return v.reshape(v.shape[0], -1, P).transpose(0, 2, 1)


def padded(a, rows_at, width):
    out = np.zeros((a.shape[0], P, 1), a.dtype)
    for g, r in enumerate(rows_at):
        out[:, r:r + width, 0] = a[:, g]
    return out


def pairs(w):
    out = np.zeros((w.shape[0], P, 2, P), w.dtype)
    for g in range(4):
        b = 64 * (g % 2)
        out[:, b:b + 64, g // 2, b:b + 64] = w[:, g]
    return out.reshape(w.shape[0], P, 2 * P)


def lay_out(x):
    L = DEPTH
    f = {}
    f["x"] = np.ascontiguousarray(x["x"][0].T)
    f["p"] = np.ascontiguousarray(x["p"][:, 0].transpose(0, 2, 1))
    f["pos"] = np.ascontiguousarray(x["positions"]).astype(np.int32)
    f["pos2"] = np.ascontiguousarray(x["positions_2"]).astype(np.int32)
    for name in ("ffn1", "ffn2"):
        f[name + "_gu"] = np.stack([tiles(x[name + "_w_gate"]), tiles(x[name + "_w_up"])], 3).reshape(L, FT, P, 2 * D)
        f[name + "_dn"] = tiles(x[name + "_w_down"])
    f["ffn3_gu"] = np.stack([tiles(x["w_gate_2"]), tiles(x["w_up_2"])], 3).reshape(L, FT, P, 2 * D)
    f["ffn3_dn"] = tiles(x["w_down_2"])

    w = x["w_in"]
    o = np.cumsum([0, 384, 256, 64, 256, 256, 256, 16, 256])
    cq, ckv, kr, mx, mv, mo, mif, fin = [w[:, :, o[i]:o[i + 1]] for i in range(8)]
    f["in1_t"] = tile_pairs(np.concatenate([cq, ckv, mx, mo, kr, kr], 2))
    gates = np.zeros((L, D, P), np.float32)
    for g in range(2):
        for d in range(2):
            r = 64 * g + 32 * d
            gates[:, :, r:r + H] = mif[:, :, 8 * g + 4 * d:8 * g + 4 * d + 4]
    f["in1_g"] = rows(gates)
    f["in1_r"] = row_parts(np.concatenate([mv, fin], 2), 2)
    uq = x["mla_w_uq"].reshape(L, 384, 4, 192)
    f["uq"] = rows(np.concatenate([uq[..., :128].reshape(L, 384, 512), uq[..., 128:].reshape(L, 384, 256)], 2))
    ukv = x["mla_w_ukv"].reshape(L, 256, 4, 256)
    f["ukv"] = rows(np.concatenate([ukv[..., :128].reshape(L, 256, 512), ukv[..., 128:].reshape(L, 256, 512)], 2))
    f["mqk"] = np.ascontiguousarray(np.concatenate([pairs(x["mlstm_w_q"]), pairs(x["mlstm_w_k"])], 2))
    f["fnw"] = pairs(x["fnet_w"])
    f["out1"] = tile_pairs(x["w_out"])
    f["pleg"] = tile_pairs(x["ple_w_gate"])
    f["plep"] = rows(x["ple_w_proj"])
    f["par1"] = np.ascontiguousarray(np.concatenate([
        column(x["ffn1_norm"]), column(x["mix_norm"]), column(x["mla_q_norm"]), column(x["mla_kv_norm"]),
        x["mlstm_conv_w"].reshape(L, 5, 2, P).transpose(0, 3, 2, 1).reshape(L, P, 10), column(x["mlstm_conv_b"]),
        padded(x["mlstm_i_bias"], (0, 32), H), padded(x["mlstm_f_bias"], (0, 32), H),
        column(x["mlstm_head_norm"]), column(x["mlstm_skip"]), column(x["fnet_b"]), column(x["ffn2_norm"]),
        column(x["ple_gate_norm"]), column(x["ple_post_norm"])], 2))

    w = x["w_in_2"]
    o = np.cumsum([0, 512, 128, 128, 256, 256, 256, 256, 768, 256, 4, 4])
    aq, ak, av, bq, bf, bv, bg, cc, cgt, cb, ca = [w[:, :, o[i]:o[i + 1]] for i in range(11)]
    order = [0, 4, 1, 5, 2, 6, 3, 7]
    aq = aq.reshape(L, D, 8, HD)[:, :, order].reshape(L, D, 512)
    gates = np.zeros((L, D, P), np.float32)
    gates[:, :, 0:H], gates[:, :, 32:32 + H] = cb, ca
    f["in2_t"] = tile_pairs(np.concatenate([aq, ak, bq, bf, bg, cc, cgt, gates], 2))
    f["in2_r"] = row_parts(np.concatenate([av, bv], 2), 2)
    wo = x["w_out_2"]
    f["out2"] = tile_pairs(np.concatenate([wo[:, :512].reshape(L, 8, HD, D)[:, order].reshape(L, 512, D), wo[:, 512:]], 1))
    f["ada"] = np.ascontiguousarray(x["ada_w_2"].reshape(L, DT // 2, 2, P, 6 * D // 768, 768).transpose(0, 4, 1, 3, 2, 5)
                                    .reshape(L, DT // 2 * (6 * D // 768), P, 2 * 768))
    two = lambda v: np.concatenate([v, v], 1)[:, :, None]
    sinks = np.broadcast_to(x["attn_sinks_2"][:, None, order], (L, P, 8))
    f["par2"] = np.ascontiguousarray(np.concatenate([
        column(x["norm_mix_2"]), two(x["attn_q_norm_2"]), two(x["attn_k_norm_2"]), sinks, two(x["hgrn_out_norm_2"]),
        x["gdn_conv_w_2"].reshape(L, 4, 6, P).transpose(0, 3, 2, 1).reshape(L, P, 24),
        padded(x["gdn_a_log_2"][:, None], (0,), H), padded(x["gdn_dt_bias_2"][:, None], (0,), H),
        two(x["gdn_out_norm_2"]), column(x["norm_ffn_2"]), column(x["ada_b_2"])], 2))
    f["parg"] = np.ascontiguousarray(np.concatenate([
        column(x["final_norm"][None])[0], column(x["c_2"])[0],
        column(x["hgrn_lb_logits_2"]).transpose(1, 0, 2).reshape(P, 4)], 1))

    i = np.arange(S)
    ang = 2 * np.pi * ((i[:, None] * i[None, :]) % S) / S
    unit = 1.0 / math.sqrt(S * HD)
    dft = np.stack([np.cos(ang) * unit, np.sin(ang) * unit]).astype(np.float32)
    f["dft"] = np.ascontiguousarray(dft.reshape(2, ST, P, S).transpose(2, 0, 1, 3).reshape(P, 2 * ST * S))
    return f


def kernel(**inputs):
    import concourse.bacc as bacc
    from concourse.bass_utils import run_bass_kernel_spmd as run

    arrays = lay_out({k: np.asarray(v) for k, v in inputs.items()})
    arrays["cst"], where = pack(constant_columns())
    nc = bacc.Bacc("TRN2", target_bir_lowering=False, num_devices=1)
    t = {k: nc.dram_tensor("in_" + k, a.shape, mybir.dt.from_np(a.dtype), kind="ExternalInput").ap()
         for k, a in arrays.items()}
    t["out"] = nc.dram_tensor("out", (D, S), F32, kind="ExternalOutput").ap()
    build(nc, t, where)
    r = run(nc, [{"in_" + k: a for k, a in arrays.items()}], core_ids=[0])
    return np.ascontiguousarray(r.results[0]["out"].T)[None]
```

```python
import math
from contextlib import ExitStack

import numpy as np

import concourse.bass as bass
from concourse import mybir

F32 = mybir.dt.float32
F32R = mybir.dt.float32r
I32 = mybir.dt.int32
ALU = mybir.AluOpType
ACT = mybir.ActivationFunctionType
AX = mybir.AxisListType

P = 128
S = 512
ST = S // P
D = 1024
DT = D // P
FF = 2816
FT = FF // P
DEPTH = 2
HD = 64
H = 4
EPS = 1e-6
BIG = 1e30
LEVELS = [1 << e for e in range(7)]
NORMS = 5
MLA_SCALE = (128 + 64) ** -0.5


def constant_columns():
    f = np.float32
    i = np.arange(P)
    same64 = (i[:, None] // 64 == i[None, :] // 64)
    out = {"ident": np.eye(P, dtype=f), "ones": np.ones((P, P), f), "heads": same64.astype(f)}

    def rotation(width):
        r = np.zeros((P, P), f)
        for base in (0, 64):
            for m in range(width // 2):
                r[base + m + width // 2, base + m] = -1.0
                r[base + m, base + m + width // 2] = 1.0
        return r

    out["rot_mla"] = rotation(64)
    out["rot_win"] = rotation(16)
    out["upto"] = (i[:, None] <= i[None, :]).astype(f)
    out["from"] = (i[:, None] >= i[None, :]).astype(f)
    out["strict4"] = np.tile((i[:, None] < i[None, :]).astype(f), (1, ST))
    lev = [((i[:, None] // (2 * L) == i[None, :] // (2 * L)) & (i[:, None] % (2 * L) < L)
            & (i[None, :] % (2 * L) >= L)).astype(f) for L in LEVELS]
    out["levels"] = np.concatenate(lev, 1)
    q, k = i[:, None], np.arange(2 * P)[None, :]
    delta = q + P - k
    rest = np.where((delta >= 0) & (delta < P), 0.0, -BIG).astype(f)
    first = np.where(k >= P, rest, -BIG).astype(f)
    out["window"] = np.concatenate([first, rest, rest], 1)
    out["restart"] = np.tile((np.arange(S) % P != 0).astype(f), (P, 1))
    c = np.arange(HD)
    ang = 2 * np.pi * ((c[:, None] * c[None, :]) % HD) / HD
    z = np.zeros((P, P), f)
    dc, ds = z.copy(), z.copy()
    for b in (0, HD):
        dc[b:b + HD, b:b + HD] = np.cos(ang)
        ds[b:b + HD, b:b + HD] = -np.sin(ang)
    out["dft_c"], out["dft_s"] = dc, ds
    sel = np.zeros((36, 8, P), f)
    selp = np.zeros((36, 4, P), f)
    for d in range(2):
        for h in range(H):
            sel[32 * d + h, 4 * d + h] = 1.0
            selp[32 * d + h, 2 * d + h // 2, 64 * (h % 2):64 * (h % 2) + 64] = 1.0
    heads_in = np.zeros((P, NORMS, 2 * NORMS), f)
    heads_out = np.zeros((2 * NORMS, NORMS, P), f)
    for r in range(NORMS):
        for e in range(2):
            heads_in[64 * e:64 * e + 64, r, 2 * r + e] = 1.0
            heads_out[2 * r + e, r, 64 * e:64 * e + 64] = 1.0
    out["heads_in"], out["heads_out"] = heads_in.reshape(P, -1), heads_out.reshape(2 * NORMS, -1)
    out["sel"] = sel.reshape(36, -1)
    out["selp"] = selp.reshape(36, -1)
    inv1 = np.zeros((P, 1), f)
    inv2 = np.zeros((P, 1), f)
    for b in (0, 64):
        t = 1.0 / (10000.0 ** (np.arange(0, 64, 2) / 64.0))
        inv1[b:b + 32, 0] = t
        inv1[b + 32:b + 64, 0] = t
        t = 500000.0 ** (-np.arange(8) * 2.0 / 16.0)
        inv2[b:b + 8, 0] = t
        inv2[b + 8:b + 16, 0] = t
    out["inv_mla"], out["inv_win"] = inv1, inv2
    out["eps"] = np.full((P, 1), EPS, f)
    out["one"] = np.full((P, 1), 1.0, f)
    return out


def pack(columns):
    at, where = 0, {}
    for name, a in columns.items():
        where[name] = (at, a.shape[1], a.shape[0])
        at += a.shape[1]
    whole = np.zeros((P, at), np.float32)
    for name, a in columns.items():
        whole[:a.shape[0], where[name][0]:where[name][0] + a.shape[1]] = a
    return whole, where


PAR1 = {"ffn1_norm": 8, "mix_norm": 8, "q_norm": 3, "kv_norm": 2, "conv_w": 10, "conv_b": 2, "i_bias": 1,
        "f_bias": 1, "head_norm": 2, "skip": 2, "fnet_b": 2, "ffn2_norm": 8, "gate_norm": 8, "post_norm": 8}
PAR2 = {"norm_mix": 8, "q_norm": 1, "k_norm": 1, "sinks": 8, "hgrn_norm": 1, "conv_w": 24, "a_log": 1,
        "dt_bias": 1, "gdn_norm": 1, "norm_ffn": 8, "ada_b": 48}
PARG = {"final_norm": 8, "cond": 8, "lb": 4}


def columns_of(table):
    at, out = 0, {}
    for name, n in table.items():
        out[name] = (at, n)
        at += n
    return out, at


def build(nc, t, where):
    ctx = ExitStack()
    with ctx:
        program(nc, t, where, ctx)


def program(nc, t, where, ctx):
    def sb(name, shape, dt=F32):
        return ctx.enter_context(nc.sbuf_tensor(name, shape, dt))

    h = sb("stream", [P, DT, S])
    hsq = sb("stream_squares", [P, S])
    cst = sb("consts", [P, t["cst"].shape[1]])
    c1, n1 = columns_of(PAR1)
    c2, n2 = columns_of(PAR2)
    cg, ng = columns_of(PARG)
    par = sb("par", [P, max(n1, n2)])
    parg = sb("parg", [P, ng])
    rope = sb("rope", [P, 4, S])
    mod = sb("mod", [P, DEPTH, 48])
    ada = sb("ada", [P, DEPTH, 48])
    lbt = sb("lbt", [P, DEPTH, 3, 2])
    ps = [ctx.enter_context(nc.psum_tensor(f"ps{i}", [P, S], F32)) for i in range(8)]

    V, A, T, G = nc.vector, nc.scalar, nc.tensor, nc.gpsimd

    class Stage:
        last = None
        count = 0

        def __init__(self):
            self.held = ExitStack()
            self.sems = {}
            Stage.count += 1

        def sem(self, name):
            if name not in self.sems:
                self.sems[name] = self.held.enter_context(nc.semaphore(f"{name}_{Stage.count}"))
            return self.sems[name]

        def clear(self, sp):
            for sem in self.sems.values():
                sp.sem_clear(sem)

        def __enter__(self):
            self.manager = nc.Block()
            self.block = self.manager.__enter__()
            if Stage.last:
                self.block.sync(Stage.last.clear)
            return self

        def __exit__(self, *e):
            r = self.manager.__exit__(*e)
            if Stage.last:
                Stage.last.held.close()
            Stage.last = self
            return r

        @staticmethod
        def clear_last():
            with nc.Block() as cleared:
                cleared.sync(Stage.last.clear)
            Stage.last.held.close()
            Stage.last = None

    class Order:

        def __init__(self, eng, sem):
            self.eng, self.sem, self.count = eng, sem, 0

        def tick(self, ins):
            ins.then_inc(self.sem, 1)
            self.count += 1
            return self.count

        def done(self, ins):
            self.tick(ins)
            self.eng.wait_ge(self.sem, self.count)

    class Scope(ExitStack):
        made = 0

        def sb(self, name, shape, dt=F32):
            Scope.made += 1
            return self.enter_context(nc.sbuf_tensor(f"{name}_{Scope.made}", shape, dt))

        def space(self, size):
            return Space(self.sb("work", [P, size]), size)

    class Space:

        def __init__(self, tensor, size, at=0):
            self.tensor, self.size, self.at = tensor, size, at

        def copy(self):
            return Space(self.tensor, self.size, self.at)

        def get(self, *shape):
            size = int(np.prod(shape))
            assert self.at + size <= self.size, (self.at + size, self.size)
            a = self.tensor[:, self.at:self.at + size]
            self.at += size
            names = "abcd"[:len(shape)]
            if len(shape) > 1:
                a = a.rearrange(f"p ({' '.join(names)}) -> p {' '.join(names)}",
                                **dict(zip(names[1:], shape[1:])))
            return a

    def C(name, rows=None, a=0, b=None):
        at, width, r = where[name]
        return cst[0:(rows or r), at + a:at + (width if b is None else b)]

    def cond(k):
        return col(cg, "cond", k)

    def col(table, name, k=0, rows=P):
        at, width = table[name]
        src = parg if table is cg else par
        return src[0:rows, at + k:at + k + 1]

    V, A, T, G = nc.vector, nc.scalar, nc.tensor, nc.gpsimd

    def products(bank, lhs, rhs, kt):
        for k in range(kt):
            mm = T.matmul(bank, lhs(k), rhs(k), start=(k == 0), stop=(k == kt - 1))
        return mm

    def split_products(bank, lhs_hi, lhs_lo, rhs_hi, rhs_lo, kt, before=None):
        for k in range(kt):
            if before:
                before(k)
            T.matmul(bank, lhs_hi(k), rhs_hi(k), start=(k == 0), stop=False)
            T.matmul(bank, lhs_hi(k), rhs_lo(k), start=False, stop=False)
            mm = T.matmul(bank, lhs_lo(k), rhs_hi(k), start=False, stop=(k == kt - 1))
        return mm

    ITEM = 2 * DT * P

    class Weights:

        def __init__(self, st, scope):
            self.raw = scope.sb("raw", [P, 2, ITEM])
            self.hi = scope.sb("w_hi", [P, 2, ITEM], F32R)
            self.lo = scope.sb("w_lo", [P, 2, ITEM], F32R)
            self.landed = [st.sem(f"w_landed{b}") for b in range(2)]
            self.hi_ready, self.lo_ready, self.used = st.sem("w_hi_ready"), st.sem("w_lo_ready"), st.sem("w_used")

        def load(self, sp, b, n, src, first=False):
            if not first:
                sp.wait_ge(self.lo_ready, 2 * n + (b - 1))
            sp.dma_start(self.raw[:, b, 0:src.shape[-1]], src).then_inc(self.landed[b], 16)

        def high(self, act, b, n, size, first=False):
            act.wait_ge(self.landed[b], 16 * n + 16)
            if not first:
                act.wait_ge(self.used, 2 * n + (b - 1))
            A.activation(self.hi[:, b, 0:size], self.raw[:, b, 0:size], ACT.Copy).then_inc(self.hi_ready, 1)

        def low(self, dve, b, n, size):
            dve.wait_ge(self.hi_ready, 2 * n + (b + 1))
            V.tensor_tensor(self.lo[:, b, 0:size], self.raw[:, b, 0:size], self.hi[:, b, 0:size].bitcast(F32), ALU.subtract) \
             .then_inc(self.lo_ready, 1)

        def wait(self, pe, b, n):
            pe.wait_ge(self.lo_ready, 2 * n + (b + 1))

    class Split:

        def __init__(self, scope, name, kt):
            self.hi = scope.sb(name + "_hi", [P, kt, S], F32R)
            self.lo = scope.sb(name + "_lo", [P, kt, S], F32R)

    class Norm:

        def __init__(self, st, name, src, dst, gains, width, space, bank, lhs="ones", shifts=None, presummed=False):
            self.src, self.dst, self.gains, self.width, self.lhs = src, dst, gains, width, lhs
            self.shifts = shifts
            self.k = len(src)
            self.bank = bank
            self.sq = space.get(2, S)
            self.presummed = presummed
            self.acc = hsq[:, :] if presummed else space.get(S)
            self.root = self.acc if self.k > 1 else self.sq[:, 1, :]
            self.rstd = space.get(S)
            self.squares = st.sem(name + "_squares")
            self.added = st.sem(name + "_added")
            self.summed = st.sem(name + "_summed")
            self.rooted = st.sem(name + "_rooted")
            self.inverted = st.sem(name + "_inverted")
            self.ready = st.sem(name + "_ready")
            self.split = isinstance(dst, Split)
            if self.split:
                self.tmp = self.sq
                self.whole = space.get(2, S) if shifts else self.tmp
                self.scaled, self.high = st.sem(name + "_scaled"), st.sem(name + "_high")

        def square(self, act):
            for k in range(0 if self.presummed else self.k):
                if k >= 2:
                    act.wait_ge(self.added, max(1, k - 2))
                A.activation(self.sq[:, k % 2, :], self.src[k], ACT.Square).then_inc(self.squares, 1)

        def add(self, dve):
            for k in range(1, 1 if self.presummed else self.k):
                dve.wait_ge(self.squares, k + 1)
                if k >= 2:
                    dve.wait_ge(self.added, k - 1)
                V.tensor_tensor(self.acc, self.sq[:, 0, :] if k == 1 else self.acc, self.sq[:, k % 2, :], ALU.add) \
                 .then_inc(self.added, 1)

        def act(self, act):
            self.square(act)
            self.take_root(act)
            self.act_finish(act)

        def take_root(self, act):
            act.wait_ge(self.summed, 1)
            A.activation(self.root, self.bank, ACT.Sqrt, scale=1.0 / self.width, bias=C("eps")) \
             .then_inc(self.rooted, 1)

        def act_finish(self, act):
            if self.split:
                for k in range(self.k):
                    act.wait_ge(self.scaled, k + 1)
                    if self.shifts:
                        if k >= 2:
                            act.wait_ge(self.ready, k - 1)
                        A.activation(self.whole[:, k % 2, :], self.tmp[:, k % 2, :], ACT.Identity, bias=self.shifts[k])
                        A.activation(self.dst.hi[:, k, :], self.tmp[:, k % 2, :], ACT.Identity, bias=self.shifts[k]) \
                         .then_inc(self.high, 1)
                    else:
                        A.activation(self.dst.hi[:, k, :], self.tmp[:, k % 2, :], ACT.Copy).then_inc(self.high, 1)

        def pe(self, pe):
            if self.presummed:
                pass
            elif self.k > 1:
                pe.wait_ge(self.added, self.k - 1)
            else:
                pe.wait_ge(self.squares, 1)
            T.matmul(self.bank, C(self.lhs), self.acc if self.k > 1 else self.sq[:, 0, :], start=True, stop=True) \
             .then_inc(self.summed, 1)

        def dve(self, dve):
            self.add(dve)
            self.invert(dve)
            self.dve_finish(dve)

        def invert(self, dve):
            dve.wait_ge(self.rooted, 1)
            V.reciprocal(self.rstd, self.root).then_inc(self.inverted, 1)

        def dve_finish(self, dve):
            dve.wait_ge(self.inverted, 1)
            for k in range(self.k + 1):
                if k < self.k:
                    if self.split and k >= 2:
                        dve.wait_ge(self.ready, k - 1)
                    V.scalar_tensor_tensor(out=self.tmp[:, k % 2, :] if self.split else self.dst[k], in0=self.src[k],
                                           scalar=self.gains[k], in1=self.rstd, op0=ALU.mult, op1=ALU.mult) \
                     .then_inc(self.scaled if self.split else self.ready, 1)
                if self.split and k >= 1:
                    dve.wait_ge(self.high, k)
                    V.tensor_tensor(self.dst.lo[:, k - 1, :], self.whole[:, (k - 1) % 2, :],
                                    self.dst.hi[:, k - 1, :].bitcast(F32), ALU.subtract).then_inc(self.ready, 1)

        def tile_wait(self, pe):
            return lambda k: pe.wait_ge(self.ready, k + 1)

    class SumOfSquares:

        def __init__(self, st, sq):
            self.sq = sq
            self.squared, self.summed = st.sem("h_squared"), st.sem("h_summed")

        def start(self, dve):
            V.memset(hsq[:, :], 0.0).then_inc(self.summed, 1)

        def add(self, dve, x, n):
            dve.wait_ge(self.summed, n + 1)
            V.tensor_tensor(self.sq, x, x, ALU.mult).then_inc(self.squared, 1)
            dve.wait_ge(self.squared, n + 1)
            V.tensor_tensor(hsq[:, :], hsq[:, :], self.sq, ALU.add).then_inc(self.summed, 1)

    class HeadNorms:

        def __init__(self, st, x, gains, width, space):
            self.x, self.gains, self.width, self.n = x, gains, width, len(x)
            self.sq, self.root, self.rstd = space.get(2, S), space.get(S), space.get(S)
            self.rows = slice(0, 2 * self.n)
            self.squares, self.summed, self.rooted, self.inverted, self.spread, self.ready = [
                st.sem("hn_" + name) for name in ("squares", "summed", "rooted", "inverted", "spread", "ready")]

        def square(self, act):
            for r in range(self.n):
                if r >= 2:
                    act.wait_ge(self.summed, r - 1)
                A.activation(self.sq[:, r % 2, :], self.x[r], ACT.Square).then_inc(self.squares, 1)

        def take_root(self, act):
            act.wait_ge(self.summed, self.n)
            A.activation(self.root[self.rows, :], ps[0][self.rows, :], ACT.Sqrt, scale=1.0 / self.width,
                         bias=C("eps")[self.rows, :]).then_inc(self.rooted, 1)

        def pe(self, pe):
            M = 2 * self.n
            for r in range(self.n):
                pe.wait_ge(self.squares, r + 1)
                T.matmul(ps[0][self.rows, :], C("heads_in", P, 2 * NORMS * r, 2 * NORMS * r + M), self.sq[:, r % 2, :],
                         start=(r == 0), stop=(r == self.n - 1)).then_inc(self.summed, 1)
            pe.wait_ge(self.inverted, 1)
            for r in range(self.n):
                T.matmul(ps[r][:, :], C("heads_out", M, P * r, P * r + P), self.rstd[self.rows, :], start=True, stop=True) \
                 .then_inc(self.spread, 1)

        def dve(self, dve):
            dve.wait_ge(self.rooted, 1)
            V.reciprocal(self.rstd[self.rows, :], self.root[self.rows, :]).then_inc(self.inverted, 1)
            for r in range(self.n):
                dve.wait_ge(self.spread, r + 1)
                V.scalar_tensor_tensor(out=self.x[r], in0=self.x[r], scalar=self.gains[r], in1=ps[r][:, :],
                                       op0=ALU.mult, op1=ALU.mult).then_inc(self.ready, 1)

    HALVES = [(0, 12), (12, 10)]
    AC = 768
    AN = 3 * D // AC

    def feed_forward(l, w_gu, w_dn, gains, shifts=None, gate_at=None, ada_half=None):
        scope = Scope()
        x = Split(scope, "x", DT)
        hid = Split(scope, "hid", max(c for _, c in HALVES))
        sp_ = scope.space(2 * 2 * S + (8 if shifts else 6) * S)
        sil, hf = sp_.get(2, S), sp_.get(2, S)
        phases, n0 = [], 0
        for t0, nt in HALVES:
            phases.append((True, t0, nt, n0, nt // 2, ITEM))
            phases.append((False, t0, nt, n0 + nt // 2, DT // 2, nt * P))
            n0 += nt // 2 + DT // 2
        sizes = [z for *_, count, z in phases for _ in range(count)]
        with Stage() as st:
            w = Weights(st, scope)
            norm = Norm(st, "norm", [h[:, k, :] for k in range(DT)], x, gains, D, sp_, ps[6][:, :], shifts=shifts,
                        presummed=True)
            squares = SumOfSquares(st, hf[:, 0, :])
            gate_done, silu_ready = st.sem("gate_done"), st.sem("silu_ready")
            if ada_half is not None:
                aw = scope.sb("ada_w", [P, 2, AC])
                acc = sp_.tensor[:, 4 * S:4 * S + 3 * D]
                a_landed, a_scaled, a_added, a_used, a_summed = [st.sem(n) for n in ("a_landed", "a_scaled", "a_added", "a_used",
                                                                                    "a_summed")]

                def load_ada(sp, n, first=False):
                    if not first:
                        sp.wait_ge(a_used, n)
                    sp.dma_start(aw.rearrange("p a n -> p (a n)"), t["ada"][l, n + AN * DT // 2 * ada_half, :, :]).then_inc(a_landed, 16)

                @st.block.gpsimd
                def _(pool):
                    pool.wait_ge(norm.ready, DT)
                    added = 0
                    for n in range(AN * DT // 2):
                        c, k0 = divmod(2 * n, DT)
                        a = acc[:, c * AC:(c + 1) * AC]
                        pool.wait_ge(a_landed, 16 * n + 16)
                        for e in range(2):
                            G.tensor_scalar(aw[:, e, :], aw[:, e, :], cond(k0 + e), None, ALU.mult).then_inc(a_scaled, 1)
                        for e in range(2):
                            pool.wait_ge(a_scaled, 2 * n + e + 1)
                            if n or e:
                                pool.wait_ge(a_added, 2 * n + e)
                            if k0 + e == 0:
                                ins = G.tensor_copy(a, aw[:, 0, :])
                            else:
                                ins = G.tensor_tensor(a, a, aw[:, e, :], ALU.add)
                            ins.then_inc(a_added, 1)
                        pool.wait_ge(a_added, 2 * n + 2)
                        pool.sem_inc(a_used, 1)
            hf_ready, hid_high, hid_ready, h_updated = (st.sem("hf_ready"), st.sem("hid_high"), st.sem("hid_ready"),
                                                        st.sem("h_updated"))

            @st.block.sync
            def _(sp):
                for gu, t0, nt, n0, count, size in phases:
                    def load(i, first=False):
                        for b in range(2):
                            src = w_gu[l, 2 * i + (t0 + b), :, :] if gu else w_dn[l, 2 * i + b, :, t0 * P:(t0 + nt) * P]
                            w.load(sp, b, i + n0, src, first)
                    first = 1 if n0 == 0 else 0
                    if first:
                        load(0, True)
                        if ada_half is not None:
                            load_ada(sp, 0, True)
                    last = count
                    if ada_half is not None:
                        last = min(count, AN * DT // 2 - n0)
                    with sp.Fori(first, last) as i:
                        load(i)
                        if ada_half is not None:
                            load_ada(sp, i + n0)
                    if last < count:
                        with sp.Fori(last, count) as i:
                            load(i)

            @st.block.tensor
            def _(pe):
                norm.pe(pe)
                for half, (gu, t0, nt, n0, count, size) in enumerate(phases):
                    def up(i, before=None):
                        for b in range(2):
                            w.wait(pe, b, i + n0)
                            pe.wait_ge(hid_ready, 2 * i + (t0 + b + 1))
                            wt = lambda part, a: lambda k: part[:, b, (a * DT + k) * P:(a * DT + k + 1) * P]
                            for a in range(2):
                                split_products(ps[2 * b + a][:, :], wt(w.hi, a), wt(w.lo, a), lambda k: x.hi[:, k, :],
                                               lambda k: x.lo[:, k, :], DT, before).then_inc(w.used if a else gate_done, 1)
                                before = None

                    def down(i):
                        for b in range(2):
                            w.wait(pe, b, i + n0)
                            pe.wait_ge(h_updated, 2 * i + (DT * (half // 2) + b + 1))
                            split_products(ps[4 + b][:, :], lambda k: w.hi[:, b, k * P:(k + 1) * P],
                                           lambda k: w.lo[:, b, k * P:(k + 1) * P], lambda k: hid.hi[:, k, :],
                                           lambda k: hid.lo[:, k, :], nt).then_inc(w.used, 1)

                    if gu and n0 == 0:
                        up(0, norm.tile_wait(pe))
                        with pe.Fori(1, count) as i:
                            up(i)
                    elif gu:
                        with pe.Fori(0, count) as i:
                            up(i)
                    else:
                        pe.wait_ge(hid_ready, 2 + t0 + nt)
                        with pe.Fori(0, count) as i:
                            down(i)
                if ada_half is not None:
                    pe.wait_ge(a_added, DT * AN)
                    for j in range(24):
                        mm = T.matmul(ps[7][:, j:j + 1], acc[:, j * P:(j + 1) * P], C("ones")[:, 0:1], start=True, stop=True)
                    mm.then_inc(a_summed, 1)

            @st.block.scalar
            def _(act):
                norm.square(act)
                norm.take_root(act)
                for b in range(2):
                    w.high(act, b, 0, ITEM, True)
                norm.act_finish(act)
                A.activation(sil[:, 0, 0:1], C("one"), ACT.Silu).then_inc(st.sem("table"), 1)
                act.wait_ge(st.sem("table"), 1)
                for gu, t0, nt, n0, count, size in phases:
                    def step(i, ahead):
                        for b in range(2):
                            if gu:
                                act.wait_ge(gate_done, 2 * i + (t0 + b + 1))
                                act.wait_ge(hid_ready, 2 * i + (t0 + b + 1))
                                A.activation(sil[:, b, :], ps[2 * b][:, :], ACT.Silu).then_inc(silu_ready, 1)
                            if ahead:
                                w.high(act, b, i + (n0 + 1), ahead)
                    with act.Fori(0, count - 1) as i:
                        step(i, size)
                    step(count - 1, sizes[n0 + count] if n0 + count < len(sizes) else 0)

            @st.block.vector
            def _(dve):
                dve.sem_inc(hid_ready, 2)
                dve.sem_inc(h_updated, 2)
                norm.add(dve)
                norm.invert(dve)
                w.low(dve, 0, 0, ITEM)
                norm.dve_finish(dve)
                w.low(dve, 1, 0, ITEM)
                for half, (gu, t0, nt, n0, count, size) in enumerate(phases):
                    def step(i, ahead):
                        for b in range(2):
                            if gu:
                                j = 2 * i + (t0 + b)
                                at = lambda part: part[:, bass.ds(2 * i + b, 1), :].rearrange("p a s -> p (a s)")
                                dve.wait_ge(silu_ready, j + 1)
                                dve.wait_ge(w.used, 2 * i + (2 * n0 + b + 1))
                                V.tensor_tensor(hf[:, b, :], sil[:, b, :], ps[2 * b + 1][:, :], ALU.mult).then_inc(hf_ready, 1)
                                dve.wait_ge(hf_ready, j + 1)
                                V.tensor_copy(at(hid.hi), hf[:, b, :]).then_inc(hid_high, 1)
                                dve.wait_ge(hid_high, j + 1)
                                V.tensor_tensor(at(hid.lo), hf[:, b, :], at(hid.hi).bitcast(F32), ALU.subtract).then_inc(hid_ready, 1)
                                dve.wait_ge(hid_ready, j + 3)
                            else:
                                dve.wait_ge(w.used, 2 * i + (2 * n0 + b + 1))
                                hx = h[:, bass.ds(2 * i + b, 1), :].rearrange("p a s -> p (a s)")
                                V.scalar_tensor_tensor(out=hx, in0=ps[4 + b][:, :],
                                                       scalar=0.5 if gate_at is None else mod[:, 0, bass.ds(2 * i + (gate_at + b), 1)],
                                                       in1=hx, op0=ALU.mult, op1=ALU.add).then_inc(h_updated, 1)
                                if half == 3:
                                    dve.wait_ge(h_updated, 2 * i + (2 + DT + b + 1))
                                    squares.add(dve, hx, 2 * i + b)
                            if ahead:
                                w.low(dve, b, i + (n0 + 1), ahead)
                    if half == 3:
                        squares.start(dve)
                    with dve.Fori(0, count - 1) as i:
                        step(i, size)
                    step(count - 1, sizes[n0 + count] if n0 + count < len(sizes) else 0)
                if ada_half is not None:
                    dve.wait_ge(a_summed, 1)
                    V.tensor_copy(ada[:, bass.ds(l, 1), 24 * ada_half:24 * ada_half + 24].rearrange("p a c -> p (a c)"), ps[7][:, 0:24])
        scope.close()

    def load_inputs():
        scope = Scope()
        sp_ = scope.space(10 * S)
        posi = scope.sb("positions", [P, 2 * S], I32)[:, :]
        pos, turns, ang, red = sp_.get(2, S), sp_.get(S), sp_.get(S), sp_.get(S)
        shifted, over = sp_.get(S), sp_.get(S)
        lbx = sp_.get(16)
        c_hi = 6.28125
        c_mid = float(np.float32(2 * math.pi - c_hi))
        c_lo = float(2 * math.pi - c_hi - c_mid)
        magic = 1.5 * 2.0 ** 23
        top = 3.1415925
        with Stage() as st:
            x_landed = st.sem("x_landed")
            landed, table_ready, reduced = st.sem("landed"), st.sem("table_ready"), st.sem("reduced")
            bounds_in, bounds_out = st.sem("bounds_in"), st.sem("bounds_out")
            squares = SumOfSquares(st, sp_.get(S))

            @st.block.sync
            def _(sp):
                sp.dma_start(posi[:, 0:S], t["pos"].partition_broadcast(P)).then_inc(landed, 16)
                sp.dma_start(posi[:, S:2 * S], t["pos2"].partition_broadcast(P)).then_inc(landed, 16)
                sp.dma_start(parg[:, :], t["parg"]).then_inc(landed, 16)
                sp.dma_start(cst[:, :], t["cst"]).then_inc(landed, 16)
                sp.dma_start(h[:, :, :], t["x"].rearrange("(k p) s -> p k s", p=P)).then_inc(x_landed, 16)

            @st.block.vector
            def _(dve):
                order = Order(dve, st.sem("dve_order"))
                dve.wait_ge(landed, 64)
                order.done(V.tensor_copy(pos.rearrange("p a s -> p (a s)"), posi))
                for r, inv in enumerate(("inv_mla", "inv_win")):
                    order.done(V.tensor_scalar(ang, pos[:, r, :], C(inv), None, ALU.mult))
                    order.done(V.tensor_scalar(turns, ang, 1.0 / (2 * math.pi), magic, ALU.mult, ALU.add))
                    order.done(V.tensor_scalar(turns, turns, magic, None, ALU.subtract))
                    order.done(V.scalar_tensor_tensor(out=red, in0=turns, scalar=-c_hi, in1=ang, op0=ALU.mult, op1=ALU.add))
                    order.done(V.scalar_tensor_tensor(out=red, in0=turns, scalar=-c_mid, in1=red, op0=ALU.mult, op1=ALU.add))
                    order.done(V.scalar_tensor_tensor(out=red, in0=turns, scalar=-c_lo, in1=red, op0=ALU.mult, op1=ALU.add))
                    order.done(V.tensor_scalar(shifted, red, math.pi / 2, None, ALU.add))
                    order.done(V.tensor_scalar(over, shifted, math.pi, -2 * math.pi, ALU.is_gt, ALU.mult))
                    order.done(V.tensor_tensor(shifted, shifted, over, ALU.add))
                    order.done(V.tensor_scalar(rope[:, 2 * r, :], shifted, top, -top, ALU.min, ALU.max))
                    V.tensor_scalar(rope[:, 2 * r + 1, :], red, top, -top, ALU.min, ALU.max).then_inc(reduced, 1)
                l0 = parg[:, cg["lb"][0]:cg["lb"][0] + 2]
                l1 = parg[:, cg["lb"][0] + 2:cg["lb"][0] + 4]
                top_ = lbx[:, 0:2]
                order.done(V.tensor_tensor(top_, l0, l1, ALU.max))
                order.done(V.tensor_tensor(lbx[:, 2:4], l0, top_, ALU.subtract))
                order.done(V.tensor_tensor(lbx[:, 4:6], l1, top_, ALU.subtract))
                V.tensor_copy(lbx[:, 12:14], lbx[:, 4:6]).then_inc(bounds_in, 1)
                dve.wait_ge(bounds_out, 1)
                order.done(V.tensor_tensor(lbx[:, 10:12], lbx[:, 6:8], lbx[:, 8:10], ALU.add))
                order.done(V.reciprocal(lbx[:, 12:14], lbx[:, 10:12]))
                V.tensor_copy(lbx[:, 14:16], lbx[:, 10:12]).then_inc(bounds_in, 1)
                order.done(V.memset(lbt[:, 0, 0, :], -BIG))
                order.done(V.memset(lbt[:, 0, 1, :], 0.0))
                order.done(V.memset(lbt[:, 0, 2, :], 1.0))
                order.done(V.tensor_tensor(lbt[:, 1, 2, :], lbx[:, 6:8], lbx[:, 12:14], ALU.mult))
                dve.wait_ge(bounds_out, 2)
                order.done(V.tensor_tensor(lbt[:, 1, 0, :], lbx[:, 4:6], lbx[:, 14:16], ALU.subtract))
                order.done(V.tensor_tensor(lbt[:, 1, 1, :], lbx[:, 2:4], lbx[:, 14:16], ALU.subtract))
                dve.wait_ge(x_landed, 16)
                squares.start(dve)
                for k in range(DT):
                    squares.add(dve, h[:, k, :], k)

            @st.block.scalar
            def _(act):
                for r in range(2):
                    act.wait_ge(reduced, r + 1)
                    for j in range(2):
                        A.activation(rope[:, 2 * r + j, :], rope[:, 2 * r + j, :], ACT.Sin).then_inc(table_ready, 1)
                at = cg["cond"][0]
                A.activation(parg[:, at:at + DT], parg[:, at:at + DT], ACT.Silu)
                act.wait_ge(bounds_in, 1)
                A.activation(lbx[:, 6:10], lbx[:, 2:6], ACT.Exp).then_inc(bounds_out, 1)
                act.wait_ge(bounds_in, 2)
                A.activation(lbx[:, 14:16], lbx[:, 14:16], ACT.Ln).then_inc(bounds_out, 1)
        scope.close()

    def load_parameters(l, name, width):
        with Stage() as st:
            @st.block.sync
            def _(sp):
                sp.dma_start(par[:, 0:width], t[name][l, :, :]).then_inc(st.sem("landed"), 16)
                sp.wait_ge(st.sem("landed"), 16)

    WORK = 22900

    def mixer1_buffers(scope):
        m = scope.space(16648)
        y = m.get(DT, S)
        latents = m.at
        cq, ckv, kr = m.get(3, S), m.get(2, S), m.get(S)
        mx = m.get(2, S + 4)
        mo = m.get(2, S)
        gi, gf = m.get(S), m.get(S)
        vz = m.get(ST, S)
        maps = m.at
        uq, ukv = m.get(3, 768), m.get(2, 1024)
        a, b = Space(m.tensor, maps, latents), Space(m.tensor, m.size, maps)
        part, spec = a.get(2, 2, S), a.get(2, S)
        dft, fw = b.get(2, ST, S), b.get(2, P)
        return (y, cq, ckv, kr, mx, mo, gi, gf, vz, uq, ukv), (part, spec, dft, fw)

    def mixer1_project(l, m):
        y, cq, ckv, kr, mx, mo, gi, gf, vz, uq, ukv = m
        scope = Scope()
        x = Split(scope, "x", DT)
        sp_ = scope.space(3 * S)
        dst = [cq[:, 0, :], cq[:, 1, :], cq[:, 2, :], ckv[:, 0, :], ckv[:, 1, :], mx[:, 0, 2:2 + S], mx[:, 1, 2:2 + S],
               mo[:, 0, :], mo[:, 1, :], kr]
        sizes = [ITEM] * 5 + [D] + [ITEM] * 2
        with Stage() as st:
            w = Weights(st, scope)
            norm = Norm(st, "norm", [h[:, k, :] for k in range(DT)], x,
                        [col(c1, "mix_norm", k) for k in range(DT)], D, sp_, ps[6][:, :], presummed=True)
            next_landed = st.sem("next_landed")
            done, copied = st.sem("done"), st.sem("copied")

            @st.block.sync
            def _(sp):
                for g in range(8):
                    src = t["in1_t"][l, g, :, :] if g < 5 else t["in1_g"][l, :, :] if g == 5 else t["in1_r"][l, g - 6, :, :]
                    w.load(sp, g % 2, g // 2, src, g < 2)
                    if g == 1:
                        sp.dma_start(uq.rearrange("p k m -> p (k m)"), t["uq"][l, :, :]).then_inc(next_landed, 16)
                        sp.dma_start(ukv.rearrange("p k m -> p (k m)"), t["ukv"][l, :, :]).then_inc(next_landed, 16)
                sp.wait_ge(next_landed, 32)

            @st.block.gpsimd
            def _(pool):
                G.memset(mx[:, :, 0:2], 0.0)
                G.memset(mx[:, :, S + 2:S + 4], 0.0)

            @st.block.tensor
            def _(pe):
                norm.pe(pe)
                before = norm.tile_wait(pe)
                for g in range(6):
                    b = g % 2
                    w.wait(pe, b, g // 2)
                    for a in range(2 if g < 5 else 1):
                        j = 2 * g + a
                        if j >= 4:
                            pe.wait_ge(copied, j - 3)
                        wt = lambda part: lambda k: part[:, b, (a * DT + k) * P:(a * DT + k + 1) * P]
                        split_products(ps[j % 4][:, :], wt(w.hi), wt(w.lo), lambda k: x.hi[:, k, :], lambda k: x.lo[:, k, :],
                                       DT, before).then_inc(done if a == 0 and g < 5 else w.used, 1)
                        before = None
                for g in (6, 7):
                    b = g % 2
                    w.wait(pe, b, g // 2)
                    for j in range(ST):
                        q = slice(j * P, (j + 1) * P)
                        wt = lambda part: lambda k: part[:, b, k * 256:(k + 1) * 256]
                        mm = split_products(ps[4 + j][:, (g - 6) * 256:(g - 5) * 256], lambda k: x.hi[:, k, q], lambda k: x.lo[:, k, q],
                                            wt(w.hi), wt(w.lo), DT)
                    mm.then_inc(w.used, 1)

            @st.block.scalar
            def _(act):
                norm.square(act)
                norm.take_root(act)
                for b in range(2):
                    w.high(act, b, 0, sizes[b], True)
                norm.act_finish(act)
                for g in range(8):
                    for a in range(2):
                        j = 2 * g + a
                        if g < 5:
                            act.wait_ge(w.used if a else done, g + 1)
                            A.activation(dst[j], ps[j % 4][:, :], ACT.Copy).then_inc(copied, 1)
                    if g == 5:
                        act.wait_ge(w.used, 6)
                        bank = ps[2]
                        for rows_, bias, r in ((gi, "i_bias", 0), (gf, "f_bias", 64)):
                            A.activation(rows_[0:32, :], bank[r:r + 32, :], ACT.Identity, bias=col(c1, bias)[0:32, :])
                            A.activation(rows_[32:36, :], bank[r + 32:r + 36, ::-1], ACT.Identity, bias=col(c1, bias)[32:36, :])
                    if g + 2 < 8:
                        w.high(act, g % 2, g // 2 + 1, sizes[g + 2])
                act.wait_ge(w.used, 8)
                for j in range(ST):
                    A.activation(vz[:, j, :], ps[4 + j][:, :], ACT.Copy)

            @st.block.vector
            def _(dve):
                norm.add(dve)
                norm.invert(dve)
                w.low(dve, 0, 0, sizes[0])
                norm.dve_finish(dve)
                w.low(dve, 1, 0, sizes[1])
                for g in range(2, 8):
                    w.low(dve, g % 2, g // 2, sizes[g])
        scope.close()

    def rotate(dve, order, x, turned, cos_sin, tmp):
        V.tensor_tensor(x, x, rope[:, cos_sin, :], ALU.mult)
        order.done(V.tensor_tensor(tmp, turned, rope[:, cos_sin + 1, :], ALU.mult))
        return V.tensor_tensor(x, x, tmp, ALU.add)

    def mlstm_buffers(sp_):
        conv, xc = sp_.get(2, S), sp_.get(2, S)
        qk = sp_.get(2, 2, S)
        ws = sp_.get(2, 2, P)
        absf, soft, lf, F, a, M = [sp_.get(S) for _ in range(6)]
        rows_a, rows_m, rows_t = sp_.get(S), sp_.get(S), sp_.get(S)
        acol = sp_.get(ST, 36)
        return conv, xc, qk, ws, absf, soft, lf, F, a, M, rows_a, rows_m, rows_t, acol

    def mixer1_attention(l, m, work):
        y, cq, ckv, kr, mx, mo, gi, gf, vz, uq, ukv = m
        sp_ = work.copy()
        conv, xc, qk, ws, absf, soft, lf, F, a, M, rows_a, rows_m, rows_t, acol = mlstm_buffers(sp_)
        cqn, ckvn = cq, ckv
        qn, qr, kn, vn = sp_.get(H, S), sp_.get(2, S), sp_.get(H, S), sp_.get(ST, S)
        tmp = sp_.get(S)
        prob = sp_.get(3, S)
        norm_space = sp_.copy()
        pT = sp_.get(2, ST, S)
        top, nmax, total, inv = sp_.get(16), sp_.get(16), sp_.get(16), sp_.get(16)
        N = H * ST
        score = [ps[b][:, :] for b in (0, 1, 6)]
        turned_src = [qr[:, 0, :], qr[:, 1, :], kr]
        with Stage() as st:
            nq = Norm(st, "nq", [cq[:, k, :] for k in range(3)], [cqn[:, k, :] for k in range(3)],
                      [col(c1, "q_norm", k) for k in range(3)], 384, norm_space, ps[6][:, :])
            nk = Norm(st, "nk", [ckv[:, k, :] for k in range(2)], [ckvn[:, k, :] for k in range(2)],
                      [col(c1, "kv_norm", k) for k in range(2)], 256, norm_space, ps[7][:, :])
            done, copied = st.sem("done"), st.sem("copied")
            turned, rotated = st.sem("turned"), st.sem("rotated")
            scores_ready, negmax_ready, exp_ready = st.sem("scores_ready"), st.sem("negmax_ready"), st.sem("exp_ready")
            probs_ready, pT_ready, pT_copied = st.sem("probs_ready"), st.sem("pT_ready"), st.sem("pT_copied")
            y_ready, y_copied = st.sem("y_ready"), st.sem("y_copied")
            landed, conv_ready, xc_ready, zeroed = st.sem("landed"), st.sem("conv_ready"), st.sem("xc_ready"), st.sem("zeroed")
            gate_in, gate_out, rows_ready, cols_done = (st.sem("gate_in"), st.sem("gate_out"), st.sem("rows_ready"),
                                                        st.sem("cols_done"))

            @st.block.sync
            def _(sp):
                sp.dma_start(ws.rearrange("p a b m -> p (a b m)"), t["mqk"][l, :, :]).then_inc(landed, 16)

            @st.block.tensor
            def _(pe):
                nq.pe(pe)
                nk.pe(pe)
                pe.wait_ge(nq.ready, 3)
                for j in range(14):
                    if j == 6:
                        pe.wait_ge(nk.ready, 2)
                    if j >= 4:
                        pe.wait_ge(copied, j - 3)
                    bank = ps[j % 4][:, :]
                    if j < 6:
                        mm = products(bank, lambda k: uq[:, k, j * P:(j + 1) * P], lambda k: cqn[:, k, :], 3)
                    elif j < 10:
                        mm = products(bank, lambda k: ukv[:, k, (j - 6) * P:(j - 5) * P], lambda k: ckvn[:, k, :], 2)
                    else:
                        mm = products(bank, lambda k: ckvn[:, k, (j - 10) * P:(j - 9) * P], lambda k: ukv[:, k, 512:1024], 2)
                    mm.then_inc(done, 1)
                pe.wait_ge(copied, 14)
                for r in range(3):
                    T.matmul(ps[4 + r][:, :], C("rot_mla"), turned_src[r], start=True, stop=True).then_inc(turned, 1)
                pe.wait_ge(landed, 16)
                for j in range(4):
                    a_, p = divmod(j, 2)
                    pe.wait_ge(xc_ready, p + 1)
                    T.matmul(ps[(14 + j) % 4][:, :], ws[:, a_, p, :], xc[:, p, :], start=True, stop=True).then_inc(done, 1)
                pe.wait_ge(rows_ready, 1)
                for j in range(ST):
                    mm = T.transpose(ps[7][:, 36 * j:36 * j + 36], rows_a[0:36, j * P:(j + 1) * P], C("ident")[0:36, 0:36])
                mm.then_inc(cols_done, 1)
                pe.wait_ge(copied, 18)
                pe.wait_ge(rotated, 3)
                for m in range(N + 3):
                    if m < N:
                        hd, i = divmod(m, ST)
                        q = slice(i * P, (i + 1) * P)
                        b = 64 * (hd % 2)
                        if m >= 3:
                            pe.wait_ge(exp_ready, m - 2)
                        T.matmul(score[m % 3], qn[:, hd, q], kn[:, hd, :], start=True, stop=False)
                        T.matmul(score[m % 3], qr[b:b + 64, hd // 2, q], kr[b:b + 64, :], start=False, stop=True) \
                         .then_inc(scores_ready, 1)
                    if 2 <= m < N + 2:
                        g = m - 2
                        pe.wait_ge(probs_ready, g + 1)
                        if g >= 2:
                            pe.wait_ge(pT_copied, g - 1)
                        for k in range(ST):
                            mm = T.transpose(ps[2 + g % 2][:, k * P:(k + 1) * P], prob[:, g % 3, k * P:(k + 1) * P],
                                             C("ident"))
                        mm.then_inc(pT_ready, 1)
                    if m >= 3:
                        hd, i = divmod(m - 3, ST)
                        if i == ST - 1:
                            pe.wait_ge(pT_copied, m - 2)
                            if hd >= 2:
                                pe.wait_ge(y_copied, hd - 1)
                            products(ps[4 + hd % 2][:, :], lambda k: vn[:, k, hd * P:(hd + 1) * P],
                                     lambda k: pT[:, hd % 2, k, :], ST).then_inc(y_ready, 1)

            @st.block.scalar
            def _(act):
                nq.square(act)
                nk.square(act)
                nq.take_root(act)
                nk.take_root(act)
                for j in range(14):
                    if j == 2:
                        act.wait_ge(gate_in, 1)
                        A.activation(soft[0:36, :], absf[0:36, :], ACT.Exp, scale=-1.0).then_inc(gate_out, 1)
                        act.wait_ge(gate_out, 1)
                        A.activation(soft[0:36, :], soft[0:36, :], ACT.Ln, bias=C("one", 36)).then_inc(gate_out, 1)
                    if j == 10:
                        act.wait_ge(gate_in, 2)
                        A.activation(M[0:36, :], M[0:36, :], ACT.Exp, scale=-1.0).then_inc(gate_out, 1)
                    if j == 5:
                        for c in range(2):
                            act.wait_ge(conv_ready, c + 1)
                            A.activation(xc[:, c, :], conv[:, c, :], ACT.Silu, bias=col(c1, "conv_b", c)).then_inc(xc_ready, 1)
                    act.wait_ge(done, j + 1)
                    dst = (qn[:, j, :] if j < 4 else qr[:, j - 4, :] if j < 6 else kn[:, j - 6, :] if j < 10
                           else vn[:, j - 10, :])
                    A.activation(dst, ps[j % 4][:, :], ACT.Copy).then_inc(copied, 1)
                for j in range(4):
                    act.wait_ge(done, 15 + j)
                    A.activation(qk[:, j // 2, j % 2, :], ps[(14 + j) % 4][:, :], ACT.Copy, scale=HD ** -0.5 if j < 2 else 1.0) \
                     .then_inc(copied, 1)
                act.wait_ge(cols_done, 1)
                A.activation(acol.rearrange("p j c -> p (j c)"), ps[7][:, 0:144], ACT.Copy)
                for m in range(N):
                    act.wait_ge(negmax_ready, m + 1)
                    if m >= 3:
                        act.wait_ge(pT_ready, m - 2)
                    A.activation(prob[:, m % 3, :], score[m % 3], ACT.Exp, scale=MLA_SCALE,
                                 bias=nmax[:, m:m + 1], accum_out=total[:, m:m + 1]).then_inc(exp_ready, 1)
                    if m % ST == 3 and m >= ST:
                        hd = m // ST - 1
                        act.wait_ge(y_ready, hd + 1)
                        A.activation(y[:, hd, :], ps[4 + hd % 2][:, :], ACT.Copy).then_inc(y_copied, 1)
                act.wait_ge(y_ready, H)
                A.activation(y[:, H - 1, :], ps[4 + (H - 1) % 2][:, :], ACT.Copy).then_inc(y_copied, 1)

            @st.block.vector
            def _(dve):
                order = Order(dve, st.sem("dve_order"))
                R = slice(0, 36)
                V.scalar_tensor_tensor(out=absf[R, :], in0=gf[R, :], scalar=-1.0, in1=gf[R, :], op0=ALU.mult, op1=ALU.max).then_inc(gate_in, 1)
                nq.add(dve)
                nk.add(dve)
                nq.invert(dve)
                nq.dve_finish(dve)
                nk.invert(dve)
                nk.dve_finish(dve)
                for c in range(2):
                    w_ = lambda k: col(c1, "conv_w", 5 * c + k)
                    order.done(V.tensor_scalar(conv[:, c, :], mx[:, c, 0:S], w_(0), None, ALU.mult))
                    for k in range(1, 5):
                        ins = V.scalar_tensor_tensor(out=conv[:, c, :], in0=mx[:, c, k:k + S], scalar=w_(k),
                                                     in1=conv[:, c, :], op0=ALU.mult, op1=ALU.add)
                        if k < 4:
                            order.done(ins)
                    ins.then_inc(conv_ready, 1)
                dve.wait_ge(gate_out, 2)
                order.done(V.scalar_tensor_tensor(out=lf[R, :], in0=gf[R, :], scalar=0.0, in1=soft[R, :], op0=ALU.min, op1=ALU.subtract))
                order.done(V.memset(absf[R, :], 1.0))
                order.done(V.tensor_tensor_scan(F[R, :], absf[R, :], lf[R, :], 0.0, ALU.mult, ALU.add))
                order.done(V.tensor_tensor(a[R, :], gi[R, :], F[R, :], ALU.subtract))
                order.done(V.tensor_tensor_scan(lf[R, :], absf[R, :], a[R, :], 0.0, ALU.mult, ALU.max))
                V.tensor_tensor(M[R, :], F[R, :], lf[R, :], ALU.add).then_inc(gate_in, 1)
                dve.wait_ge(gate_in, 2)
                order.done(V.tensor_scalar(F[R, :], lf[R, :], -1.0, None, ALU.mult))
                for m, (dst, src) in enumerate(((rows_a, a), (rows_m, F), (rows_t, M))):
                    if m == 2:
                        dve.wait_ge(gate_out, 3)
                    V.tensor_copy(dst[0:32, :], src[0:32, :]).then_inc(zeroed, 1)
                    dve.wait_ge(zeroed, m + 1)
                    V.tensor_copy(dst[32:36, :], src[32:36, ::-1]).then_inc(rows_ready, 1)
                for r in range(3):
                    dve.wait_ge(turned, r + 1)
                    rotate(dve, order, turned_src[r], ps[4 + r][:, :], 0, tmp).then_inc(rotated, 1)
                    dve.wait_ge(rotated, r + 1)
                for m in range(N + 3):
                    if m >= 3:
                        hd, i = divmod(m - 3, ST)
                        dve.wait_ge(pT_ready, m - 2)
                        if i == 0 and hd >= 2:
                            dve.wait_ge(y_ready, hd - 1)
                        V.tensor_copy(pT[:, hd % 2, :, i * P:(i + 1) * P],
                                      ps[2 + (m - 3) % 2][:, :].rearrange("p (k q) -> p k q", k=ST)).then_inc(pT_copied, 1)
                    if m < N:
                        dve.wait_ge(scores_ready, m + 1)
                        order.done(V.reduce_max(top[:, m:m + 1], score[m % 3], AX.X))
                        V.tensor_scalar(nmax[:, m:m + 1], top[:, m:m + 1], -MLA_SCALE, None, ALU.mult) \
                         .then_inc(negmax_ready, 1)
                    if 1 <= m <= N:
                        g = m - 1
                        dve.wait_ge(exp_ready, g + 1)
                        order.done(V.reciprocal(inv[:, g:g + 1], total[:, g:g + 1]))
                        V.tensor_scalar(prob[:, g % 3, :], prob[:, g % 3, :], inv[:, g:g + 1], None, ALU.mult) \
                         .then_inc(probs_ready, 1)

    def project_out(l, w_dram, y, gate=None):
        scope = Scope()
        x = Split(scope, "x", DT)
        with Stage() as st:
            w = Weights(st, scope)
            squares = SumOfSquares(st, scope.sb("square", [P, S])[:, :])
            y_high, y_low, done, added = st.sem("y_high"), st.sem("y_low"), st.sem("done"), st.sem("added")

            @st.block.sync
            def _(sp):
                for g in range(4):
                    w.load(sp, g % 2, g // 2, w_dram[l, g, :, :], g < 2)

            @st.block.tensor
            def _(pe):
                before = lambda k: pe.wait_ge(y_low, k + 1)
                for g in range(4):
                    b = g % 2
                    w.wait(pe, b, g // 2)
                    for a in range(2):
                        j = 2 * g + a
                        if j >= 4:
                            pe.wait_ge(added, j - 3)
                        wt = lambda part: lambda k: part[:, b, (a * DT + k) * P:(a * DT + k + 1) * P]
                        split_products(ps[j % 4][:, :], wt(w.hi), wt(w.lo), lambda k: x.hi[:, k, :], lambda k: x.lo[:, k, :],
                                       DT, before).then_inc(w.used if a else done, 1)
                        before = None

            @st.block.scalar
            def _(act):
                for k in range(DT):
                    A.activation(x.hi[:, k, :], y[:, k, :], ACT.Copy).then_inc(y_high, 1)
                    if k < 2:
                        w.high(act, k, 0, ITEM, True)
                for g in (2, 3):
                    w.high(act, g % 2, 1, ITEM)

            @st.block.vector
            def _(dve):
                for k in range(DT):
                    dve.wait_ge(y_high, k + 1)
                    V.tensor_tensor(x.lo[:, k, :], y[:, k, :], x.hi[:, k, :].bitcast(F32), ALU.subtract).then_inc(y_low, 1)
                    if k < 2:
                        w.low(dve, k, 0, ITEM)
                squares.start(dve)
                for j in range(DT):
                    dve.wait_ge(w.used if j % 2 else done, j // 2 + 1)
                    V.scalar_tensor_tensor(out=h[:, j, :], in0=ps[j % 4][:, :], scalar=1.0 if gate is None else gate[j],
                                           in1=h[:, j, :], op0=ALU.mult, op1=ALU.add).then_inc(added, 1)
                    if j in (1, 3):
                        w.low(dve, j // 2, 1, ITEM)
                    dve.wait_ge(added, j + 1)
                    squares.add(dve, h[:, j, :], j)
        scope.close()

    def embed_layer(l):
        scope = Scope()
        x = Split(scope, "x", DT)
        sp_ = scope.space(4096 + 1024 + 2048 + 1024 + 10 * S)
        e = sp_.get(DT, S)
        pt = sp_.get(2, S)
        wp = sp_.get(2, D)
        sig = sp_.get(2, S)
        with Stage() as st:
            w = Weights(st, scope)
            p_landed = st.sem("p_landed")
            e_done, e_copied, done, sig_ready = st.sem("e_done"), st.sem("e_copied"), st.sem("done"), st.sem("sig_ready")
            gated, added = st.sem("gated"), st.sem("added")
            ng_ = Norm(st, "norm", [h[:, k, :] for k in range(DT)], x,
                       [col(c1, "gate_norm", k) for k in range(DT)], D, sp_, ps[6][:, :], presummed=True)
            squares = SumOfSquares(st, sp_.get(S))
            ne = Norm(st, "ne", [e[:, k, :] for k in range(DT)], [e[:, k, :] for k in range(DT)],
                      [col(c1, "post_norm", k) for k in range(DT)], D, sp_, ps[7][:, :])

            @st.block.sync
            def _(sp):
                sp.dma_start(pt, t["p"][l, :, :].rearrange("(k p) s -> p k s", p=P)).then_inc(p_landed, 16)
                sp.dma_start(wp.rearrange("p k m -> p (k m)"), t["plep"][l, :, :]).then_inc(p_landed, 16)
                for g in range(4):
                    w.load(sp, g % 2, g // 2, t["pleg"][l, g, :, :], g < 2)

            @st.block.tensor
            def _(pe):
                ng_.pe(pe)
                pe.wait_ge(p_landed, 32)
                for j in range(DT):
                    if j >= 4:
                        pe.wait_ge(e_copied, j - 3)
                    products(ps[j % 4][:, :], lambda k: wp[:, k, j * P:(j + 1) * P], lambda k: pt[:, k, :], 2).then_inc(e_done, 1)
                pe.wait_ge(e_copied, DT)
                ne.pe(pe)
                before = ng_.tile_wait(pe)
                for g in range(4):
                    b = g % 2
                    w.wait(pe, b, g // 2)
                    for a in range(2):
                        j = 2 * g + a
                        if j >= 4:
                            pe.wait_ge(sig_ready, j - 3)
                        wt = lambda part: lambda k: part[:, b, (a * DT + k) * P:(a * DT + k + 1) * P]
                        split_products(ps[j % 4][:, :], wt(w.hi), wt(w.lo), lambda k: x.hi[:, k, :], lambda k: x.lo[:, k, :],
                                       DT, before).then_inc(w.used if a else done, 1)
                        before = None

            @st.block.scalar
            def _(act):
                ng_.square(act)
                ng_.take_root(act)
                for b in range(2):
                    w.high(act, b, 0, ITEM, True)
                ng_.act_finish(act)
                for j in range(DT):
                    act.wait_ge(e_done, j + 1)
                    A.activation(e[:, j, :], ps[j % 4][:, :], ACT.Copy).then_inc(e_copied, 1)
                act.wait_ge(e_copied, DT)
                ne.act(act)
                for j in range(DT):
                    act.wait_ge(w.used if j % 2 else done, j // 2 + 1)
                    if j >= 2:
                        act.wait_ge(gated, j - 1)
                    A.activation(sig[:, j % 2, :], ps[j % 4][:, :], ACT.Sigmoid).then_inc(sig_ready, 1)
                    if j in (1, 3):
                        w.high(act, j // 2, 1, ITEM)

            @st.block.vector
            def _(dve):
                ng_.add(dve)
                ng_.invert(dve)
                w.low(dve, 0, 0, ITEM)
                ng_.dve_finish(dve)
                w.low(dve, 1, 0, ITEM)
                ne.dve(dve)
                dve.wait_ge(ne.ready, DT)
                squares.start(dve)
                for j in range(DT):
                    dve.wait_ge(sig_ready, j + 1)
                    V.tensor_tensor(e[:, j, :], e[:, j, :], sig[:, j % 2, :], ALU.mult).then_inc(gated, 1)
                    dve.wait_ge(gated, j + 1)
                    V.tensor_tensor(h[:, j, :], h[:, j, :], e[:, j, :], ALU.add).then_inc(added, 1)
                    if j in (1, 3):
                        w.low(dve, j // 2, 1, ITEM)
                    dve.wait_ge(added, j + 1)
                    squares.add(dve, h[:, j, :], j)
        scope.close()

    def final_norm():
        scope = Scope()
        sp_ = scope.space(4 * S)
        with Stage() as st:
            norm = Norm(st, "norm", [h[:, k, :] for k in range(DT)], [h[:, k, :] for k in range(DT)],
                        [col(cg, "final_norm", k) for k in range(DT)], D, sp_, ps[6][:, :], presummed=True)
            squares = SumOfSquares(st, sp_.get(S))
            st.block.tensor(norm.pe)
            st.block.scalar(norm.act)

            @st.block.vector
            def _(dve):
                norm.dve(dve)
                squares.start(dve)
                for k in range(DT):
                    dve.wait_ge(norm.ready, k + 1)
                    squares.add(dve, h[:, k, :], k)
        scope.close()

    def mixer1_mlstm(l, m, work, spectrum):
        part, spec, dft, fw = spectrum
        y, cq, ckv, kr, mx, mo, gi, gf, vz, uq, ukv = m
        sp_ = work.copy()
        conv, xc, qk, ws, absf, soft, lf, F, a, M, rows_a, rows_m, rows_t, acol = mlstm_buffers(sp_)
        finish = sp_.copy()
        qks = sp_.get(2, 2, ST, S)
        wgt = sp_.get(4, S)
        thr, larger = conv, absf
        den, num = sp_.get(S), sp_.get(S)
        hsum = sp_.get(2, S)
        groups = [(p, d, e) for p in range(2) for d in range(2) for e in range(2)]
        steps = [(g, j) for g in range(8) for j in (range(ST) if groups[g][1] == 0 else range(ST - 1, -1, -1))]

        def head(a_, p, e, cols):
            return qk[64 * e:64 * e + 64, a_, p, cols]

        def span(g, j):
            return slice(j * P, S) if groups[g][1] == 0 else slice(0, (j + 1) * P)

        with Stage() as st:
            dft_landed, dft_done, dft_copied = st.sem("dft_landed"), st.sem("dft_done"), st.sem("dft_copied")
            evacuated = st.sem("evacuated")
            qk_done, qk_copied = st.sem("qk_done"), st.sem("qk_copied")
            m_spread, arg_ready, exp_ready, wgt_ready = (st.sem("m_spread"), st.sem("arg_ready"), st.sem("exp_ready"),
                                                         st.sem("wgt_ready"))
            used, t_spread, thr_ready, dir_ready = st.sem("used"), st.sem("t_spread"), st.sem("thr_ready"), st.sem("dir_ready")

            @st.block.sync
            def _(sp):
                sp.dma_start(dft.rearrange("p a j s -> p (a j s)"), t["dft"]).then_inc(dft_landed, 16)
                sp.dma_start(fw.rearrange("p a m -> p (a m)"), t["fnw"][l, :, :]).then_inc(dft_landed, 16)

            def fourier(pe, j):
                bank = ps[4][:, :]
                if j:
                    pe.wait_ge(dft_copied, j)
                else:
                    pe.wait_ge(dft_landed, 32)
                c = j // 2 if j < 4 else j % 2
                if j < 4:
                    mm = products(bank, lambda k: vz[:, k, 256 + c * P:256 + (c + 1) * P], lambda k: dft[:, j % 2, k, :], ST)
                elif j < 6:
                    mm = products(bank, lambda k: C("dft_s") if k else C("dft_c"), lambda k: part[:, c, k, :], 2)
                else:
                    mm = T.matmul(bank, fw[:, c, :], spec[:, c, :], start=True, stop=True)
                mm.then_inc(dft_done, 1)

            def fourier_copy(act, j):
                act.wait_ge(dft_done, j + 1)
                if j < 6:
                    ins = A.activation(part[:, j // 2, j % 2, :] if j < 4 else spec[:, j - 4, :], ps[4][:, :], ACT.Copy)
                else:
                    ins = A.activation(y[:, j, :], ps[4][:, :], ACT.Identity, bias=col(c1, "fnet_b", j - 6))
                ins.then_inc(dft_copied, 1)

            def scores(pe, m):
                p, hh, jj = m // 8, m // ST % 2, m % ST
                if m >= 2:
                    pe.wait_ge(qk_copied, m - 1)
                T.matmul(ps[m % 2][:, :], head(1, p, hh, slice(jj * P, (jj + 1) * P)), head(0, p, hh, slice(0, S)),
                         start=True, stop=True).then_inc(qk_done, 1)

            def scores_copy(act, m):
                act.wait_ge(qk_done, m + 1)
                A.activation(qks[:, m // 8, m // ST % 2, m % ST, :], ps[m % 2][:, :], ACT.Copy).then_inc(qk_copied, 1)

            @st.block.tensor
            def _(pe):
                for m in range(8):
                    scores(pe, m)
                for s_, (g, j) in enumerate(steps):
                    p, d, e = groups[g]
                    b = 64 * e
                    first = s_ % ST == 0
                    if first:
                        for g_ in ([0, 1] if g == 0 else [g + 1] if g < 7 else []):
                            p_, d_, e_ = groups[g_]
                            if g_ >= 2:
                                pe.wait_ge(arg_ready, ST * (g_ - 1))
                            c_ = 4 * d_ + 2 * p_ + e_
                            T.matmul(ps[2 + g_ % 2][:, :], C("sel", 36, c_ * P, (c_ + 1) * P), rows_m[0:36, :],
                                     start=True, stop=True).then_inc(m_spread, 1)
                        if e == 0:
                            if g:
                                pe.wait_ge(thr_ready, g // 2)
                            T.matmul(ps[7][:, :], C("selp", 36, (2 * d + p) * P, (2 * d + p + 1) * P), rows_t[0:36, :],
                                     start=True, stop=True).then_inc(t_spread, 1)
                    if first and e == 0 and g:
                        pe.wait_ge(evacuated, g)
                    pe.wait_ge(wgt_ready, s_ + 1)
                    r = span(g, j)
                    hd = 2 * p + e
                    T.matmul(ps[5][b:b + 64, r], vz[:, j, hd * HD:(hd + 1) * HD], wgt[:, s_ % 4, r], start=first,
                             stop=(s_ % ST == ST - 1))
                    T.matmul(ps[6][b:b + 64, r], C("ones")[:, 0:HD], wgt[:, s_ % 4, r], start=first,
                             stop=(s_ % ST == ST - 1)).then_inc(used, 1)
                    if first:
                        fourier(pe, g)
                        if g < 4:
                            scores(pe, 8 + 2 * g)
                            scores(pe, 9 + 2 * g)

            def evacuate(act, q):
                act.wait_ge(used, 2 * ST * q)
                if q >= 2:
                    act.wait_ge(dir_ready, q - 1)
                A.activation(num, ps[5][:, :], ACT.Copy).then_inc(evacuated, 1)
                A.activation(den, ps[6][:, :], ACT.Copy).then_inc(evacuated, 1)

            @st.block.scalar
            def _(act):
                for m in range(8):
                    scores_copy(act, m)
                for s_, (g, j) in enumerate(steps):
                    p, d, e = groups[g]
                    first = s_ % ST == 0
                    if first and e == 0:
                        act.wait_ge(t_spread, g // 2 + 1)
                        if g >= 4:
                            act.wait_ge(dir_ready, g // 2 - 1)
                        A.activation(thr[:, g // 2 % 2, :], ps[7][:, :], ACT.Copy).then_inc(thr_ready, 1)
                    act.wait_ge(arg_ready, s_ + 1)
                    A.activation(wgt[:, s_ % 4, span(g, j)], wgt[:, s_ % 4, span(g, j)], ACT.Exp).then_inc(exp_ready, 1)
                    if s_ and s_ % (2 * ST) == 0:
                        evacuate(act, g // 2)
                    if s_ % ST == ST - 1:
                        fourier_copy(act, g)
                        if g < 4:
                            scores_copy(act, 8 + 2 * g)
                            scores_copy(act, 9 + 2 * g)

                evacuate(act, 4)

            order = Order(V, st.sem("dve_order"))

            def divide(dve, q):
                p, d = divmod(q - 1, 2)
                dve.wait_ge(evacuated, 2 * q)
                dve.wait_ge(thr_ready, q)
                order.done(V.scalar_tensor_tensor(out=larger, in0=den, scalar=-1.0, in1=thr[:, (q - 1) % 2, :],
                                                  op0=ALU.mult, op1=ALU.max))
                order.done(V.tensor_tensor(den, den, larger, ALU.max))
                order.done(V.reciprocal(den, den))
                if d == 0:
                    V.tensor_tensor(hsum[:, p, :], num, den, ALU.mult).then_inc(dir_ready, 1)
                else:
                    order.done(V.tensor_tensor(num, num, den, ALU.mult))
                    V.tensor_tensor(hsum[:, p, :], hsum[:, p, :], num, ALU.add).then_inc(dir_ready, 1)
                dve.wait_ge(dir_ready, q)

            @st.block.vector
            def _(dve):
                order.eng = dve
                for s_ in range(len(steps) + 1):
                    if s_ < len(steps):
                        g, j = steps[s_]
                        p, d, e = groups[g]
                        r = span(g, j)
                        if s_ % ST == 0:
                            dve.wait_ge(m_spread, g + 1)
                        if s_ >= 4:
                            dve.wait_ge(used, s_ - 3)
                        rc = 32 * d + 2 * p + e
                        V.tensor_scalar(wgt[:, s_ % 4, r], ps[2 + g % 2][:, r], acol[:, j, rc:rc + 1], 0.0, ALU.add, ALU.min) \
                         .then_inc(arg_ready, 1)
                    if s_ >= 1:
                        g, j = steps[s_ - 1]
                        p, d, e = groups[g]
                        r = span(g, j)
                        dve.wait_ge(exp_ready, s_)
                        if (s_ - 1) % 16 == 0:
                            dve.wait_ge(qk_copied, 8 * p + 8)
                        wx = wgt[:, (s_ - 1) % 4, :]
                        order.done(V.tensor_tensor(wx[:, r], wx[:, r], qks[:, p, e, j, r], ALU.mult))
                        dg = slice(j * P, (j + 1) * P)
                        V.tensor_tensor(wx[:, dg], wx[:, dg], C("upto") if d == 0 else C("from"), ALU.mult) \
                         .then_inc(wgt_ready, 1)
                        if s_ > 2 * ST and s_ % (2 * ST) == 2:
                            divide(dve, s_ // (2 * ST))
                divide(dve, 4)

        outn, sig = finish.get(2, S), finish.get(2, S)
        with Stage() as st:
            norms = [Norm(st, f"nh{p}", [hsum[:, p, :]], [outn[:, p, :]], [col(c1, "head_norm", p)], HD, finish, ps[p][:, :],
                          lhs="heads") for p in range(2)]
            sig_ready, skipped = st.sem("sig_ready"), st.sem("skipped")

            @st.block.tensor
            def _(pe):
                for x in norms:
                    x.pe(pe)

            @st.block.scalar
            def _(act):
                for x in norms:
                    x.act(act)
                A.activation(sig.rearrange("p a s -> p (a s)"), mo.rearrange("p a s -> p (a s)"), ACT.Sigmoid).then_inc(sig_ready, 1)

            @st.block.vector
            def _(dve):
                for p, x in enumerate(norms):
                    x.dve(dve)
                for p, x in enumerate(norms):
                    dve.wait_ge(x.ready, 1)
                    V.scalar_tensor_tensor(out=outn[:, p, :], in0=xc[:, p, :], scalar=col(c1, "skip", p), in1=outn[:, p, :],
                                           op0=ALU.mult, op1=ALU.add).then_inc(skipped, 1)
                dve.wait_ge(sig_ready, 1)
                dve.wait_ge(skipped, 2)
                V.tensor_tensor(y[:, 4:6, :].rearrange("p a s -> p (a s)"), outn.rearrange("p a s -> p (a s)"),
                                sig.rearrange("p a s -> p (a s)"), ALU.mult)

    modc = mod[:, 0, :]
    gain_m, gain_f = mod[:, 1, 0:8], mod[:, 1, 8:16]
    lbc = mod[:, 1, 16:22]

    def adaptive(l):
        with Stage() as st:
            p_landed = st.sem("p_landed")

            @st.block.sync
            def _(sp):
                sp.dma_start(par[:, 0:n2], t["par2"][l, :, :]).then_inc(p_landed, 16)

            @st.block.vector
            def _(dve):
                order = Order(dve, st.sem("dve_order"))
                order.done(V.tensor_copy(lbc, lbt[:, bass.ds(l, 1), :, :].rearrange("p a b c -> p (a b c)")))
                dve.wait_ge(p_landed, 16)
                ab = c2["ada_b"][0]
                order.done(V.tensor_tensor(modc, ada[:, bass.ds(l, 1), :].rearrange("p a c -> p (a c)"), par[:, ab:ab + 48], ALU.add))
                for dst, name, at in ((gain_m, "norm_mix", 8), (gain_f, "norm_ffn", 32)):
                    g0 = c2[name][0]
                    order.done(V.scalar_tensor_tensor(out=dst, in0=modc[:, at:at + 8], scalar=1.0, in1=par[:, g0:g0 + 8],
                                                      op0=ALU.add, op1=ALU.mult))

    def mixer2_buffers(scope):
        m = scope.space(16530)
        y = m.get(DT, S)
        aq = m.get(4, S)
        ak = m.get(P + S)
        bq, bf, bg = m.get(2, S), m.get(2, S), m.get(2, S)
        cx = m.get(6, S + 3)
        cgt = m.get(2, S)
        cb, ca = m.get(S), m.get(S)
        vn = m.get(ST, 384)
        return y, aq, ak, bq, bf, bg, cx, cgt, cb, ca, vn

    def mixer2_project(l, m):
        y, aq, ak, bq, bf, bg, cx, cgt, cb, ca, vn = m
        scope = Scope()
        x = Split(scope, "x", DT)
        sp_ = scope.space(5 * S)
        dst = ([aq[:, k, :] for k in range(4)] + [ak[:, P:P + S]] + [bq[:, k, :] for k in range(2)]
               + [bf[:, k, :] for k in range(2)] + [bg[:, k, :] for k in range(2)]
               + [cx[:, k, 3:3 + S] for k in range(6)] + [cgt[:, k, :] for k in range(2)])
        sizes = [ITEM] * 10 + [DT * 192] * 2
        with Stage() as st:
            w = Weights(st, scope)
            norm = Norm(st, "norm", [h[:, k, :] for k in range(DT)], x,
                        [gain_m[:, k:k + 1] for k in range(DT)], D, sp_, ps[6][:, :],
                        shifts=[modc[:, k:k + 1] for k in range(DT)], presummed=True)
            done, copied = st.sem("done"), st.sem("copied")

            @st.block.sync
            def _(sp):
                for g in range(12):
                    w.load(sp, g % 2, g // 2, t["in2_t"][l, g, :, :] if g < 10 else t["in2_r"][l, g - 10, :, :], g < 2)

            @st.block.gpsimd
            def _(pool):
                G.memset(ak[:, 0:P], 0.0)
                G.memset(cx[:, :, 0:3], 0.0)

            @st.block.tensor
            def _(pe):
                norm.pe(pe)
                before = norm.tile_wait(pe)
                for g in range(10):
                    b = g % 2
                    w.wait(pe, b, g // 2)
                    for a in range(2):
                        j = 2 * g + a
                        if j >= 4:
                            pe.wait_ge(copied, j - 3)
                        wt = lambda part: lambda k: part[:, b, (a * DT + k) * P:(a * DT + k + 1) * P]
                        split_products(ps[j % 4][:, :], wt(w.hi), wt(w.lo), lambda k: x.hi[:, k, :], lambda k: x.lo[:, k, :],
                                       DT, before).then_inc(w.used if a else done, 1)
                        before = None
                for g in (10, 11):
                    b = g % 2
                    w.wait(pe, b, g // 2)
                    for j in range(ST):
                        q = slice(j * P, (j + 1) * P)
                        wt = lambda part: lambda k: part[:, b, k * 192:(k + 1) * 192]
                        mm = split_products(ps[4 + j][:, (g - 10) * 192:(g - 9) * 192], lambda k: x.hi[:, k, q],
                                            lambda k: x.lo[:, k, q], wt(w.hi), wt(w.lo), DT)
                    mm.then_inc(w.used, 1)

            @st.block.scalar
            def _(act):
                norm.square(act)
                norm.take_root(act)
                for b in range(2):
                    w.high(act, b, 0, sizes[b], True)
                norm.act_finish(act)
                for g in range(12):
                    for a in range(2 if g < 10 else 0):
                        j = 2 * g + a
                        act.wait_ge(w.used if a else done, g + 1)
                        bank = ps[j % 4]
                        if j < 19:
                            A.activation(dst[j], bank[:, :], ACT.Copy).then_inc(copied, 1)
                        else:
                            A.activation(cb[0:4, :], bank[0:4, :], ACT.Copy)
                            A.activation(ca[0:4, :], bank[32:36, :], ACT.Copy).then_inc(copied, 1)
                    if g + 2 < 12:
                        w.high(act, g % 2, g // 2 + 1, sizes[g + 2])
                act.wait_ge(w.used, 12)
                for j in range(ST):
                    A.activation(vn[:, j, :], ps[4 + j][:, 0:384], ACT.Copy)

            @st.block.vector
            def _(dve):
                norm.add(dve)
                norm.invert(dve)
                w.low(dve, 0, 0, sizes[0])
                norm.dve_finish(dve)
                w.low(dve, 1, 0, sizes[1])
                for g in range(2, 12):
                    w.low(dve, g % 2, g // 2, sizes[g])
        scope.close()

    def hgrn_buffers(sp_):
        return [sp_.get(2, S) for _ in range(7)]

    def mixer2_window(l, m, work):
        y, aq, ak, bq, bf, bg, cx, cgt, cb, ca, vn = m
        sp_ = work.copy()
        cv = sp_.get(6, S)
        az, sp2, B, mxv, lf, kk, cum = hgrn_buffers(sp_)
        flat = lambda a: a.rearrange("p c s -> p (c s)")
        taps = sp_.get(2, S)
        tmp = sp_.get(S)
        sc = sp_.get(3, ST, 2 * P)
        pT = sp_.get(2, ST, 2, P)
        top, nmax, total, esink, inv = [sp_.get(8, ST) for _ in range(5)]
        heads = [(j, f) for j in range(4) for f in range(2)]
        x = [aq[:, j, :] for j in range(4)] + [ak[:, P:P + S]]
        with Stage() as st:
            norms = HeadNorms(st, x, [col(c2, "q_norm" if r < 4 else "k_norm") for r in range(5)], HD, sp_)
            f_in, f_out = st.sem("f_in"), st.sem("f_out")
            conv_ready, tap_ready = st.sem("conv_ready"), st.sem("tap_ready")

            @st.block.gpsimd
            def _(pool):
                order = Order(pool, st.sem("pool_order"))
                for c in range(6):
                    w_ = lambda k: col(c2, "conv_w", 4 * c + k)
                    G.tensor_scalar(cv[:, c, :], cx[:, c, 0:S], w_(0), None, ALU.mult).then_inc(tap_ready, 1)
                    for k in range(1, 4):
                        G.tensor_scalar(taps[:, k % 2, :], cx[:, c, k:k + S], w_(k), None, ALU.mult).then_inc(tap_ready, 1)
                        pool.wait_ge(tap_ready, 4 * c + k + 1)
                        ins = G.tensor_tensor(cv[:, c, :], cv[:, c, :], taps[:, k % 2, :], ALU.add)
                        order.done(ins)
                    pool.sem_inc(conv_ready, 1)
            turned, rotated = st.sem("turned"), st.sem("rotated")
            scores_ready, negmax_ready, exp_ready = st.sem("scores_ready"), st.sem("negmax_ready"), st.sem("exp_ready")
            masked, probs_ready = st.sem("masked"), st.sem("probs_ready")
            pT_ready, pT_copied, y_ready, y_copied = (st.sem("pT_ready"), st.sem("pT_copied"), st.sem("y_ready"),
                                                      st.sem("y_copied"))

            @st.block.tensor
            def _(pe):
                norms.pe(pe)
                for r in range(5):
                    pe.wait_ge(norms.ready, r + 1)
                    if r >= 3:
                        pe.wait_ge(rotated, r - 2)
                    T.matmul(ps[5 + r % 3][:, :], C("rot_win"), x[r], start=True, stop=True).then_inc(turned, 1)
                pe.wait_ge(rotated, 5)
                for m in range(11):
                    if m < 8:
                        j, f = heads[m]
                        b = 64 * f
                        if m >= 2:
                            pe.wait_ge(masked, 2 * m - 2)
                        for q in range(ST):
                            mm = T.matmul(ps[2 * (m % 2) + q // 2][:, (q % 2) * 256:(q % 2) * 256 + 256],
                                          aq[b:b + 64, j, q * P:(q + 1) * P], ak[b:b + 64, q * P:(q + 2) * P],
                                          start=True, stop=True)
                        mm.then_inc(scores_ready, 1)
                    if 2 <= m < 10:
                        g = m - 2
                        pe.wait_ge(probs_ready, ST * (g + 1))
                        if g:
                            pe.wait_ge(pT_copied, 2 * g)
                        for q in range(ST):
                            for a in range(2):
                                mm = T.transpose(ps[4 + q // 2][:, (q % 2) * 256 + a * P:(q % 2) * 256 + (a + 1) * P],
                                                 sc[:, g % 3, q, a * P:(a + 1) * P], C("ident"))
                        mm.then_inc(pT_ready, 1)
                    if m >= 3:
                        g = m - 3
                        j, f = heads[g]
                        b = 64 * f
                        pe.wait_ge(pT_copied, 2 * g + 2)
                        if g >= 2:
                            pe.wait_ge(y_copied, g - 1)
                        for q in range(ST):
                            for a in range(0 if q else 1, 2):
                                mm = T.matmul(ps[6 + g % 2][b:b + 64, q * P:(q + 1) * P],
                                              vn[:, q - 1 + a, f * HD:(f + 1) * HD], pT[:, g % 2, q, a, :],
                                              start=(a == 0 or q == 0), stop=(a == 1))
                        mm.then_inc(y_ready, 1)

            @st.block.scalar
            def _(act):
                norms.square(act)
                norms.take_root(act)
                act.wait_ge(f_in, 1)
                A.activation(flat(sp2), flat(az), ACT.Exp, scale=-1.0).then_inc(f_out, 1)
                act.wait_ge(f_out, 1)
                A.activation(flat(sp2), flat(sp2), ACT.Ln, bias=C("one")).then_inc(f_out, 1)
                act.wait_ge(f_in, 2)
                A.activation(flat(az), flat(az), ACT.Exp).then_inc(f_out, 1)
                act.wait_ge(f_out, 3)
                A.activation(flat(az), flat(az), ACT.Ln, bias=C("one")).then_inc(f_out, 1)
                A.activation(flat(kk), flat(bf), ACT.Sigmoid, scale=-1.0).then_inc(f_out, 1)
                sk = c2["sinks"][0]
                for m in range(11):
                    if m < 8:
                        act.wait_ge(negmax_ready, m + 1)
                        for q in range(ST):
                            A.activation(sc[:, m % 3, q, :], sc[:, m % 3, q, :], ACT.Exp, bias=nmax[:, m, q:q + 1],
                                         accum_out=total[:, m, q:q + 1])
                        A.activation(esink[:, m, :], nmax[:, m, :], ACT.Exp, bias=par[:, sk + m:sk + m + 1]) \
                         .then_inc(exp_ready, 1)
                    if 2 <= m < 10:
                        g = m - 2
                        act.wait_ge(pT_ready, g + 1)
                        if g >= 2:
                            act.wait_ge(y_ready, g - 1)
                        for a in range(2):
                            A.activation(pT[:, g % 2, 2 * a:2 * a + 2, :, :].rearrange("p q a k -> p (q a k)"),
                                         ps[4 + a][:, :], ACT.Copy).then_inc(pT_copied, 1)
                    if m >= 3:
                        g = m - 3
                        j, f = heads[g]
                        act.wait_ge(y_ready, g + 1)
                        A.activation(y[64 * f:64 * f + 64, j, :], ps[6 + g % 2][64 * f:64 * f + 64, :], ACT.Copy) \
                         .then_inc(y_copied, 1)
                for c in range(6):
                    act.wait_ge(conv_ready, c + 1)
                    A.activation(cv[:, c, :], cv[:, c, :], ACT.Silu)

            @st.block.vector
            def _(dve):
                order = Order(dve, st.sem("dve_order"))
                ln_lb, ln_1m, one_m = lbc[:, 0:2], lbc[:, 2:4], lbc[:, 4:6]
                V.scalar_tensor_tensor(out=flat(az), in0=flat(bf), scalar=-1.0, in1=flat(bf), op0=ALU.mult, op1=ALU.max) \
                 .then_inc(f_in, 1)
                norms.dve(dve)
                dve.wait_ge(f_out, 2)
                order.done(V.scalar_tensor_tensor(out=flat(B), in0=flat(bf), scalar=0.0, in1=flat(sp2), op0=ALU.min, op1=ALU.subtract))
                for c in range(2):
                    order.done(V.tensor_scalar(B[:, c, :], B[:, c, :], ln_1m[:, c:c + 1], None, ALU.add))
                    order.done(V.tensor_scalar(mxv[:, c, :], B[:, c, :], ln_lb[:, c:c + 1], None, ALU.max))
                    order.done(V.scalar_tensor_tensor(out=az[:, c, :], in0=B[:, c, :], scalar=ln_lb[:, c:c + 1],
                                                      in1=mxv[:, c, :], op0=ALU.min, op1=ALU.subtract))
                dve.sem_inc(f_in, 1)
                for r in range(5):
                    dve.wait_ge(turned, r + 1)
                    rotate(dve, order, x[r], ps[5 + r % 3][:, :], 2, tmp).then_inc(rotated, 1)
                    dve.wait_ge(rotated, r + 1)
                sk = c2["sinks"][0]
                for m in range(9):
                    if m < 8:
                        dve.wait_ge(scores_ready, m + 1)
                        if m >= 3:
                            dve.wait_ge(pT_ready, m - 2)
                        for a in range(2):
                            V.scalar_tensor_tensor(out=sc[:, m % 3, 2 * a:2 * a + 2, :].rearrange("p q k -> p (q k)"),
                                                   in0=ps[2 * (m % 2) + a][:, :], scalar=HD ** -0.5,
                                                   in1=C("window", None, 256 * a, 256 * a + 512),
                                                   op0=ALU.mult, op1=ALU.add).then_inc(masked, 1)
                        dve.wait_ge(masked, 2 * m + 2)
                        order.done(V.reduce_max(top[:, m, :], sc[:, m % 3, :, :], AX.X))
                        V.tensor_scalar(nmax[:, m, :], top[:, m, :], par[:, sk + m:sk + m + 1], -1.0, ALU.max, ALU.mult) \
                         .then_inc(negmax_ready, 1)
                    if m == 1:
                        dve.wait_ge(f_out, 4)
                        order.done(V.tensor_tensor(flat(lf), flat(mxv), flat(az), ALU.add))
                        for c in range(2):
                            order.done(V.tensor_tensor_scan(cum[:, c, :], C("restart"), lf[:, c, :], 0.0, ALU.mult, ALU.add))
                        dve.wait_ge(f_out, 5)
                        for c in range(2):
                            V.tensor_scalar(kk[:, c, :], kk[:, c, :], one_m[:, c:c + 1], None, ALU.mult)
                    if m >= 1:
                        g = m - 1
                        dve.wait_ge(exp_ready, m)
                        order.done(V.tensor_tensor(inv[:, g, :], total[:, g, :], esink[:, g, :], ALU.add))
                        order.done(V.reciprocal(inv[:, g, :], inv[:, g, :]))
                        for q in range(ST):
                            V.tensor_scalar(sc[:, g % 3, q, :], sc[:, g % 3, q, :], inv[:, g, q:q + 1], None, ALU.mult) \
                             .then_inc(probs_ready, 1)

    def head_output(st, sp_, tag, src, gain, gate, y, y_at, tmp):
        norms = [Norm(st, f"{tag}{c}", [src[:, c, :]], [src[:, c, :]], [gain], HD, sp_, ps[c][:, :], lhs="heads")
                 for c in range(2)]
        gate_ready = st.sem(tag + "_gate")

        def pe_(pe):
            for x in norms:
                x.pe(pe)

        def act_(act):
            for x in norms:
                x.act(act)
            A.activation(tmp, gate, ACT.Silu).then_inc(gate_ready, 1)

        def dve_(dve):
            for x in norms:
                x.dve(dve)
            dve.wait_ge(gate_ready, 1)
            for c, x in enumerate(norms):
                dve.wait_ge(x.ready, 1)
                V.tensor_tensor(y[:, y_at + c, :], src[:, c, :], tmp[:, c, :], ALU.mult)

        return pe_, act_, dve_

    def mixer2_hgrn(l, m, work):
        y, aq, ak, bq, bf, bg, cx, cgt, cb, ca, vn = m
        sp_ = work.copy()
        sp_.get(6, S)
        finish = sp_.copy()
        az, sp2, B, mxv, lf, kk, cum = hgrn_buffers(sp_)
        E = sp_.get(2, S)
        X = sp_.get(2, S)
        diag = sp_.get(H, ST, P)
        off = sp_.get(H, 6 * P)
        et = sp_.get(2, ST)
        qd, kd, far = sp_.get(2, S), sp_.get(2, S), sp_.get(2, 2, P)
        o = sp_.get(2, S)
        flat = lambda a: a.rearrange("p c s -> p (c s)")
        NL = len(LEVELS)
        steps = [(v, c) for v in range(NL) for c in range(2)]

        def halves(a, c, L):
            v = a[:, c, :].rearrange("p (b a k) -> p b a k", a=2, k=L)
            return v[:, :, 0, :], v[:, :, 1, :]

        with Stage() as st:
            diff_ready, decay_ready, x_ready = st.sem("diff_ready"), st.sem("decay_ready"), st.sem("x_ready")
            own_done, own_copied = st.sem("own_done"), st.sem("own_copied")
            lev_done, lev_copied = st.sem("lev_done"), st.sem("lev_copied")
            tail_in, tail_exp, tail_ready = st.sem("tail_in"), st.sem("tail_exp"), st.sem("tail_ready")
            off_done, off_copied, o_done = st.sem("off_done"), st.sem("off_copied"), st.sem("o_done")

            @st.block.scalar
            def _(act):
                for i in range(len(steps)):
                    act.wait_ge(diff_ready, 2 * i + 2)
                    A.activation(E[:, i % 2, :], E[:, i % 2, :], ACT.Exp).then_inc(decay_ready, 1)
                act.wait_ge(tail_in, 2)
                A.activation(flat(kd), flat(kd), ACT.Exp).then_inc(tail_exp, 1)
                A.activation(flat(qd), flat(cum), ACT.Exp).then_inc(tail_exp, 1)
                A.activation(et, cum.rearrange("p c (j k) -> p c j k", k=P)[:, :, :, P - 1], ACT.Exp).then_inc(tail_exp, 1)
                for hd in range(H):
                    act.wait_ge(off_done, hd + 1)
                    b0 = 4 * (hd % 2)
                    A.activation(off[:, hd, 0:512], ps[b0][:, :], ACT.Copy).then_inc(off_copied, 1)
                    A.activation(off[:, hd, 512:768], ps[b0 + 1][:, 0:256], ACT.Copy).then_inc(off_copied, 1)
                for c in range(2):
                    act.wait_ge(o_done, c + 1)
                    A.activation(o[:, c, :], ps[2 + 4 * c][:, :], ACT.Copy)

            @st.block.vector
            def _(dve):
                order = Order(dve, st.sem("dve_order"))
                V.memset(et, 0.0).then_inc(x_ready, 1)
                for hd in range(H):
                    dve.wait_ge(own_done, hd + 1)
                    V.tensor_tensor(diag[:, hd, :, :], ps[hd][:, :].rearrange("p (j k) -> p j k", k=P),
                                    C("ident").unsqueeze(1).to_broadcast([P, ST, P]), ALU.mult).then_inc(own_copied, 1)
                dve.wait_ge(own_copied, H)
                for i in range(len(steps) + 2):
                    if i < len(steps):
                        v, c = steps[i]
                        L = LEVELS[v]
                        c0, c1_ = halves(cum, c, L)
                        e0, e1 = halves(E[:, i % 2:i % 2 + 1, :], 0, L)
                        mid = c0[:, :, L - 1:L].to_broadcast([P, S // (2 * L), L])
                        if i >= 2:
                            dve.wait_ge(x_ready, 2 * i - 1)
                        V.tensor_tensor(e0, mid, c0, ALU.subtract).then_inc(diff_ready, 1)
                        V.tensor_tensor(e1, c1_, mid, ALU.subtract).then_inc(diff_ready, 1)
                    if 1 <= i <= len(steps):
                        g = i - 1
                        v, c = steps[g]
                        L = LEVELS[v]
                        e0, e1 = halves(E[:, g % 2:g % 2 + 1, :], 0, L)
                        x0, x1 = halves(X[:, g % 2:g % 2 + 1, :], 0, L)
                        k0, _ = halves(kk, c, L)
                        _, q1 = halves(bq, c, L)
                        dve.wait_ge(decay_ready, i)
                        if g >= 2:
                            dve.wait_ge(lev_done, 2 * g - 2)
                        V.tensor_tensor(x0, e0, k0, ALU.mult).then_inc(x_ready, 1)
                        V.tensor_tensor(x1, e1, q1, ALU.mult).then_inc(x_ready, 1)
                    if i >= 2:
                        g = i - 2
                        v, c = steps[g]
                        lev = C("levels", None, v * P, (v + 1) * P).bitcast(I32)
                        for e in range(2):
                            hd = 2 * c + e
                            dve.wait_ge(lev_done, 2 * g + e + 1)
                            if v:
                                dve.wait_ge(lev_copied, 2 * (g - 2) + e + 1)
                            V.copy_predicated(diag[:, hd, :, :], lev.unsqueeze(1).to_broadcast([P, ST, P]),
                                              ps[4 + 2 * (g % 2) + e][:, :].rearrange("p (j k) -> p j k", k=P)) \
                             .then_inc(lev_copied, 1)
                for c in range(2):
                    cv = cum[:, c, :].rearrange("p (j k) -> p j k", k=P)
                    V.tensor_tensor(kd[:, c, :].rearrange("p (j k) -> p j k", k=P), cv[:, :, P - 1:P].to_broadcast([P, ST, P]),
                                    cv, ALU.subtract).then_inc(tail_in, 1)
                dve.wait_ge(tail_exp, 3)
                order.done(V.tensor_tensor(flat(kd), flat(kd), flat(kk), ALU.mult))
                order.done(V.tensor_tensor(flat(qd), flat(qd), flat(bq), ALU.mult))
                for c in range(2):
                    V.tensor_scalar(far[:, c, 0, :], kd[:, c, 0:P], et[:, c, 1:2], None, ALU.mult).then_inc(tail_ready, 1)
                    V.tensor_scalar(far[:, c, 1, :], qd[:, c, 3 * P:S], et[:, c, 2:3], None, ALU.mult).then_inc(tail_ready, 1)

            @st.block.tensor
            def _(pe):
                for hd in range(H):
                    r = slice(64 * (hd % 2), 64 * (hd % 2) + 64)
                    for j in range(ST):
                        q = slice(j * P, (j + 1) * P)
                        mm = T.matmul(ps[hd][:, q], kk[r, hd // 2, q], bq[r, hd // 2, q], start=True, stop=True)
                    mm.then_inc(own_done, 1)
                for g, (v, c) in enumerate(steps):
                    pe.wait_ge(x_ready, 2 * g + 3)
                    for e in range(2):
                        if g >= 2:
                            pe.wait_ge(lev_copied, 2 * (g - 2) + e + 1)
                        r = slice(64 * e, 64 * e + 64)
                        for j in range(ST):
                            q = slice(j * P, (j + 1) * P)
                            mm = T.matmul(ps[4 + 2 * (g % 2) + e][:, q], X[r, g % 2, q], X[r, g % 2, q], start=True, stop=True)
                        mm.then_inc(lev_done, 1)
                pe.wait_ge(tail_ready, 4)
                pe.wait_ge(lev_copied, 4 * NL)
                for hd in range(H):
                    c, e = divmod(hd, 2)
                    r = slice(64 * e, 64 * e + 64)
                    b0 = 4 * (hd % 2)
                    if hd >= 2:
                        pe.wait_ge(off_copied, 2 * (hd - 2) + 2)
                    T.matmul(ps[b0][:, 0:P], kd[r, c, 0:P], qd[r, c, P:2 * P], start=True, stop=True)
                    T.matmul(ps[b0][:, P:2 * P], kd[r, c, 2 * P:3 * P], qd[r, c, 3 * P:S], start=True, stop=True)
                    for a, (lhs, bank, at) in enumerate(((far[r, c, 0, :], ps[b0], 2 * P), (kd[r, c, P:2 * P], ps[b0 + 1], 0))):
                        T.matmul(bank[:, at:at + P], lhs, qd[r, c, 2 * P:3 * P], start=True, stop=True)
                        mm = T.matmul(bank[:, at + P:at + 2 * P], lhs, far[r, c, 1, :], start=True, stop=True)
                    mm.then_inc(off_done, 1)
                for hd in range(H):
                    c, e = divmod(hd, 2)
                    pe.wait_ge(off_copied, 2 * hd + 2)
                    out = ps[2 + 4 * c][64 * e:64 * e + 64, :]
                    v_ = lambda j: vn[:, j, P + hd * HD:P + (hd + 1) * HD]
                    T.matmul(out[:, 0:P], v_(0), diag[:, hd, 0, :], start=True, stop=True)
                    T.matmul(out[:, P:2 * P], v_(0), off[:, hd, 0:P], start=True, stop=False)
                    T.matmul(out[:, P:2 * P], v_(1), diag[:, hd, 1, :], start=False, stop=True)
                    T.matmul(out[:, 2 * P:S], v_(0), off[:, hd, 2 * P:4 * P], start=True, stop=False)
                    T.matmul(out[:, 2 * P:S], v_(1), off[:, hd, 4 * P:6 * P], start=False, stop=False)
                    T.matmul(out[:, 2 * P:3 * P], v_(2), diag[:, hd, 2, :], start=False, stop=False)
                    T.matmul(out[:, 3 * P:S], v_(2), off[:, hd, P:2 * P], start=False, stop=False)
                    mm = T.matmul(out[:, 3 * P:S], v_(3), diag[:, hd, 3, :], start=False, stop=True)
                    if e:
                        mm.then_inc(o_done, 1)

        with Stage() as st:
            p_, a_, v_ = head_output(st, finish, "hg", o, col(c2, "hgrn_norm"), bg, y, 4, qd)
            st.block.tensor(p_)
            st.block.scalar(a_)
            st.block.vector(v_)

    def mixer2_delta(l, m, work):
        y, aq, ak, bq, bf, bg, cx, cgt, cb, ca, vn = m
        sp_ = work.copy()
        cv = sp_.get(6, S)
        rowg, rowG, rs1, rs2 = [sp_.get(S) for _ in range(4)]
        rowc = sp_.get(S)
        cols = sp_.get(ST, 68)
        ecol = sp_.get(ST, 12)
        gm, Lm, kb = sp_.get(2, S), sp_.get(2, S), sp_.get(2, S)
        finish = sp_.copy()
        AT, qkT = sp_.get(H, ST, P), sp_.get(H, ST, P)
        Tn, Tt = sp_.get(H, ST, P), sp_.get(H, ST, P)
        low = gm.rearrange("p a (j k) -> p a j k", k=P)
        Xs = Lm.rearrange("p a (j k) -> p a j k", k=P)
        nega = sp_.get(2)
        early = Space(work.tensor, work.size, sp_.at + 4 * S)
        n = sp_.get(DT, S)
        kN = n[:, 0:2, :].rearrange("p a (b c) -> p (a b) c", c=256)
        vN = n[:, 2:4, :].rearrange("p a (b c) -> p (a b) c", c=256)
        kdec = n[:, 4:6, :].rearrange("p a (b c) -> p (a b) c", c=256)
        U = n[:, 6:8, :].rearrange("p a (b c) -> p (a b) c", c=256)
        qd = cx[:, 0:2, 0:S]
        WT = cx[:, 2:4, 0:S]
        eGB = cx[:, 4:6, 0:S]
        flat = lambda a: a.rearrange("p c s -> p (c s)")
        chunks = lambda a: a.rearrange("p (j k) -> p j k", k=P)

        def headcols(i):
            return ecol[:, :, 4 * i:4 * i + 4].unsqueeze(3).to_broadcast([P, ST, H, HD])

        R = slice(0, 4)
        with Stage() as st:
            g_in, g_out, rows_ready = st.sem("g_in"), st.sem("g_out"), st.sem("rows_ready")
            zeroed, cols_done, cols_ready = st.sem("zeroed"), st.sem("cols_done"), st.sem("cols_ready")
            spread, scan_ready, decay_ready, head_ready = (st.sem("spread"), st.sem("scan_ready"), st.sem("decay_ready"),
                                                           st.sem("head_ready"))
            nat_done, nat_copied, eg_done, eg_ready = (st.sem("nat_done"), st.sem("nat_copied"), st.sem("eg_done"),
                                                       st.sem("eg_ready"))
            norms = HeadNorms(st, [cv[:, c, :] for c in range(4)], [HD ** -0.5 if c < 2 else 1.0 for c in range(4)], 1.0, early)
            b_spread, kb_ready, kk_done = st.sem("b_spread"), st.sem("kb_ready"), st.sem("kk_done")

            @st.block.gpsimd
            def _(pool):
                G.memset(rowc[0:68, :], 0.0).then_inc(zeroed, 1)

            @st.block.scalar
            def _(act):
                act.wait_ge(zeroed, 1)
                A.activation(rowc[R, :], cb[R, :], ACT.Sigmoid).then_inc(g_out, 1)
                A.activation(nega[R, 0:1], col(c2, "a_log", 0, 4), ACT.Exp).then_inc(g_out, 1)
                A.activation(rowg[R, :], ca[R, :], ACT.Identity, bias=col(c2, "dt_bias", 0, 4)).then_inc(g_out, 1)
                norms.square(act)
                act.wait_ge(g_in, 1)
                A.activation(rs1[R, :], rs1[R, :], ACT.Exp, scale=-1.0).then_inc(g_out, 1)
                act.wait_ge(g_out, 4)
                A.activation(rs1[R, :], rs1[R, :], ACT.Ln, bias=C("one", 4)).then_inc(g_out, 1)
                norms.take_root(act)
                act.wait_ge(cols_done, 1)
                A.activation(cols.rearrange("p j c -> p (j c)"), ps[7][:, 0:ST * 68], ACT.Copy).then_inc(cols_ready, 1)
                act.wait_ge(cols_ready, 1)
                A.activation(ecol[:, :, 0:4], cols[:, :, 32:36], ACT.Exp).then_inc(cols_ready, 1)
                A.activation(ecol[:, :, 4:8], cols[:, :, 64:68], ACT.Exp).then_inc(cols_ready, 1)
                for c in range(2):
                    act.wait_ge(eg_done, c + 1)
                    A.activation(eGB[:, c, :], ps[4 + c][:, :], ACT.Exp).then_inc(eg_ready, 1)
                for j in range(4):
                    act.wait_ge(nat_done, j + 1)
                    A.activation((kN if j < 2 else vN)[:, 2 * (j % 2):2 * (j % 2) + 2, :].rearrange("p a c -> p (a c)"),
                                 ps[6 + j % 2][:, :], ACT.Copy).then_inc(nat_copied, 1)
                for hd in range(H):
                    act.wait_ge(scan_ready, hd + 1)
                    if hd >= 2:
                        act.wait_ge(head_ready, 2 * (hd - 2) + 2)
                    A.activation(Lm[:, hd % 2, :], gm[:, hd % 2, :], ACT.Exp).then_inc(decay_ready, 1)

            @st.block.tensor
            def _(pe):
                norms.pe(pe)
                pe.wait_ge(rows_ready, 1)
                for j in range(ST):
                    mm = T.transpose(ps[7][:, 68 * j:68 * j + 68], rowc[0:68, j * P:(j + 1) * P], C("ident")[0:68, 0:68])
                mm.then_inc(cols_done, 1)
                for c in range(2):
                    T.matmul(ps[4 + c][:, :], C("selp", 4, c * P, (c + 1) * P), rowG[R, :], start=True, stop=True).then_inc(eg_done, 1)
                pe.wait_ge(cols_ready, 1)
                pe.wait_ge(norms.ready, 4)
                for j in range(4):
                    if j >= 2:
                        pe.wait_ge(nat_copied, j - 1)
                    for a in range(2):
                        for p in range(2):
                            ch = 2 * (j % 2) + a
                            mm = T.transpose(ps[6 + j % 2][:, a * 256 + p * P:a * 256 + (p + 1) * P],
                                             cv[:, 2 + 2 * (j // 2) + p, ch * P:(ch + 1) * P], C("ident"))
                    mm.then_inc(nat_done, 1)
                pe.wait_ge(nat_copied, 4)
                for c in range(2):
                    T.matmul(ps[6 + c][:, :], C("selp", 4, c * P, (c + 1) * P), rowc[R, :], start=True, stop=True).then_inc(b_spread, 1)
                pe.wait_ge(eg_ready, 2)
                for hd in range(H):
                    r = slice(64 * (hd % 2), 64 * (hd % 2) + 64)
                    b0 = 3 * (hd % 2)
                    if hd >= 2:
                        pe.wait_ge(head_ready, 2 * (hd - 2) + 2)
                    T.matmul(ps[b0][:, :], C("sel", 4, hd * P, (hd + 1) * P), rowg[R, :], start=True, stop=True).then_inc(spread, 1)
                    if hd % 2 == 0:
                        pe.wait_ge(kb_ready, hd // 2 + 1)
                    for a, rhs in enumerate((kb, cv)):
                        for j in range(ST):
                            q = slice(j * P, (j + 1) * P)
                            mm = T.matmul(ps[b0 + 1 + a][:, q], cv[r, 2 + hd // 2, q], rhs[r, hd // 2, q], start=True, stop=True)
                    mm.then_inc(kk_done, 1)

            @st.block.vector
            def _(dve):
                order = Order(dve, st.sem("dve_order"))
                dve.wait_ge(g_out, 3)
                V.scalar_tensor_tensor(out=rs1[R, :], in0=rowg[R, :], scalar=-1.0, in1=rowg[R, :], op0=ALU.mult, op1=ALU.max) \
                 .then_inc(g_in, 1)
                dve.wait_ge(g_out, 5)
                order.done(V.scalar_tensor_tensor(out=rs2[R, :], in0=rowg[R, :], scalar=0.0, in1=rs1[R, :], op0=ALU.max, op1=ALU.add))
                order.done(V.tensor_scalar(rowg[R, :], rs2[R, :], nega[R, 0:1], -1.0, ALU.mult, ALU.mult))
                order.done(V.tensor_tensor_scan(rowG[R, :], C("restart", 4), rowg[R, :], 0.0, ALU.mult, ALU.add))
                gv = chunks(rowG[R, :])
                order.done(V.tensor_copy(rowc[32:36, :], rowG[R, :]))
                V.tensor_tensor(chunks(rowc[64:68, :]), gv[:, :, P - 1:P].to_broadcast([4, ST, P]), gv, ALU.subtract) \
                 .then_inc(rows_ready, 1)
                norms.dve(dve)
                dve.wait_ge(norms.ready, 4)
                dve.wait_ge(cols_ready, 3)
                order.done(V.tensor_tensor(ecol[:, :, 8:12], ecol[:, :, 0:4], cols[:, :, 0:4], ALU.mult))
                dve.wait_ge(eg_ready, 2)
                order.done(V.tensor_tensor(qd, cv[:, 0:2, :], eGB, ALU.mult))
                dve.wait_ge(nat_copied, 4)
                hv = lambda a: a.rearrange("p j (e c) -> p j e c", c=HD)
                order.done(V.tensor_tensor(hv(kdec), hv(kN), headcols(1), ALU.mult))
                order.done(V.tensor_tensor(hv(kN), hv(kN), headcols(2), ALU.mult))
                order.done(V.tensor_tensor(hv(vN), hv(vN), cols[:, :, 0:4].unsqueeze(3).to_broadcast([P, ST, H, HD]), ALU.mult))
                for c in range(2):
                    dve.wait_ge(b_spread, c + 1)
                    V.tensor_tensor(kb[:, c, :], cv[:, 2 + c, :], ps[6 + c][:, :], ALU.mult).then_inc(kb_ready, 1)
                for hd in range(H + 1):
                    if hd < H:
                        dve.wait_ge(spread, hd + 1)
                        if hd >= 2:
                            dve.wait_ge(decay_ready, hd - 1)
                        gx = gm[:, hd % 2, :]
                        order.done(V.tensor_tensor(gx, ps[3 * (hd % 2)][:, :], C("strict4"), ALU.mult))
                        V.tensor_tensor_scan(gx, C("strict4"), gx, 0.0, ALU.mult, ALU.add).then_inc(scan_ready, 1)
                    if hd >= 1:
                        g = hd - 1
                        b0 = 3 * (g % 2)
                        Lx = Lm[:, g % 2, :]
                        flat4 = lambda a: a[:, g, :, :].rearrange("p j k -> p (j k)")
                        dve.wait_ge(decay_ready, g + 1)
                        order.done(V.tensor_tensor(chunks(Lx), chunks(Lx), C("upto").unsqueeze(1).to_broadcast([P, ST, P]), ALU.mult))
                        dve.wait_ge(kk_done, g + 1)
                        V.tensor_tensor(flat4(AT), Lx, ps[b0 + 1][:, :], ALU.mult).then_inc(head_ready, 1)
                        V.tensor_tensor(flat4(qkT), Lx, ps[b0 + 2][:, :], ALU.mult).then_inc(head_ready, 1)

        NL = len(LEVELS)
        steps = [(v, hd) for v in range(NL) for hd in range(H)]
        NS = len(steps)

        def twice(i):
            return 2 * (i + 1) - max(0, i + 1 - (NL - 1) * H)

        with Stage() as st:
            low_ready, x_done, x_ready = st.sem("low_ready"), st.sem("x_done"), st.sem("x_ready")
            yz_done, updated = st.sem("yz_done"), st.sem("updated")

            @st.block.gpsimd
            def _(pool):
                for i, (v, hd) in enumerate(steps):
                    if i >= 2:
                        pool.wait_ge(x_done, i - 1)
                        if i - 2 < H:
                            pool.wait_ge(updated, twice(i - 2))
                    G.tensor_tensor(low[:, i % 2, :, :], AT[:, hd, :, :],
                                    C("levels", None, v * P, (v + 1) * P).unsqueeze(1).to_broadcast([P, ST, P]), ALU.mult) \
                     .then_inc(low_ready, 1)

            @st.block.scalar
            def _(act):
                for i in range(H, NS):
                    act.wait_ge(x_done, i + 1)
                    if i - 2 >= H:
                        act.wait_ge(yz_done, twice(i - 2) - 2 * H)
                    A.activation(Xs[:, i % 2, :, :].rearrange("p j k -> p (j k)"), ps[i % 2][:, :], ACT.Copy).then_inc(x_ready, 1)

            @st.block.tensor
            def _(pe):
                for i in range(NS + 1):
                    if i < NS:
                        v, hd = steps[i]
                        pe.wait_ge(low_ready, i + 1)
                        if v:
                            pe.wait_ge(updated, twice(i - H))
                        if i >= 2:
                            if i - 2 < H:
                                pe.wait_ge(updated, twice(i - 2))
                            else:
                                pe.wait_ge(x_ready, i - 1 - H)
                        for j in range(ST):
                            if v:
                                mm = T.matmul(ps[i % 2][:, j * P:(j + 1) * P], low[:, i % 2, j, :], Tn[:, hd, j, :], start=True, stop=True)
                            else:
                                mm = T.transpose(ps[i % 2][:, j * P:(j + 1) * P], low[:, i % 2, j, :], C("ident"))
                        mm.then_inc(x_done, 1)
                    if i - 1 >= H:
                        g = i - 1
                        v, hd = steps[g]
                        pe.wait_ge(x_ready, g + 1 - H)
                        if g - 2 >= H:
                            pe.wait_ge(updated, twice(g - 2))
                        if v < NL - 1:
                            for j in range(ST):
                                mm = T.matmul(ps[2 + g % 2][:, j * P:(j + 1) * P], Tt[:, hd, j, :], Xs[:, g % 2, j, :], start=True, stop=True)
                            mm.then_inc(yz_done, 1)
                        for j in range(ST):
                            mm = T.matmul(ps[4 + g % 2][:, j * P:(j + 1) * P], Xs[:, g % 2, j, :], Tt[:, hd, j, :], start=True, stop=True)
                        mm.then_inc(yz_done, 1)

            @st.block.vector
            def _(dve):
                eye = C("ident").unsqueeze(1).to_broadcast([P, ST, P])
                for i, (v, hd) in enumerate(steps):
                    if v == 0:
                        dve.wait_ge(low_ready, i + 1)
                        V.tensor_tensor(Tt[:, hd, :, :], eye, low[:, i % 2, :, :], ALU.subtract).then_inc(updated, 1)
                        dve.wait_ge(x_done, i + 1)
                        V.tensor_tensor(Tn[:, hd, :, :], eye, chunks(ps[i % 2][:, :]), ALU.subtract).then_inc(updated, 1)
                        continue
                    dve.wait_ge(updated, twice(i - H))
                    dve.wait_ge(yz_done, twice(i) - 2 * H)
                    for a, X_ in enumerate((Tn, Tt)):
                        if a == 0 and v == NL - 1:
                            continue
                        f = X_[:, hd, :, :].rearrange("p j k -> p (j k)")
                        V.tensor_tensor(f, f, ps[2 + 2 * a + i % 2][:, :], ALU.subtract).then_inc(updated, 1)

        state = rowg[:, 0:2 * HD].rearrange("p (a c) -> p a c", c=HD)
        vnew = rowG[:, 0:H * HD].rearrange("p (a c) -> p a c", c=HD)
        o = low[:, 0:2, :, :].rearrange("p a j k -> p a (j k)")
        with Stage() as st:
            u_done, u_copied, w_done, w_copied = st.sem("u_done"), st.sem("u_copied"), st.sem("w_done"), st.sem("w_copied")
            zeroed, ws_done, v_ready, s_done, s_ready = (st.sem("zeroed"), st.sem("ws_done"), st.sem("v_ready"), st.sem("s_done"),
                                                         st.sem("s_ready"))
            o_done = st.sem("o_done")

            @st.block.gpsimd
            def _(pool):
                G.memset(state, 0.0).then_inc(zeroed, 1)

            @st.block.tensor
            def _(pe):
                for j in range(ST):
                    for hd in range(H):
                        mm = T.matmul(ps[j // 2][:, (j % 2) * 256 + hd * HD:(j % 2) * 256 + (hd + 1) * HD], Tt[:, hd, j, :],
                                      vN[:, j, hd * HD:(hd + 1) * HD], start=True, stop=True)
                mm.then_inc(u_done, 1)
                for hd in range(H):
                    for j in range(ST):
                        mm = T.matmul(ps[2 + hd // 2][64 * (hd % 2):64 * (hd % 2) + 64, j * P:(j + 1) * P],
                                      kN[:, j, hd * HD:(hd + 1) * HD], Tt[:, hd, j, :], start=True, stop=True)
                mm.then_inc(w_done, 1)
                pe.wait_ge(w_copied, 2)
                pe.wait_ge(u_copied, 2)
                pe.wait_ge(zeroed, 1)
                for j in range(ST):
                    q = slice(j * P, (j + 1) * P)
                    if j:
                        pe.wait_ge(s_ready, 2 * j)
                    for hd in range(H):
                        r = slice(64 * (hd % 2), 64 * (hd % 2) + 64)
                        mm = T.matmul(ps[4 * (1 - hd % 2)][:, (hd // 2) * HD:(hd // 2 + 1) * HD], WT[r, hd // 2, q], state[r, hd // 2, :],
                                      start=True, stop=True)
                        if hd >= 2:
                            mm.then_inc(ws_done, 1)
                    pe.wait_ge(v_ready, 2 * j + 2)
                    for hd in range(H):
                        r = slice(64 * (hd % 2), 64 * (hd % 2) + 64)
                        mm = T.matmul(ps[5][r, (hd // 2) * HD:(hd // 2 + 1) * HD], kdec[:, j, hd * HD:(hd + 1) * HD], vnew[:, hd, :],
                                      start=True, stop=True)
                    for hd in range(H):
                        r = slice(64 * (hd % 2), 64 * (hd % 2) + 64)
                        out = ps[6 + hd // 2][r, q]
                        T.matmul(out, state[r, hd // 2, :], qd[r, hd // 2, q], start=True, stop=False)
                        mm = T.matmul(out, vnew[:, hd, :], qkT[:, hd, j, :], start=False, stop=True)
                    mm.then_inc(s_done, 1)

            @st.block.scalar
            def _(act):
                act.wait_ge(u_done, 1)
                for a in range(2):
                    A.activation(U[:, 2 * a:2 * a + 2, :].rearrange("p a c -> p (a c)"), ps[a][:, :], ACT.Copy).then_inc(u_copied, 1)
                act.wait_ge(w_done, 1)
                for c in range(2):
                    A.activation(WT[:, c, :], ps[2 + c][:, :], ACT.Copy).then_inc(w_copied, 1)
                act.wait_ge(s_done, ST)
                for c in range(2):
                    A.activation(o[:, c, :], ps[6 + c][:, :], ACT.Copy).then_inc(o_done, 1)

            @st.block.vector
            def _(dve):
                dve.wait_ge(u_copied, 2)
                for j in range(ST):
                    dve.wait_ge(ws_done, 2 * j + 2)
                    if j:
                        dve.wait_ge(s_done, j)
                    for e in range(2):
                        V.tensor_tensor(vnew.rearrange("p (a e) c -> p a e c", e=2)[:, :, e, :],
                                        U[:, j, :].rearrange("p (a e c) -> p a e c", e=2, c=HD)[:, :, e, :],
                                        ps[4 * (1 - e)][:, 0:2 * HD].rearrange("p (a c) -> p a c", c=HD), ALU.subtract) \
                         .then_inc(v_ready, 1)
                    dve.wait_ge(s_done, j + 1)
                    for c in range(2):
                        V.scalar_tensor_tensor(out=state[:, c, :], in0=state[:, c, :], scalar=eGB[:, c, (j + 1) * P - 1:(j + 1) * P],
                                               in1=ps[5][:, c * HD:(c + 1) * HD], op0=ALU.mult, op1=ALU.add).then_inc(s_ready, 1)

        with Stage() as st:
            p_, a_, v_ = head_output(st, finish, "gd", o, col(c2, "gdn_norm"), cgt, y, 6, qd)
            st.block.tensor(p_)
            st.block.scalar(a_)
            st.block.vector(v_)

    load_inputs()
    Stage.clear_last()
    with nc.Fori(0, DEPTH) as l:
        load_parameters(l, "par1", n1)
        feed_forward(l, t["ffn1_gu"], t["ffn1_dn"], [col(c1, "ffn1_norm", k) for k in range(DT)], ada_half=0)
        scope = Scope()
        m, spectrum = mixer1_buffers(scope)
        mixer1_project(l, m)
        inner = Scope()
        work = inner.space(WORK)
        mixer1_attention(l, m, work)
        mixer1_mlstm(l, m, work, spectrum)
        inner.close()
        project_out(l, t["out1"], m[0])
        scope.close()
        feed_forward(l, t["ffn2_gu"], t["ffn2_dn"], [col(c1, "ffn2_norm", k) for k in range(DT)], ada_half=1)
        embed_layer(l)
        Stage.clear_last()
    final_norm()
    Stage.clear_last()
    with nc.Fori(0, DEPTH) as l:
        adaptive(l)
        scope = Scope()
        m = mixer2_buffers(scope)
        mixer2_project(l, m)
        inner = Scope()
        work = inner.space(WORK)
        mixer2_window(l, m, work)
        mixer2_hgrn(l, m, work)
        mixer2_delta(l, m, work)
        inner.close()
        project_out(l, t["out2"], m[0], [modc[:, 16 + k:17 + k] for k in range(DT)])
        scope.close()
        feed_forward(l, t["ffn3_gu"], t["ffn3_dn"], [gain_f[:, k:k + 1] for k in range(DT)],
                     [modc[:, 24 + k:25 + k] for k in range(DT)], 40)
        Stage.clear_last()
    with Stage() as st:
        @st.block.sync
        def _(sp):
            sp.dma_start(t["out"].rearrange("(k p) s -> p k s", p=P), h[:, :, :]).then_inc(st.sem("stored"), 16)
            sp.wait_ge(st.sem("stored"), 16)
    Stage.clear_last()


def tiles(w, cols=None):
    L, K, N = w.shape
    return np.ascontiguousarray(w.reshape(L, K // P, P, N // P, P).transpose(0, 3, 2, 1, 4)
                                .reshape(L, N // P, P, K))


def tile_pairs(w):
    a = tiles(w)
    L, n, _, K = a.shape
    return np.ascontiguousarray(a.reshape(L, n // 2, 2, P, K).transpose(0, 1, 3, 2, 4).reshape(L, n // 2, P, 2 * K))


def row_parts(w, n):
    L, K, N = w.shape
    return np.ascontiguousarray(w.reshape(L, K // P, P, n, N // n).transpose(0, 3, 2, 1, 4).reshape(L, n, P, -1))


def rows(w):
    L, K, N = w.shape
    return np.ascontiguousarray(w.reshape(L, K // P, P, N).transpose(0, 2, 1, 3).reshape(L, P, -1))


def column(v):
    return v.reshape(v.shape[0], -1, P).transpose(0, 2, 1)


def padded(a, rows_at, width):
    out = np.zeros((a.shape[0], P, 1), a.dtype)
    for g, r in enumerate(rows_at):
        out[:, r:r + width, 0] = a[:, g]
    return out


def pairs(w):
    out = np.zeros((w.shape[0], P, 2, P), w.dtype)
    for g in range(4):
        b = 64 * (g % 2)
        out[:, b:b + 64, g // 2, b:b + 64] = w[:, g]
    return out.reshape(w.shape[0], P, 2 * P)


def lay_out(x):
    L = DEPTH
    f = {}
    f["x"] = np.ascontiguousarray(x["x"][0].T)
    f["p"] = np.ascontiguousarray(x["p"][:, 0].transpose(0, 2, 1))
    f["pos"] = np.ascontiguousarray(x["positions"]).astype(np.int32)
    f["pos2"] = np.ascontiguousarray(x["positions_2"]).astype(np.int32)
    for name in ("ffn1", "ffn2"):
        f[name + "_gu"] = np.stack([tiles(x[name + "_w_gate"]), tiles(x[name + "_w_up"])], 3).reshape(L, FT, P, 2 * D)
        f[name + "_dn"] = tiles(x[name + "_w_down"])
    f["ffn3_gu"] = np.stack([tiles(x["w_gate_2"]), tiles(x["w_up_2"])], 3).reshape(L, FT, P, 2 * D)
    f["ffn3_dn"] = tiles(x["w_down_2"])

    w = x["w_in"]
    o = np.cumsum([0, 384, 256, 64, 256, 256, 256, 16, 256])
    cq, ckv, kr, mx, mv, mo, mif, fin = [w[:, :, o[i]:o[i + 1]] for i in range(8)]
    f["in1_t"] = tile_pairs(np.concatenate([cq, ckv, mx, mo, kr, kr], 2))
    gates = np.zeros((L, D, P), np.float32)
    for g in range(2):
        for d in range(2):
            r = 64 * g + 32 * d
            gates[:, :, r:r + H] = mif[:, :, 8 * g + 4 * d:8 * g + 4 * d + 4]
    f["in1_g"] = rows(gates)
    f["in1_r"] = row_parts(np.concatenate([mv, fin], 2), 2)
    uq = x["mla_w_uq"].reshape(L, 384, 4, 192)
    f["uq"] = rows(np.concatenate([uq[..., :128].reshape(L, 384, 512), uq[..., 128:].reshape(L, 384, 256)], 2))
    ukv = x["mla_w_ukv"].reshape(L, 256, 4, 256)
    f["ukv"] = rows(np.concatenate([ukv[..., :128].reshape(L, 256, 512), ukv[..., 128:].reshape(L, 256, 512)], 2))
    f["mqk"] = np.ascontiguousarray(np.concatenate([pairs(x["mlstm_w_q"]), pairs(x["mlstm_w_k"])], 2))
    f["fnw"] = pairs(x["fnet_w"])
    f["out1"] = tile_pairs(x["w_out"])
    f["pleg"] = tile_pairs(x["ple_w_gate"])
    f["plep"] = rows(x["ple_w_proj"])
    f["par1"] = np.ascontiguousarray(np.concatenate([
        column(x["ffn1_norm"]), column(x["mix_norm"]), column(x["mla_q_norm"]), column(x["mla_kv_norm"]),
        x["mlstm_conv_w"].reshape(L, 5, 2, P).transpose(0, 3, 2, 1).reshape(L, P, 10), column(x["mlstm_conv_b"]),
        padded(x["mlstm_i_bias"], (0, 32), H), padded(x["mlstm_f_bias"], (0, 32), H),
        column(x["mlstm_head_norm"]), column(x["mlstm_skip"]), column(x["fnet_b"]), column(x["ffn2_norm"]),
        column(x["ple_gate_norm"]), column(x["ple_post_norm"])], 2))

    w = x["w_in_2"]
    o = np.cumsum([0, 512, 128, 128, 256, 256, 256, 256, 768, 256, 4, 4])
    aq, ak, av, bq, bf, bv, bg, cc, cgt, cb, ca = [w[:, :, o[i]:o[i + 1]] for i in range(11)]
    order = [0, 4, 1, 5, 2, 6, 3, 7]
    aq = aq.reshape(L, D, 8, HD)[:, :, order].reshape(L, D, 512)
    gates = np.zeros((L, D, P), np.float32)
    gates[:, :, 0:H], gates[:, :, 32:32 + H] = cb, ca
    f["in2_t"] = tile_pairs(np.concatenate([aq, ak, bq, bf, bg, cc, cgt, gates], 2))
    f["in2_r"] = row_parts(np.concatenate([av, bv], 2), 2)
    wo = x["w_out_2"]
    f["out2"] = tile_pairs(np.concatenate([wo[:, :512].reshape(L, 8, HD, D)[:, order].reshape(L, 512, D), wo[:, 512:]], 1))
    f["ada"] = np.ascontiguousarray(x["ada_w_2"].reshape(L, DT // 2, 2, P, 6 * D // 768, 768).transpose(0, 4, 1, 3, 2, 5)
                                    .reshape(L, DT // 2 * (6 * D // 768), P, 2 * 768))
    two = lambda v: np.concatenate([v, v], 1)[:, :, None]
    sinks = np.broadcast_to(x["attn_sinks_2"][:, None, order], (L, P, 8))
    f["par2"] = np.ascontiguousarray(np.concatenate([
        column(x["norm_mix_2"]), two(x["attn_q_norm_2"]), two(x["attn_k_norm_2"]), sinks, two(x["hgrn_out_norm_2"]),
        x["gdn_conv_w_2"].reshape(L, 4, 6, P).transpose(0, 3, 2, 1).reshape(L, P, 24),
        padded(x["gdn_a_log_2"][:, None], (0,), H), padded(x["gdn_dt_bias_2"][:, None], (0,), H),
        two(x["gdn_out_norm_2"]), column(x["norm_ffn_2"]), column(x["ada_b_2"])], 2))
    f["parg"] = np.ascontiguousarray(np.concatenate([
        column(x["final_norm"][None])[0], column(x["c_2"])[0],
        column(x["hgrn_lb_logits_2"]).transpose(1, 0, 2).reshape(P, 4)], 1))

    i = np.arange(S)
    ang = 2 * np.pi * ((i[:, None] * i[None, :]) % S) / S
    unit = 1.0 / math.sqrt(S * HD)
    dft = np.stack([np.cos(ang) * unit, np.sin(ang) * unit]).astype(np.float32)
    f["dft"] = np.ascontiguousarray(dft.reshape(2, ST, P, S).transpose(2, 0, 1, 3).reshape(P, 2 * ST * S))
    return f


def kernel(**inputs):
    import concourse.bacc as bacc
    from concourse.bass_utils import run_bass_kernel_spmd as run

    arrays = lay_out({k: np.asarray(v) for k, v in inputs.items()})
    arrays["cst"], where = pack(constant_columns())
    nc = bacc.Bacc("TRN2", target_bir_lowering=False, num_devices=1)
    t = {k: nc.dram_tensor("in_" + k, a.shape, mybir.dt.from_np(a.dtype), kind="ExternalInput").ap()
         for k, a in arrays.items()}
    t["out"] = nc.dram_tensor("out", (D, S), F32, kind="ExternalOutput").ap()
    build(nc, t, where)
    r = run(nc, [{"in_" + k: a for k, a in arrays.items()}], core_ids=[0])
    return np.ascontiguousarray(r.results[0]["out"].T)[None]
```
